# Optimizing a Trainium2 kernel written in Bass

```python
import math
import jax, jax.numpy as jnp
from jax import lax
import numpy as np

D_MODEL = 1024
BATCH = 1
SEQ = 512
DEPTH = 1

HG_HEADS = 8
HG_DK = 128
HG_DV = D_MODEL // HG_HEADS
HG_CHUNK = 32

NSA_HEADS = 8
NSA_GROUPS = 2
NSA_REP = NSA_HEADS // NSA_GROUPS
NSA_DK = 128
NSA_DV = 128
CMP_BLOCK = 32
CMP_STRIDE = 16
CMP_HIDDEN = 128
SLC_BLOCK = 64
SLC_TOPK = 16
WINDOW = 512
Q_BLOCK = 64
FORCE_SCORE = 1e4

REL_BUCKETS = 32
REL_MAX_DIST = 128

N_GROUPS = 4
EXP_PER_GROUP = 8
N_EXPERTS = N_GROUPS * EXP_PER_GROUP
TOPK_IN_GROUP = 2
D_EXPERT = D_MODEL // 2
MOE_BLOCK = 128

ALPHA = (2 * DEPTH) ** 0.25
BETA = (8 * DEPTH) ** -0.25

SPLITS = (HG_HEADS * HG_DK, HG_HEADS * HG_DK, HG_HEADS * HG_DV, HG_HEADS * HG_DV,
          NSA_HEADS * NSA_DK,
          NSA_GROUPS * NSA_DK, NSA_GROUPS * NSA_DV,
          NSA_GROUPS * NSA_DK, NSA_GROUPS * NSA_DV,
          NSA_GROUPS * NSA_DK, NSA_GROUPS * NSA_DV,
          3 * NSA_HEADS, D_MODEL, D_MODEL)
D_IN = sum(SPLITS)


def _layer_norm(x, eps=1e-5):
    xf = x.astype(jnp.float32)
    mu = jnp.mean(xf, axis=-1, keepdims=True)
    var = jnp.mean(jnp.square(xf - mu), axis=-1, keepdims=True)
    return ((xf - mu) * lax.rsqrt(var + eps)).astype(x.dtype)

def _rms_norm(x, eps=1e-6):
    xf = x.astype(jnp.float32)
    return (xf * lax.rsqrt(jnp.mean(jnp.square(xf), axis=-1, keepdims=True) + eps)).astype(x.dtype)

def _masked_softmax(logits, mask):
    lf = jnp.where(mask, logits.astype(jnp.float32), -1e30)
    p = jax.nn.softmax(lf, axis=-1)
    return jnp.where(mask, p, 0.0)

def _rel_bucket(dist):
    n = jnp.maximum(dist, 0)
    max_exact = REL_BUCKETS // 2
    nf = jnp.maximum(n, 1).astype(jnp.float32)
    large = max_exact + (jnp.log(nf / max_exact) / math.log(REL_MAX_DIST / max_exact)
                         * (REL_BUCKETS - max_exact)).astype(jnp.int32)
    large = jnp.minimum(large, REL_BUCKETS - 1)
    return jnp.where(n < max_exact, n, large)

def _hgrn2(q, f_raw, v, lb):
    B, T = q.shape[:2]
    N = T // HG_CHUNK
    lb = lb.reshape(HG_HEADS, HG_DK).astype(q.dtype)
    f = lb + (1 - lb) * jax.nn.sigmoid(f_raw)
    log_f = jnp.log(f)
    k = 1 - f

    def chunks(a):
        return a.reshape(B, N, HG_CHUNK, HG_HEADS, a.shape[-1]).transpose(1, 0, 3, 2, 4)

    qc, kc, vc, lfc = chunks(q), chunks(k), chunks(v), chunks(log_f)
    b = jnp.cumsum(lfc, axis=3)
    b_last = b[:, :, :, -1:, :]
    q_in = qc * jnp.exp(b)
    k_in = kc * jnp.exp(-b)
    k_end = kc * jnp.exp(b_last - b)
    causal = jnp.tril(jnp.ones((HG_CHUNK, HG_CHUNK), dtype=bool))
    att = jnp.einsum('nbhid,nbhjd->nbhij', q_in, k_in)
    att = jnp.where(causal, att, 0)
    o_intra = jnp.einsum('nbhij,nbhje->nbhie', att, vc)
    upd = jnp.einsum('nbhcd,nbhce->nbhde', k_end, vc)
    decay = jnp.exp(b_last[:, :, :, 0, :])

    def step(S, xs):
        q_n, dec_n, u_n = xs
        o_n = jnp.einsum('bhcd,bhde->bhce', q_n, S)
        S = dec_n[..., None] * S + u_n
        return S, o_n

    S0 = jnp.zeros((B, HG_HEADS, HG_DK, HG_DV), q.dtype)
    _, o_inter = lax.scan(step, S0, (q_in, decay, upd))
    o = o_intra + o_inter
    return o.transpose(1, 0, 3, 2, 4).reshape(B, T, HG_HEADS, HG_DV)

def _compress(kv, pos, w1, b1, w2):
    B, G, T, d = kv.shape
    r = CMP_BLOCK // CMP_STRIDE
    ns = T // CMP_STRIDE
    sub = kv.reshape(B, G, ns, CMP_STRIDE, d)
    blocks = jnp.concatenate([sub[:, :, j:ns - r + 1 + j] for j in range(r)], axis=3)
    blocks = (blocks + pos).reshape(B, G, ns - r + 1, CMP_BLOCK * d)
    return jax.nn.silu(blocks @ w1 + b1) @ w2

def _nsa(q, kc, vc, ks, vs, kw, vw, gate_raw, rel_bias,
         pos_k, w1_k, b1_k, w2_k, pos_v, w1_v, b1_v, w2_v):
    B, T = q.shape[:2]
    G, R = NSA_GROUPS, NSA_REP
    NQB = T // Q_BLOCK
    NSLC = T // SLC_BLOCK
    NSEL = min(SLC_TOPK, NSLC)
    scale = NSA_DK ** -0.5
    to_g = lambda a: a.transpose(0, 2, 1, 3)

    k_cmp = _compress(to_g(kc), pos_k, w1_k, b1_k, w2_k)
    v_cmp = _compress(to_g(vc), pos_v, w1_v, b1_v, w2_v)
    NC = k_cmp.shape[2]
    cmp_end = jnp.arange(NC) * CMP_STRIDE + CMP_BLOCK - 1
    cs = np.arange(NC) * CMP_STRIDE
    ss = np.arange(NSLC) * SLC_BLOCK
    overlap = jnp.asarray(((cs[:, None] < ss[None, :] + SLC_BLOCK)
                           & (cs[:, None] + CMP_BLOCK > ss[None, :])).astype(np.float32))

    k_slc = to_g(ks).reshape(B, G, NSLC, SLC_BLOCK, NSA_DK)
    v_slc = to_g(vs).reshape(B, G, NSLC, SLC_BLOCK, NSA_DV)
    pad = ((0, 0), (0, 0), (WINDOW, 0), (0, 0))
    k_win = jnp.pad(to_g(kw), pad)
    v_win = jnp.pad(to_g(vw), pad)
    table = rel_bias.reshape(G, R, REL_BUCKETS)
    g_ix = jnp.arange(G)[None, :, None, None, None]
    r_ix = jnp.arange(R)[None, None, :, None, None]
    blk_start = jnp.arange(NSLC) * SLC_BLOCK
    j_ix = jnp.arange(NSLC)

    q_blocks = q.reshape(B, NQB, Q_BLOCK, G, R, NSA_DK).transpose(1, 0, 3, 4, 2, 5)
    gate_blocks = jax.nn.sigmoid(gate_raw).reshape(B, NQB, Q_BLOCK, G, R, 3).transpose(1, 0, 3, 4, 2, 5)
    gather = jax.vmap(jax.vmap(lambda blk, ix: blk[ix]))

    def block_fn(args):
        qb, q_blk, g_blk = args
        t = qb * Q_BLOCK + jnp.arange(Q_BLOCK)
        dist_c = t[:, None] - cmp_end[None, :]
        s_c = jnp.einsum('bgrqd,bgnd->bgrqn', q_blk, k_cmp) * scale + table[:, :, _rel_bucket(dist_c)]
        p_c = _masked_softmax(s_c, dist_c >= 0)
        o_c = jnp.einsum('bgrqn,bgnd->bgrqd', p_c.astype(v_cmp.dtype), v_cmp)
        imp = jnp.einsum('bgqn,nj->bgqj', p_c.sum(axis=2), overlap)
        cur = t // SLC_BLOCK
        forced = (j_ix[None, :] == 0) | (j_ix[None, :] == cur[:, None]) | (j_ix[None, :] == cur[:, None] - 1)
        valid = blk_start[None, :] <= t[:, None]
        score = jnp.where(valid, jnp.where(forced, FORCE_SCORE, imp), -1.0)
        _, idx = lax.top_k(score, NSEL)
        k_sel = gather(k_slc, idx).reshape(B, G, Q_BLOCK, NSEL * SLC_BLOCK, NSA_DK)
        v_sel = gather(v_slc, idx).reshape(B, G, Q_BLOCK, NSEL * SLC_BLOCK, NSA_DV)
        s_pos = (idx[..., None] * SLC_BLOCK + jnp.arange(SLC_BLOCK)).reshape(B, G, Q_BLOCK, NSEL * SLC_BLOCK)
        dist_s = t[None, None, :, None] - s_pos
        s_s = (jnp.einsum('bgrqd,bgqkd->bgrqk', q_blk, k_sel) * scale
               + table[g_ix, r_ix, _rel_bucket(dist_s)[:, :, None]])
        p_s = _masked_softmax(s_s, (dist_s >= 0)[:, :, None])
        o_s = jnp.einsum('bgrqk,bgqkd->bgrqd', p_s.astype(v_sel.dtype), v_sel)
        k_w = lax.dynamic_slice_in_dim(k_win, qb * Q_BLOCK, WINDOW + Q_BLOCK, axis=2)
        v_w = lax.dynamic_slice_in_dim(v_win, qb * Q_BLOCK, WINDOW + Q_BLOCK, axis=2)
        pos_w = qb * Q_BLOCK - WINDOW + jnp.arange(WINDOW + Q_BLOCK)
        dist_w = t[:, None] - pos_w[None, :]
        mask_w = (dist_w >= 0) & (dist_w < WINDOW) & (pos_w[None, :] >= 0)
        s_w = jnp.einsum('bgrqd,bgkd->bgrqk', q_blk, k_w) * scale + table[:, :, _rel_bucket(dist_w)]
        p_w = _masked_softmax(s_w, mask_w)
        o_w = jnp.einsum('bgrqk,bgkd->bgrqd', p_w.astype(v_w.dtype), v_w)
        return g_blk[..., 0:1] * o_c + g_blk[..., 1:2] * o_s + g_blk[..., 2:3] * o_w

    o = lax.map(block_fn, (jnp.arange(NQB), q_blocks, gate_blocks))
    return o.transpose(1, 0, 4, 2, 3, 5).reshape(B, T, NSA_HEADS * NSA_DV)

def _hier_moe(h, w_grp, b_grp, w_exp, b_exp, w1, w3, w2):
    B, T, D = h.shape
    x = h.reshape(-1, D)
    NT = x.shape[0]
    grp_prob = jax.nn.softmax((x @ w_grp + b_grp).astype(jnp.float32), axis=-1)
    grp_p, grp_idx = lax.top_k(grp_prob, 1)
    exp_logits = (x @ w_exp + b_exp).astype(jnp.float32).reshape(NT, N_GROUPS, EXP_PER_GROUP)
    in_grp = exp_logits[jnp.arange(NT), grp_idx[:, 0]]
    top_l, top_i = lax.top_k(in_grp, TOPK_IN_GROUP)
    comb = grp_p * jax.nn.softmax(top_l, axis=-1)
    expert = grp_idx * EXP_PER_GROUP + top_i

    A = NT * TOPK_IN_GROUP
    e_flat = expert.reshape(-1)
    tok_flat = jnp.repeat(jnp.arange(NT), TOPK_IN_GROUP)
    order = jnp.argsort(e_flat)
    e_s, tok_s, w_s = e_flat[order], tok_flat[order], comb.reshape(-1)[order]
    counts = jnp.bincount(e_flat, length=N_EXPERTS)
    starts = jnp.cumsum(counts) - counts
    padded = (counts + MOE_BLOCK - 1) // MOE_BLOCK * MOE_BLOCK
    pend = jnp.cumsum(padded)
    pstarts = pend - padded
    dest = pstarts[e_s] + jnp.arange(A) - starts[e_s]
    n_blocks = -(-A // MOE_BLOCK) + N_EXPERTS
    x_pad = jnp.zeros((n_blocks * MOE_BLOCK, D), x.dtype).at[dest].set(x[tok_s])
    block_expert = jnp.minimum(jnp.searchsorted(pend, jnp.arange(n_blocks) * MOE_BLOCK, side='right'),
                               N_EXPERTS - 1)

    def expert_block(args):
        xb, e = args
        return (jax.nn.silu(xb @ w1[e]) * (xb @ w3[e])) @ w2[e]

    y_pad = lax.map(expert_block, (x_pad.reshape(n_blocks, MOE_BLOCK, D), block_expert)).reshape(-1, D)
    y = y_pad[dest] * w_s[:, None].astype(x.dtype)
    out = jnp.zeros_like(x).at[tok_s].add(y)
    return out.reshape(B, T, D)

def first_inputs(seed: int = 0) -> dict:
    key = jax.random.key(seed)
    ks = iter(jax.random.split(key, 40))
    nrm = lambda shape, s: jax.random.normal(next(ks), shape, jnp.float32) * s
    L, D = DEPTH, D_MODEL
    return {
        'x': nrm((BATCH, SEQ, D), 1.0),
        'c': nrm((BATCH, D), 1.0),
        'ada_w': nrm((L, D, 6 * D), 0.1 * D ** -0.5),
        'ada_b': nrm((L, 6 * D), 0.02),
        'w_in': nrm((L, D, D_IN), D ** -0.5),
        'b_in': nrm((L, D_IN), 0.02),
        'hg_lb_logits': nrm((DEPTH + 1, HG_HEADS * HG_DK), 0.1),
        'hg_norm_w': 1.0 + nrm((L, HG_HEADS * HG_DV), 0.05),
        'cmp_pos_k': nrm((L, CMP_BLOCK, NSA_DK), 0.1),
        'cmp_w1_k': nrm((L, CMP_BLOCK * NSA_DK, CMP_HIDDEN), (CMP_BLOCK * NSA_DK) ** -0.5),
        'cmp_b1_k': nrm((L, CMP_HIDDEN), 0.02),
        'cmp_w2_k': nrm((L, CMP_HIDDEN, NSA_DK), CMP_HIDDEN ** -0.5),
        'cmp_pos_v': nrm((L, CMP_BLOCK, NSA_DV), 0.1),
        'cmp_w1_v': nrm((L, CMP_BLOCK * NSA_DV, CMP_HIDDEN), (CMP_BLOCK * NSA_DV) ** -0.5),
        'cmp_b1_v': nrm((L, CMP_HIDDEN), 0.02),
        'cmp_w2_v': nrm((L, CMP_HIDDEN, NSA_DV), CMP_HIDDEN ** -0.5),
        'rel_bias': nrm((NSA_HEADS, REL_BUCKETS), 0.5),
        'w_br_hg': nrm((L, HG_HEADS * HG_DV, D), BETA * (HG_HEADS * HG_DV) ** -0.5),
        'w_br_nsa': nrm((L, NSA_HEADS * NSA_DV, D), BETA * (NSA_HEADS * NSA_DV) ** -0.5),
        'w_out': nrm((L, D, D), BETA * D ** -0.5),
        'ln1_g': 1.0 + nrm((L, D), 0.05),
        'ln1_b': nrm((L, D), 0.02),
        'router_grp_w': nrm((L, D, N_GROUPS), D ** -0.5),
        'router_grp_b': nrm((L, N_GROUPS), 0.01),
        'router_exp_w': nrm((L, D, N_EXPERTS), D ** -0.5),
        'router_exp_b': nrm((L, N_EXPERTS), 0.01),
        'exp_w1': nrm((L, N_EXPERTS, D, D_EXPERT), D ** -0.5),
        'exp_w3': nrm((L, N_EXPERTS, D, D_EXPERT), D ** -0.5),
        'exp_w2': nrm((L, N_EXPERTS, D_EXPERT, D), BETA * D_EXPERT ** -0.5),
        'ln2_g': 1.0 + nrm((L, D), 0.05),
        'ln2_b': nrm((L, D), 0.02),
    }

def first_block(x, c, ada_w, ada_b, w_in, b_in, hg_lb_logits, hg_norm_w,
              cmp_pos_k, cmp_w1_k, cmp_b1_k, cmp_w2_k, cmp_pos_v, cmp_w1_v, cmp_b1_v, cmp_w2_v,
              rel_bias, w_br_hg, w_br_nsa, w_out, ln1_g, ln1_b,
              router_grp_w, router_grp_b, router_exp_w, router_exp_b,
              exp_w1, exp_w3, exp_w2, ln2_g, ln2_b):
    B, T, D = x.shape
    split_idx = [int(v) for v in np.cumsum(SPLITS)[:-1]]
    lb_all = jnp.cumsum(jax.nn.softmax(hg_lb_logits.astype(jnp.float32), axis=0), axis=0)
    c_act = jax.nn.silu(c)
    for l in range(DEPTH):
        mod = c_act @ ada_w[l] + ada_b[l]
        sh1, sc1, g1, sh2, sc2, g2 = jnp.split(mod, 6, axis=-1)

        h = _layer_norm(x) * (1 + sc1[:, None]) + sh1[:, None]
        proj = h @ w_in[l] + b_in[l]
        (hq, hf, hi, hg, nq, kc, vc, ks, vs, kw, vw, ngate, mg_h, mg_n) = jnp.split(proj, split_idx, axis=-1)
        o_h = _hgrn2(hq.reshape(B, T, HG_HEADS, HG_DK), hf.reshape(B, T, HG_HEADS, HG_DK),
                     hi.reshape(B, T, HG_HEADS, HG_DV), lb_all[l])
        o_h = (_rms_norm(o_h) * hg_norm_w[l].reshape(HG_HEADS, HG_DV)
               * jax.nn.sigmoid(hg.reshape(B, T, HG_HEADS, HG_DV))).reshape(B, T, HG_HEADS * HG_DV)
        gsz = (B, T, NSA_GROUPS, NSA_DK)
        o_n = _nsa(nq.reshape(B, T, NSA_HEADS, NSA_DK),
                   kc.reshape(gsz), vc.reshape(gsz), ks.reshape(gsz), vs.reshape(gsz),
                   kw.reshape(gsz), vw.reshape(gsz),
                   ngate.reshape(B, T, NSA_HEADS, 3), rel_bias,
                   cmp_pos_k[l], cmp_w1_k[l], cmp_b1_k[l], cmp_w2_k[l],
                   cmp_pos_v[l], cmp_w1_v[l], cmp_b1_v[l], cmp_w2_v[l])
        merged = jax.nn.sigmoid(mg_h) * (o_h @ w_br_hg[l]) + jax.nn.sigmoid(mg_n) * (o_n @ w_br_nsa[l])
        y = (1 + g1[:, None]) * (merged @ w_out[l])
        x = _layer_norm(ALPHA * x + y) * ln1_g[l] + ln1_b[l]

        h = _layer_norm(x) * (1 + sc2[:, None]) + sh2[:, None]
        y = (1 + g2[:, None]) * _hier_moe(h, router_grp_w[l], router_grp_b[l], router_exp_w[l],
                                          router_exp_b[l], exp_w1[l], exp_w3[l], exp_w2[l])
        x = _layer_norm(ALPHA * x + y) * ln2_g[l] + ln2_b[l]
    return x


CHUNK = 64
N_MIXERS = 4
N_HEADS = 16
HEAD_DIM = D_MODEL // N_HEADS
SB_BLOCK = 128
GMLP_BLOCK = 128
GMLP_WIDTH = 2 * D_MODEL
GMLP_GROUPS = 8
CONV_WIDTH = 3
BAND_CHUNKS = 8
REL_CLIP = 128
D_FF = -(-8 * D_MODEL // (3 * 256)) * 256
EPS = 1e-6


def rms_norm(x, g):
    xf = x.astype(jnp.float32)
    y = xf * lax.rsqrt(jnp.mean(xf * xf, axis=-1, keepdims=True) + EPS)
    return (y * g.astype(jnp.float32)).astype(x.dtype)

def layer_norm(x, g):
    xf = x.astype(jnp.float32)
    mu = jnp.mean(xf, axis=-1, keepdims=True)
    xc = xf - mu
    var = jnp.mean(xc * xc, axis=-1, keepdims=True)
    return (xc * lax.rsqrt(var + EPS) * g.astype(jnp.float32)).astype(x.dtype)

def modulate(h, shift, scale):
    return h * (1 + scale) + shift

def stick_breaking_mixer(h, w_qkv, w_o):
    b, s, _ = h.shape
    qkv = (h @ w_qkv).reshape(b, s, 3, N_HEADS, HEAD_DIM)
    q, k, v = qkv[:, :, 0], qkv[:, :, 1], qkv[:, :, 2]
    scale = HEAD_DIM ** -0.5
    outs = []
    for q0 in range(0, s, SB_BLOCK):
        end = q0 + SB_BLOCK
        z = jnp.einsum('bthd,bshd->bhts', q[:, q0:end], k[:, :end]).astype(jnp.float32) * scale
        t_pos = q0 + jnp.arange(SB_BLOCK)[:, None]
        s_pos = jnp.arange(end)[None, :]
        mask = s_pos < t_pos
        sp = jnp.where(mask, jax.nn.softplus(z), 0.0)
        rest = lax.cumsum(sp, axis=3, reverse=True)
        log_a = jnp.where(mask, z - rest, -jnp.inf)
        a = jnp.exp(log_a).astype(v.dtype)
        outs.append(jnp.einsum('bhts,bshd->bthd', a, v[:, :end]))
    o = jnp.concatenate(outs, axis=1).reshape(b, s, D_MODEL)
    return o @ w_o

def spatial_gating_mixer(h, w_in, ln_g, w_s, s_bias, w_out):
    b, s, _ = h.shape
    z = jax.nn.gelu(h @ w_in)
    u, v = jnp.split(z, 2, axis=-1)
    v = layer_norm(v, ln_g)
    nb = s // GMLP_BLOCK
    gc = GMLP_WIDTH // GMLP_GROUPS
    v = v.reshape(b, nb, GMLP_BLOCK, GMLP_GROUPS, gc)
    pos_chunk = jnp.arange(GMLP_BLOCK) // CHUNK
    mask = pos_chunk[:, None] >= pos_chunk[None, :]
    ws = jnp.where(mask[None], w_s, 0.0).astype(v.dtype)
    sv = jnp.einsum('gij,bnjgc->bnigc', ws, v) + s_bias.T[:, :, None].astype(v.dtype)
    y = u * sv.reshape(b, s, GMLP_WIDTH)
    return y @ w_out

def short_conv_mixer(h, w_in, conv_w, w_out):
    gb, gc, xt = jnp.split(h @ w_in, 3, axis=-1)
    y = gc * xt
    yc = lax.conv_general_dilated(
        y, conv_w.reshape(CONV_WIDTH, 1, D_MODEL).astype(y.dtype),
        window_strides=(1,), padding=[(CONV_WIDTH - 1, 0)],
        dimension_numbers=('NWC', 'WIO', 'NWC'), feature_group_count=D_MODEL)
    return (gb * yc) @ w_out

def chunk_band_attention_mixer(h, w_qkv, rel_bias, w_o):
    b, s, _ = h.shape
    nc = s // CHUNK
    nband = BAND_CHUNKS + 1
    qkv = (h @ w_qkv).reshape(b, s, 3, N_HEADS, HEAD_DIM)
    q = qkv[:, :, 0].reshape(b, nc, CHUNK, N_HEADS, HEAD_DIM)
    pad = ((0, 0), (BAND_CHUNKS * CHUNK, 0), (0, 0), (0, 0))
    kp = jnp.pad(qkv[:, :, 1], pad).reshape(b, nc + BAND_CHUNKS, CHUNK, N_HEADS, HEAD_DIM)
    vp = jnp.pad(qkv[:, :, 2], pad).reshape(b, nc + BAND_CHUNKS, CHUNK, N_HEADS, HEAD_DIM)
    scale = HEAD_DIM ** -0.5
    scores = jnp.concatenate(
        [jnp.einsum('bcihd,bcjhd->bhcij', q, kp[:, o:o + nc]) for o in range(nband)],
        axis=-1).astype(jnp.float32) * scale
    i_pos = jnp.arange(CHUNK)[:, None]
    j_pos = jnp.arange(nband * CHUNK)[None, :]
    dist = i_pos + BAND_CHUNKS * CHUNK - j_pos
    idx = jnp.clip(dist, -REL_CLIP, REL_CLIP) + REL_CLIP
    bias = rel_bias[:, idx].astype(jnp.float32)
    key_chunk = jnp.arange(nc)[:, None] - BAND_CHUNKS + j_pos // CHUNK
    valid = (key_chunk >= 0)[:, None, :]
    scores = jnp.where(valid, scores + bias[:, None], -jnp.inf)
    p = jax.nn.softmax(scores, axis=-1).astype(vp.dtype)
    out = jnp.einsum('bhcij,bcjhd->bcihd', p[..., :CHUNK], vp[:, 0:nc])
    for o in range(1, nband):
        out = out + jnp.einsum('bhcij,bcjhd->bcihd', p[..., o * CHUNK:(o + 1) * CHUNK], vp[:, o:o + nc])
    return out.reshape(b, s, D_MODEL) @ w_o

def swiglu_ffn(h, w_in, w_out):
    g, u = jnp.split(h @ w_in, 2, axis=-1)
    return (jax.nn.silu(g) * u) @ w_out

def _n_layers_of(m):
    return len(range(m, DEPTH, N_MIXERS))

def _dense(key, shape, fan_in, gain=1.0):
    return jax.random.normal(key, shape, jnp.float32) * (gain * fan_in ** -0.5)

def second_inputs(seed: int = 0) -> dict:
    key = jax.random.key(seed)
    ks = jax.random.split(key, 21)
    na, nb, ncv, nd = (_n_layers_of(m) for m in range(N_MIXERS))
    D = D_MODEL
    nrm = lambda k, shape: jax.random.normal(k, shape, jnp.float32)
    return {
        "x": nrm(ks[0], (BATCH, SEQ, D)),
        "c": nrm(ks[1], (BATCH, D)),
        "ada_w": _dense(ks[2], (DEPTH, D, 6 * D), D, 0.5),
        "ada_b": 0.02 * nrm(ks[3], (DEPTH, 6 * D)),
        "norm_g": 1.0 + 0.1 * nrm(ks[4], (DEPTH, 4, D)),
        "ffn_w_in": _dense(ks[5], (DEPTH, D, 2 * D_FF), D),
        "ffn_w_out": _dense(ks[6], (DEPTH, D_FF, D), D_FF),
        "sb_w_qkv": _dense(ks[7], (na, D, 3 * D), D),
        "sb_w_o": _dense(ks[8], (na, D, D), D),
        "sg_w_in": _dense(ks[9], (nb, D, 2 * GMLP_WIDTH), D),
        "sg_ln_g": 1.0 + 0.1 * nrm(ks[10], (nb, GMLP_WIDTH)),
        "sg_w_s": _dense(ks[11], (nb, GMLP_GROUPS, GMLP_BLOCK, GMLP_BLOCK), GMLP_BLOCK),
        "sg_bias": 1.0 + 0.1 * nrm(ks[12], (nb, GMLP_GROUPS, GMLP_BLOCK)),
        "sg_w_out": _dense(ks[13], (nb, GMLP_WIDTH, D), GMLP_WIDTH),
        "sc_w_in": _dense(ks[14], (ncv, D, 3 * D), D),
        "sc_conv_w": _dense(ks[15], (ncv, CONV_WIDTH, D), CONV_WIDTH),
        "sc_w_out": _dense(ks[16], (ncv, D, D), D),
        "cb_w_qkv": _dense(ks[17], (nd, D, 3 * D), D),
        "cb_rel_bias": 0.5 * nrm(ks[18], (nd, N_HEADS, 2 * REL_CLIP + 1)),
        "cb_w_o": _dense(ks[19], (nd, D, D), D),
    }

def second_block(x, c, ada_w, ada_b, norm_g, ffn_w_in, ffn_w_out,
              sb_w_qkv, sb_w_o,
              sg_w_in, sg_ln_g, sg_w_s, sg_bias, sg_w_out,
              sc_w_in, sc_conv_w, sc_w_out,
              cb_w_qkv, cb_rel_bias, cb_w_o):
    mod_all = jnp.einsum('bd,lde->lbe', jax.nn.silu(c), ada_w) + ada_b[:, None]
    for i in range(DEPTH):
        m, r = i % N_MIXERS, i // N_MIXERS
        sh_m, sc_m, gt_m, sh_f, sc_f, gt_f = jnp.split(mod_all[i][:, None, :], 6, axis=-1)
        h = modulate(rms_norm(x, norm_g[i, 0]), sh_m, sc_m)
        if m == 0:
            y = stick_breaking_mixer(h, sb_w_qkv[r], sb_w_o[r])
        elif m == 1:
            y = spatial_gating_mixer(h, sg_w_in[r], sg_ln_g[r], sg_w_s[r], sg_bias[r], sg_w_out[r])
        elif m == 2:
            y = short_conv_mixer(h, sc_w_in[r], sc_conv_w[r], sc_w_out[r])
        else:
            y = chunk_band_attention_mixer(h, cb_w_qkv[r], cb_rel_bias[r], cb_w_o[r])
        x = x + gt_m * rms_norm(y, norm_g[i, 1])
        h = modulate(rms_norm(x, norm_g[i, 2]), sh_f, sc_f)
        y = swiglu_ffn(h, ffn_w_in[i], ffn_w_out[i])
        x = x + gt_f * rms_norm(y, norm_g[i, 3])
    return x


def setup_inputs(seed=0):
    out = dict(first_inputs(seed))
    for name, value in second_inputs(seed + 1).items():
        if name != "x":
            out[name + "_2"] = value
    return out


def reference(
    x, c, ada_w, ada_b, w_in, b_in, hg_lb_logits, hg_norm_w, cmp_pos_k, cmp_w1_k, cmp_b1_k,
    cmp_w2_k, cmp_pos_v, cmp_w1_v, cmp_b1_v, cmp_w2_v, rel_bias, w_br_hg, w_br_nsa, w_out,
    ln1_g, ln1_b, router_grp_w, router_grp_b, router_exp_w, router_exp_b, exp_w1, exp_w3,
    exp_w2, ln2_g, ln2_b, c_2, ada_w_2, ada_b_2, norm_g_2, ffn_w_in_2, ffn_w_out_2, sb_w_qkv_2,
    sb_w_o_2, sg_w_in_2, sg_ln_g_2, sg_w_s_2, sg_bias_2, sg_w_out_2, sc_w_in_2, sc_conv_w_2,
    sc_w_out_2, cb_w_qkv_2, cb_rel_bias_2, cb_w_o_2,
):
    x = first_block(
        x, c, ada_w, ada_b, w_in, b_in, hg_lb_logits, hg_norm_w, cmp_pos_k, cmp_w1_k, cmp_b1_k,
        cmp_w2_k, cmp_pos_v, cmp_w1_v, cmp_b1_v, cmp_w2_v, rel_bias, w_br_hg, w_br_nsa, w_out,
        ln1_g, ln1_b, router_grp_w, router_grp_b, router_exp_w, router_exp_b, exp_w1, exp_w3,
        exp_w2, ln2_g, ln2_b,
    )
    return second_block(
        x, c_2, ada_w_2, ada_b_2, norm_g_2, ffn_w_in_2, ffn_w_out_2, sb_w_qkv_2, sb_w_o_2,
        sg_w_in_2, sg_ln_g_2, sg_w_s_2, sg_bias_2, sg_w_out_2, sc_w_in_2, sc_conv_w_2,
        sc_w_out_2, cb_w_qkv_2, cb_rel_bias_2, cb_w_o_2,
    )


_drawn_inputs = setup_inputs


def setup_inputs(seed=0):
    import zlib

    import numpy as np

    out = dict(_drawn_inputs(seed))
    spreads = {}
    factors = {'b_in': 5.6,
     'hg_lb_logits': 4.167,
     'hg_norm_w': 4.765,
     'cmp_pos_k': 8.0,
     'cmp_w1_k': 3.786,
     'cmp_b1_k': 64.0,
     'cmp_w2_k': 4.246,
     'cmp_pos_v': 6.76,
     'cmp_b1_v': 34.875,
     'rel_bias': 3.037,
     'router_grp_b': 22.815,
     'router_exp_b': 16.789}
    for name, (base, spread) in spreads.items():
        noise = np.random.default_rng([zlib.crc32(name.encode()), seed]).standard_normal(out[name].shape)
        drawn = base * np.exp(spread * noise) if base else spread * noise
        out[name] = __import__('jax').numpy.asarray(drawn.astype(out[name].dtype))
    for name, factor in factors.items():
        out[name] = (out[name] * factor).astype(out[name].dtype)
    return out
```

```python
import math
from contextlib import ExitStack

import numpy as np
import concourse.bass as bass
from concourse import mybir

P = 128
T = 512
D = 1024
NT = T // P
KD = D // P
HEADS = 8
GROUPS = 2
REP = HEADS // GROUPS
CHUNK = 32
NCHUNK = T // CHUNK
CPT = P // CHUNK
CMP = 32
STRIDE = 16
NCMP = T // STRIDE - CMP // STRIDE + 1
BUCKETS = 32
MAX_DIST = 128
NEXP = 32
EXP_GROUPS = 4
EPG = NEXP // EXP_GROUPS
DE = 512
CAP = 64
OVB = (2 * T - 1) // CAP
MAIN = NEXP * CAP
SLOTS = 24 * P
SB_HEADS = 16
DFF = 2816
FT = DFF // P
ALPHA = 2 ** 0.25
NEG = -1e30
SCALE = P ** -0.5
SB_SCALE = 64 ** -0.5
Q_H, F_H, I_H, G_H, Q_N, KV_N, GATE_N = 0, 1024, 2048, 3072, 4096, 5120, 6656
MG_H = GATE_N + 3 * HEADS
MG_N = MG_H + D
REL = 2 * T - 1

_at, _c = {}, 0
for _name, _n in (("ident", P), ("ones", P), ("before", P), ("sbmask", P), ("chunk", CPT), ("reset", T),
                  ("zeros", T), ("attmask", P), ("iota", NEXP), ("slot0", NEXP), ("token", NT),
                  ("full", 7), ("block", 16)):
    _at[_name] = (_c, _n)
    _c += _n
NCONST = _c


def shape_constants():
    p = np.arange(P)
    c = np.zeros((P, NCONST), np.float32)

    def put(name, value):
        a, n = _at[name]
        c[:, a:a + n] = value

    put("ident", np.eye(P))
    put("ones", 1.0)
    put("before", p[:, None] < p[None, :])
    put("sbmask", np.where(p[None, :] < p[:, None], 0.0, NEG))
    put("chunk", p[:, None] // CHUNK == np.arange(CPT)[None])
    put("reset", (np.arange(T) % CHUNK != 0)[None])
    put("attmask", (p[:, None] // CHUNK == p[None] // CHUNK) & (p[:, None] <= p[None]))
    put("iota", np.arange(NEXP)[None])
    put("slot0", CAP * np.arange(NEXP)[None])
    put("token", p[:, None] + P * np.arange(NT)[None])
    put("full", CAP * np.arange(1, 8)[None])
    put("block", np.arange(16)[None])
    dist = np.arange(REL) - (T - 1)
    n = np.maximum(dist, 0)
    nf = np.maximum(n, 1).astype(np.float32)
    half = BUCKETS // 2
    large = half + (np.log(nf / half) / math.log(MAX_DIST / half) * (BUCKETS - half)).astype(np.int32)
    bucket = np.where(n < half, n, np.minimum(large, BUCKETS - 1))
    bucket = np.where(dist < 0, BUCKETS, bucket)
    hot = np.zeros((BUCKETS + 1, REL + 1), np.float32)
    hot[bucket, np.arange(REL)] = 1.0
    return {"shape_const": c, "rel_hot": hot, "neg_row": np.full((1, HEADS), NEG, np.float32),
            "no_token": np.zeros((SLOTS, 1), np.int32)}


def block_kernel(nc, io, out):
    f32, i32, u32 = mybir.dt.float32, mybir.dt.int32, mybir.dt.uint32
    ACT, ALU, AX = mybir.ActivationFunctionType, mybir.AluOpType, mybir.AxisListType
    ctx = ExitStack()
    with ctx:
        def sb(name, shape, dt=f32):
            return ctx.enter_context(nc.sbuf_tensor(name, shape, dt))

        sems = {}

        def sem(name):
            if name not in sems:
                sems[name] = ctx.enter_context(nc.semaphore(name))
            return sems[name]

        NS = 4
        ring = sb("ring", [P, NS, 4096])
        xres = sb("xres", [P, NT, D])
        hT = sb("hT", [P, KD, T])
        brn = sb("brn", [P, 2, 4096])
        scr = sb("scr", [P, FT * T])
        rows = sb("rows", [P, 6, D])
        cst = sb("cst", [P, NCONST])
        vec = sb("vec", [P, 3, P])
        mod = sb("mod", [P, 12, KD])
        csil = sb("csil", [P, 2 * KD])
        colb = sb("colb", [P, 40])
        st = sb("st", [P, 96])
        bnb = sb("bnb", [P, NT, 2, 6])
        mv = sb("mv", [P, NT, 2])
        comb = sb("comb", [P, NT, 2])
        dest = sb("dest", [P, NT, 2], i32)
        token = sb("token", [P, NT], i32)
        slot_token = sb("slot_token", [P, SLOTS // P], i32)
        over = sb("over", [P, 16], i32)
        over_token = sb("over_token", [CAP, 1], i32)
        ps = ctx.enter_context(nc.psum_tensor("ps", [P, 8, 512], f32))
        rel_dram = nc.dram_tensor("rel_scratch", (HEADS, REL + 1), f32).ap()
        xn_dram = nc.dram_tensor("xn_scratch", (T, D), f32).ap()
        slot_dram = nc.dram_tensor("slot_scratch", (SLOTS, 1), i32).ap()
        y_dram = nc.dram_tensor("y_scratch", (SLOTS, D), f32).ap()

        def const(name):
            a, n = _at[name]
            return cst[:, a:a + n]

        def grow(ap, n, at=2):
            ap = ap.unsqueeze(at)
            shape = list(ap.shape)
            shape[at] = n
            return ap.to_broadcast(shape)

        ident, ones = const("ident"), const("ones")
        oH = brn[:, 0, :].rearrange("p (k t) -> p k t", k=KD)
        oN = brn[:, 1, :].rearrange("p (k t) -> p k t", k=KD)
        SH1, SC1, G1, SH2, SC2, G2, SHM, SCM, GM, SHF, SCF, GF = range(12)
        ROW_G1, ROW_G2, ROW_GM, ROW_GF, ROW_A, ROW_B = range(6)

        full = [sem(f"bank{b}_full") for b in range(8)]
        empty = [sem(f"bank{b}_empty") for b in range(8)]
        fills = [0] * 8
        filling = {}

        def open_bank(pe, b, name):
            if fills[b]:
                pe.wait_ge(empty[b], fills[b])
            fills[b] += 1
            filling[name] = (b, fills[b])
            return ps[:, b, :]

        def close_bank(name, instruction):
            instruction.then_inc(full[filling[name][0]], 1)

        def filled(eng, name):
            b, n = filling[name]
            eng.wait_ge(full[b], n)
            return ps[:, b, :]

        def emptied(eng, name):
            b, n = filling[name]
            eng.wait_ge(empty[b], n)

        def free_bank(name, instruction):
            instruction.then_inc(empty[filling[name][0]], 1)

        arrived_sem = [sem(f"chunk_slot{s}_full") for s in range(NS)]
        chunk_no = {}
        used_by = {}

        chunk_list = []

        def plan(name, parts):
            chunk_no[name] = len(chunk_list)
            chunk_list.append((name, parts))

        def slot_of(name):
            return ring[:, chunk_no[name] % NS, :]

        arrived_at = {}

        def arrived(pe, name):
            n = chunk_no[name]
            pe.wait_ge(arrived_sem[n % NS], arrived_at[name])
            return slot_of(name)

        def last_use(name, fill):
            used_by[chunk_no[name]] = fill

        def cols(w, a, n):
            return w[0, :, a:a + n].rearrange("(k p) n -> p k n", p=P)

        def plan_wide(name, w, a):
            plan(name, [(lambda s: s.rearrange("p (k n) -> p k n", k=KD), cols(w, a, 512))])

        def plan_quad(name, quad):
            plan(name, [((lambda s, j=j: s[:, j * 1024:(j + 1) * 1024].rearrange("p (k n) -> p k n", k=KD)),
                         cols(w, a, P)) for j, (w, a) in enumerate(quad)])

        def wide(s):
            return s.rearrange("p (k n) -> p k n", k=KD)

        def quad(s, j):
            return s[:, j * 1024:(j + 1) * 1024].rearrange("p (k n) -> p k n", k=KD)

        A = io
        ada_todo = [(1, c) for c in (4, 5, 6, 7, 8, 9, 10, 11)] + [(2, c) for c in range(12)]
        ada_at = {("attn", h): ada_todo[h] for h in range(8)}
        for h in range(8):
            ada_at[("hg", h)] = ada_todo[8 + h]
        for j in range(4):
            ada_at[("merge", j)] = ada_todo[16 + j]

        def plan_ada(m, c):
            plan_wide(("ada", m, c), A["ada_w"] if m == 1 else A["ada_w_2"], 512 * c)

        for c in range(4):
            plan_ada(1, c)
        for c in range(3):
            plan_wide(("kv", c), A["w_in"], KV_N + 512 * c)
        for kv in ("k", "v"):
            plan(("cmp", kv), [(lambda s: s.rearrange("p (t n) -> p t n", t=CMP),
                                A[f"cmp_w1_{kv}"][0].rearrange("(t p) n -> p t n", p=P))])
        for h in range(8):
            if h in (0, 1, 3, 5):
                j = (h + 1) // 2
                plan(("nq", j), [(lambda s: s[:, 0:2048].rearrange("p (k n) -> p k n", k=KD),
                                  cols(A["w_in"], Q_N + 256 * j, 256))])
            plan_ada(*ada_at[("attn", h)])

        def plan_head(h):
            w = A["w_in"]
            plan_quad(("hg", h), [(w, Q_H + P * h), (w, F_H + P * h), (w, G_H + P * h), (w, I_H + P * h)])

        plan_head(0)
        for h in range(8):
            if h < 7:
                plan_head(h + 1)
            plan_ada(*ada_at[("hg", h)])
        for j in range(8):
            plan_quad(("merge", j), [(A["w_in"], MG_H + P * j), (A["w_in"], MG_N + P * j),
                                     (A["w_br_hg"], P * j), (A["w_br_nsa"], P * j)])
            if j < 4:
                plan_ada(*ada_at[("merge", j)])
        for c in range(2):
            plan_wide(("wout", c), A["w_out"], 512 * c)
        AFTER_MOE = len(chunk_list)
        for j in range(KD):
            w = A["sb_w_qkv_2"]
            plan_quad(("sb", j), [(w, P * j), (w, D + P * j), (w, 2 * D + P * j)])
        for c in range(2):
            plan_wide(("wo", c), A["sb_w_o_2"], 512 * c)
        for c in range(FT // 2):
            w = A["ffn_w_in_2"]
            plan(("fi", c), [((lambda s, j=j: s[:, j * 2048:(j + 1) * 2048].rearrange("p (k n) -> p k n", k=KD)),
                              cols(w, j * DFF + 256 * c, 256)) for j in range(2)])
        for c in range(-(-FT // 4)):
            n = min(4, FT - 4 * c)
            plan(("fo", c), [((lambda s, n=n: s[:, 0:n * D].rearrange("p (k n) -> p k n", k=n)),
                              A["ffn_w_out_2"][0, 4 * P * c:4 * P * c + n * P, :].rearrange("(k p) n -> p k n", p=P))])
        count = [0] * NS
        for name, parts in chunk_list:
            s = chunk_no[name] % NS
            count[s] += 16 * len(parts)
            arrived_at[name] = count[s]

        class Cut:

            def __init__(self, base=0):
                self.at = base

            def __call__(self, n):
                a, self.at = self.at, self.at + n
                assert self.at <= FT * T, self.at
                return scr[:, a:a + n]

        cut = Cut()
        bias_back = cut(HEADS * T).rearrange("p (h j) -> p h j", h=HEADS)
        biasT = bias_back[:, :, ::-1]
        cbias = cut(HEADS * NT * NCMP).rearrange("p (h i n) -> p h i n", h=HEADS, i=NT)
        cmask = cut(NT * NCMP).rearrange("p (i n) -> p i n", i=NT)
        gates = sb("gates", [P, NT, 24])[:, :, :]
        kcmpT = sb("kcmpT", [P, GROUPS * NCMP])[:, :]
        vcmp = cut(GROUPS * P).rearrange("p (g n) -> p g n", g=GROUPS)
        w2cmp = cut(2 * P).rearrange("p (a n) -> p a n", a=2)
        attn_base = cut.at
        qT = cut(2 * T).rearrange("p (a n) -> p a n", a=2)
        SW = 2 * T + 32
        prob = cut(2 * SW).rearrange("p (a n) -> p a n", a=2)
        probT = cut(2 * 9 * P).rearrange("p (a k n) -> p a k n", a=2, k=9)
        kfull = brn[:, 0, 0:2048].rearrange("p (a g t) -> p a g t", a=2, g=GROUPS)
        vfull = brn[:, 0, 2048:4096].rearrange("p (a i n) -> p a i n", a=2, i=NT)
        kvc = brn[:, 1, 0:2048].rearrange("p (a g t) -> p a g t", a=2, g=GROUPS)
        cut2 = Cut(attn_base)
        blocks = cut2(CMP * GROUPS * NCMP).rearrange("p (t g n) -> p t g n", t=CMP, g=GROUPS)
        hid = cut2(2 * GROUPS * NCMP).rearrange("p (a n) -> p a n", a=2)
        hsig = cut2(2 * GROUPS * NCMP).rearrange("p (a n) -> p a n", a=2)
        wgate = cut2(KD * 24).rearrange("p (k n) -> p k n", k=KD)
        vbias = cut2(T).rearrange("p (a n) -> p a n", a=2)
        gbias = cut2(24)
        tab = sb("tab", [P, HEADS])
        xn = scr[:, attn_base:attn_base + NT * D].rearrange("p (i n) -> p i n", i=NT)
        longb_back = brn[:, :, :].rearrange("p a n -> p (a n)")[:, 0:HEADS * 896].rearrange("p (h j) -> p h j", h=HEADS)
        longb = longb_back[:, :, ::-1]
        hot = hT[0:BUCKETS + 1, 0:2, :].rearrange("p a n -> p (a n)")
        relrow = hT[0:HEADS, 2:4, :].rearrange("p a n -> p (a n)")
        packs = rows[:, 0:1, 0:3 * P].rearrange("p a (b n) -> p (a b) n", b=3)

        block = ctx.enter_context(nc.Block())

        c_col = lambda k: vec[:, 0, k:k + 1]
        ADAB1 = 16
        POSK, POSV = 64, 96
        BIN, BMG, ADAB2, HGN, B1 = 0, 52, 68, 116, 124

        def bin_col(a):
            j = a // P if a < GATE_N else BMG + (a - MG_H) // P
            return vec[:, 1, j:j + 1]

        def gemm(pe, dst, lhs, rhs, n=KD, start=True):
            for k in range(n):
                last = pe.matmul(dst, lhs(k), rhs(k), start=start and k == 0, stop=k == n - 1)
            return last

        def pe_ada(pe, m, c, bank):
            name = ("ada", m, c)
            s = wide(arrived(pe, name))
            dst = open_bank(pe, bank, name)
            for j in range(4):
                last = gemm(pe, dst[:, j:j + 1], lambda k: s[:, k, j * P:(j + 1) * P],
                            lambda k: csil[:, (m - 1) * KD + k:(m - 1) * KD + k + 1])
            close_bank(name, last)
            last_use(name, name)

        def pe_start(pe):
            pe.wait_ge(sem("const_in"), 16)
            pe.wait_ge(sem("packs_in"), 16 * N_PACK)
            t = open_bank(pe, 7, "vec")
            for b, n in ((0, P), (1, 126), (2, 48)):
                last = pe.transpose(t[:, b * P:b * P + n], packs[0:n, b, :], ident[0:n, 0:n])
            close_bank("vec", last)
            pe.wait_ge(sem("rel_in"), 48)
            for c in range(2):
                t = open_bank(pe, 5 + c, ("rel", c))
                close_bank(("rel", c), pe.matmul(t[0:HEADS, :], tab[0:BUCKETS + 1, :],
                                                 hot[:, c * 512:(c + 1) * 512], start=True, stop=True))
            pe.wait_ge(sem("silu_c"), 1)
            for c in range(4):
                pe_ada(pe, 1, c, c % 2)
            pe.wait_ge(sem("ln_done"), 4)
            pe_transposes(pe, "h1", xn)

        def pe_transposes(pe, name, src):
            for k in range(KD):
                t = open_bank(pe, 2 + k % 4, (name, k))
                for i in range(NT):
                    last = pe.transpose(t[:, i * P:(i + 1) * P], src[:, i, k * P:(k + 1) * P], ident)
                close_bank((name, k), last)

        def feature_major(pe, bank, name, w, src=None):
            t = open_bank(pe, bank, name)
            close_bank(name, gemm(pe, t, w, lambda k: (src if src is not None else hT)[:, k, :]))

        def pe_kv(pe):
            for k in range(KD):
                emptied(pe, ("h1", k))
            for c in range(3):
                s = wide(arrived(pe, ("kv", c)))
                nf = 4 if c == 0 else 2
                for j in range(nf):
                    feature_major(pe, j, ("kvT", c, j), lambda k: s[:, k, j * P:(j + 1) * P])
                name = ("kvT", c, nf - 1)
                if c:
                    for i2 in range(2):
                        name = ("vtok", c, i2)
                        t = open_bank(pe, 4 + i2, name)
                        for i in (2 * i2, 2 * i2 + 1):
                            last = gemm(pe, t[:, (i % 2) * 256:(i % 2) * 256 + 256],
                                        lambda k: hT[:, k, i * P:(i + 1) * P], lambda k: s[:, k, 256:512])
                        close_bank(name, last)
                last_use(("kv", c), name)
            pe.wait_ge(sem("small_in"), 16 * N_SMALL)
            t = open_bank(pe, 6, "gate")
            for i in range(NT):
                last = gemm(pe, t[:, i * 24:(i + 1) * 24], lambda k: hT[:, k, i * P:(i + 1) * P],
                            lambda k: wgate[:, k, :])
            close_bank("gate", last)
            for a, kv in enumerate("kv"):
                s = arrived(pe, ("cmp", kv)).rearrange("p (t n) -> p t n", t=CMP)
                pe.wait_ge(sem("blocks_ready"), 4 * (a + 1))
                name = ("hid", kv)
                t = open_bank(pe, 7, name)
                last = gemm(pe, t[:, 0:GROUPS * NCMP], lambda k: s[:, k, :],
                            lambda k: blocks[:, k, :, :].rearrange("p g n -> p (g n)"), n=CMP)
                close_bank(name, last)
                last_use(("cmp", kv), name)
            emptied(pe, ("hid", "v"))
            t = open_bank(pe, 0, "kcmp")
            close_bank("kcmp", pe.matmul(t[:, 0:GROUPS * NCMP], w2cmp[:, 0, :], hid[:, 0, :], start=True, stop=True))
            t = open_bank(pe, 1, "vcmp")
            for g in range(GROUPS):
                last = pe.matmul(t[0:NCMP, g * P:(g + 1) * P], hid[:, 1, g * NCMP:(g + 1) * NCMP],
                                 w2cmp[:, 1, :], start=True, stop=True)
            close_bank("vcmp", last)

        UNITS = [(h, i) for h in range(HEADS) for i in range(NT)]

        def pe_attention(pe):
            emptied(pe, "kcmp")
            emptied(pe, "vcmp")
            for c in (1, 2):
                for j in range(2):
                    emptied(pe, ("kvT", c, j))
                    emptied(pe, ("vtok", c, j))

            def query(h):
                s = arrived(pe, ("nq", h // 2))[:, 0:2048].rearrange("p (k n) -> p k n", k=KD)
                feature_major(pe, 4, ("nqT", h), lambda k: s[:, k, (h % 2) * P:(h % 2 + 1) * P])
                if h % 2:
                    last_use(("nq", h // 2), ("nqT", h))

            def scores(u):
                h, i = UNITS[u]
                g, n = h // REP, P * (i + 1)
                if i == 0:
                    emptied(pe, ("nqT", h))
                q = qT[:, h % 2, i * P:(i + 1) * P]
                for a in range(2):
                    name = ("S", a, u)
                    t = open_bank(pe, 2 * a + u % 2, name)
                    close_bank(name, pe.matmul(t[:, 0:n], q, kfull[:, a, g, 0:n], start=True, stop=True))
                t = open_bank(pe, 4, ("S", 2, u))
                close_bank(("S", 2, u), pe.matmul(t[:, 0:NCMP], q, kcmpT[:, g * NCMP:(g + 1) * NCMP],
                                                  start=True, stop=True))

            query(0)
            scores(0)
            for u, (h, i) in enumerate(UNITS):
                if i == 1 and h + 1 < HEADS:
                    query(h + 1)
                if u + 1 < len(UNITS):
                    scores(u + 1)
                if i == 2:
                    pe_ada(pe, *ada_at[("attn", h)], 7)
                for a in range(2):
                    pe.wait_ge(sem("prob_scaled"), 2 * u + a + 1)
                    t = open_bank(pe, 5 + a, ("T", a, u))
                    for j in range(i + 1):
                        last = pe.transpose(t[:, j * P:(j + 1) * P],
                                            prob[:, u % 2, a * T + j * P:a * T + (j + 1) * P], ident)
                    close_bank(("T", a, u), last)
                pe.wait_ge(sem("prob_c_scaled"), 3 * (u + 1))
                t = open_bank(pe, 4, ("T", 2, u))
                close_bank(("T", 2, u), pe.transpose(t[0:NCMP, 0:P], prob[:, u % 2, 2 * T:2 * T + NCMP], ident))
                t = open_bank(pe, 7, ("O", u))
                for a in range(2):
                    emptied(pe, ("T", a, u))
                    for j in range(i + 1):
                        g = h // REP
                        pe.matmul(t[:, 0:P], vfull[:, a, j, g * P:(g + 1) * P], probT[:, u % 2, 4 * a + j, :],
                                  start=a == 0 and j == 0, stop=False)
                emptied(pe, ("T", 2, u))
                close_bank(("O", u), pe.matmul(t[:, 0:P], vcmp[0:NCMP, h // REP, :], probT[0:NCMP, u % 2, 8, :],
                                               start=False, stop=True))

        def state_ready(eng, h, n):
            i, c = (n - 1) // CPT, (n - 1) % CPT
            if c == CPT - 1 or n == NCHUNK - 1:
                emptied(eng, ("U", h, i))
            else:
                eng.wait_ge(sem("hg_state"), 11 * h + 3 * i + c + 1)

        def pe_hgrn(pe):
            def project(h, which):
                s = arrived(pe, ("hg", h))
                if which < 3:
                    name = (("hq", "hf", "hg")[which], h)
                    feature_major(pe, which, name, lambda k: quad(s, which)[:, k, :])
                else:
                    t = open_bank(pe, 3, ("hi", h))
                    w = quad(s, 3)
                    for i in range(NT):
                        last = gemm(pe, t[:, i * P:(i + 1) * P], lambda k: hT[:, k, i * P:(i + 1) * P],
                                    lambda k: w[:, k, :])
                    close_bank(("hi", h), last)
                    last_use(("hg", h), ("hi", h))

            for which in range(4):
                project(0, which)
            for h in range(HEADS):
                more = h + 1 < HEADS
                if more:
                    project(h + 1, 0)
                    project(h + 1, 1)
                pe.wait_ge(sem("hg_kend"), h + 1)
                t = open_bank(pe, 4, ("kendT", h))
                for i in range(NT):
                    last = pe.transpose(t[:, i * P:(i + 1) * P], hKN[:, i * P:(i + 1) * P], ident)
                close_bank(("kendT", h), last)
                t = open_bank(pe, 5, ("att", h))
                for i in range(NT):
                    c = slice(i * P, (i + 1) * P)
                    last = pe.matmul(t[:, c], hKI[:, c], hQ[:, h % 2, c], start=True, stop=True)
                close_bank(("att", h), last)
                if more:
                    project(h + 1, 2)
                    project(h + 1, 3)
                emptied(pe, ("hi", h))
                for i in range(NT):
                    if i < NT - 1:
                        pe.wait_ge(sem("hg_kblocks"), (NT - 1) * h + i + 1)
                    else:
                        emptied(pe, ("kendT", h))
                    t = open_bank(pe, 6 + i % 2, ("U", h, i))
                    for c in range(CPT):
                        last = pe.matmul(t[:, c * P:(c + 1) * P], hKX[:, i % 2, c, :], hV[:, h % 2, i, :],
                                         start=True, stop=True)
                    close_bank(("U", h, i), last)
                emptied(pe, ("att", h))
                t = open_bank(pe, 4, ("oT", h))
                for i in range(NT):
                    c = slice(i * P, (i + 1) * P)
                    last = pe.matmul(t[:, c], hV[:, h % 2, i, :], hAT[:, c], start=True, stop=False,
                                     skip_group_check=True)
                    for n in range(CPT * i, CPT * (i + 1)):
                        if n:
                            state_ready(pe, h, n)
                            last = pe.matmul(t[:, n * CHUNK:(n + 1) * CHUNK], hS[:, n, :],
                                             hQ[:, h % 2, n * CHUNK:(n + 1) * CHUNK], start=False,
                                             stop=n == CPT * (i + 1) - 1, skip_group_check=True)
                close_bank(("oT", h), last)
                pe_ada(pe, *ada_at[("hg", h)], 6)
                pe.wait_ge(sem("hg_square"), h + 1)
                t = open_bank(pe, 5, ("ss", h))
                close_bank(("ss", h), pe.matmul(t, ones, hT2[:, :], start=True, stop=True))

        def pe_merge(pe):
            for j in range(KD):
                if j >= 4:
                    for x in (2 * j - 8, 2 * j - 7):
                        pe.wait_ge(sem("gate_diag"), x + 1)
                        t = open_bank(pe, 7 - 4 * (j % 2), ("row", x))
                        close_bank(("row", x), pe.matmul(t, ones, mD[:, x % 2, :], start=True, stop=True))
                s = arrived(pe, ("merge", j))
                b = 4 * (j % 2)
                feature_major(pe, b, ("mgh", j), lambda k: quad(s, 0)[:, k, :])
                feature_major(pe, b + 1, ("mgn", j), lambda k: quad(s, 1)[:, k, :])
                feature_major(pe, b + 3, ("mN", j), lambda k: quad(s, 3)[:, k, :], oN)
                if j == 0:
                    pe.wait_ge(sem("hg_out"), 2 * HEADS)
                feature_major(pe, b + 2, ("mH", j), lambda k: quad(s, 2)[:, k, :], oH)
                last_use(("merge", j), ("mH", j))
                if j < 4:
                    pe_ada(pe, *ada_at[("merge", j)], 7 - b)
            pe.wait_ge(sem("merged"), KD)
            w = [wide(arrived(pe, ("wout", c))) for c in range(2)]
            for i in range(NT):
                for c in range(2):
                    name = ("wout", c, i)
                    t = open_bank(pe, 4 * c + i, name)
                    close_bank(name, gemm(pe, t, lambda k: mT[:, k, i * P:(i + 1) * P], lambda k: w[c][:, k, :]))
            for c in range(2):
                last_use(("wout", c), name)

        cut3 = Cut()
        hQ = cut3(2 * T).rearrange("p (a n) -> p a n", a=2)
        hF = cut3(2 * T).rearrange("p (a n) -> p a n", a=2)
        hG = cut3(2 * T).rearrange("p (a n) -> p a n", a=2)
        hV = cut3(2 * T).rearrange("p (a i n) -> p a i n", a=2, i=NT)
        hK, hB, hEB, hT2, hKI, hKN, hAT, hO = (cut3(T) for _ in range(8))
        hKX = cut3(2 * CPT * P).rearrange("p (a c n) -> p a c n", a=2, c=CPT)
        hS = cut3(NCHUNK * P).rearrange("p (c n) -> p c n", c=NCHUNK)
        cut4 = Cut()
        mT = cut4(KD * T).rearrange("p (k t) -> p k t", k=KD)
        mS = cut4(4 * T).rearrange("p (a n) -> p a n", a=4)
        mD = cut4(2 * T).rearrange("p (a n) -> p a n", a=2)
        mP = cut4(4 * T).rearrange("p (a n) -> p a n", a=4)

        cut5 = Cut()
        xn2 = cut5(NT * D).rearrange("p (i n) -> p i n", i=NT)
        lg = cut5(NT * 36).rearrange("p (i n) -> p i n", i=NT)
        g8, gtop, etop = (cut5(NT * 8).rearrange("p (i n) -> p i n", i=NT) for _ in range(3))
        gat, eat = (cut5(NT * 8).rearrange("p (i n) -> p i n", i=NT).bitcast(u32) for _ in range(2))
        gexp, gone = (cut5(NT * EXP_GROUPS).rearrange("p (i n) -> p i n", i=NT) for _ in range(2))
        gsum, emax2 = (cut5(NT) for _ in range(2))
        masked, hot0, hot1, both, rank, place, tmp32 = (cut5(NT * NEXP).rearrange("p (i n) -> p i n", i=NT) for _ in range(7))
        counts, blocks_of, block_end, over0, tmp1 = (cut5(NEXP) for _ in range(5))
        cmp7 = cut5(NEXP * 7).rearrange("p (e n) -> p e n", e=NEXP)
        cmp16 = cut5(15 * NEXP).rearrange("p (b e) -> p b e", b=15)
        idxf = cut5(NT * 3).rearrange("p (i n) -> p i n", i=NT)
        slotf = cut5(NT * 2).rearrange("p (i n) -> p i n", i=NT)
        overf = cut5(16)
        tabi = cut5(P).bitcast(i32)
        tabf = cut5(P)
        assert cut5.at <= 9216
        cut5.at = 9216
        rw = cut5(KD * 36).rearrange("p (k n) -> p k n", k=KD)
        rbias = cut5(36)
        cut6 = Cut()
        gx = cut6(D)
        xT = cut6(KD * P).rearrange("p (k n) -> p k n", k=KD)
        sg = cut6(2 * DE).rearrange("p (a n) -> p a n", a=2)
        hx = cut6(2 * DE).rearrange("p (a n) -> p a n", a=2)
        aT = cut6(2 * 4 * CAP).rearrange("p (a k n) -> p a k n", a=2, k=4)
        ysb = cut6(2 * 512).rearrange("p (a n) -> p a n", a=2)
        cut6.at = max(cut6.at, 0)
        yg = scr[:, 0:2 * NT * D].rearrange("p (i a n) -> p i a n", i=NT, a=2)
        w0 = chunk_no[("wout", 0)]
        moe_slot = [ring[:, (w0 - 2) % NS, :], ring[:, (w0 - 1) % NS, :], brn[:, 0, :], brn[:, 1, :],
                    ring[:, w0 % NS, :], ring[:, (w0 + 1) % NS, :]]
        cut7 = Cut()
        zq, zk = (cut7(2 * T).rearrange("p (a n) -> p a n", a=2) for _ in range(2))
        zv = cut7(2 * T).rearrange("p (a i n) -> p a i n", a=2, i=NT)
        zA, zU, zT = (cut7(2 * T).rearrange("p (a n) -> p a n", a=2) for _ in range(3))
        zR = cut7(2 * (T + 4)).rearrange("p (a n) -> p a n", a=2)
        yb = scr[:, 0:NT * D].rearrange("p (i n) -> p i n", i=NT)
        xn3 = brn[:, 0, :].rearrange("p (i n) -> p i n", i=NT)
        sT = oN
        ff = scr[:, :].rearrange("p (f t) -> p f t", f=FT)
        fS = brn[:, 1, 0:2048].rearrange("p (a n) -> p a n", a=4)
        ZU = [(j, hh, i) for j in range(KD) for hh in range(2) for i in range(NT)]

        def pe_router(pe):
            pe.wait_ge(sem("xn2_done"), NT)
            pe_transposes(pe, "h2", xn2)
            for k in range(KD):
                emptied(pe, ("h2", k))
            pe.wait_ge(sem("router_in"), 64)
            t = open_bank(pe, 0, "logits")
            for i in range(NT):
                last = gemm(pe, t[:, i * 36:(i + 1) * 36], lambda k: hT[:, k, i * P:(i + 1) * P], lambda k: rw[:, k, :])
            close_bank("logits", last)
            pe.wait_ge(sem("chosen"), 1)
            t = open_bank(pe, 1, "rank")
            for i in range(NT + 1):
                for j in range(min(i + 1, NT)):
                    last = pe.matmul(t[:, i * NEXP:(i + 1) * NEXP], const("before") if j == i else ones, both[:, j, :],
                                     start=j == 0, stop=j == min(i, NT - 1))
            close_bank("rank", last)
            pe.wait_ge(sem("slots_float"), 1)
            t = open_bank(pe, 0, "slots")
            close_bank("slots", pe.transpose(t[:, 0:SLOTS // P], tabf[0:SLOTS // P, :], ident[0:SLOTS // P, 0:SLOTS // P]))

        fills_before_moe = [0] * 8

        def pe_experts(pe):
            base = fills_before_moe
            base[:] = fills

            def gathered(p):
                pe.wait_ge(sem("gathered"), 16 * (p + 1) if isinstance(p, int) else p * 16 + 16)
                for b in range(2):
                    pe.wait_ge(empty[b], p + base[b])
                    for k in range(4 * b, 4 * b + 4):
                        last = pe.transpose(ps[:, b, (k % 4) * P:(k % 4 + 1) * P], gx[:, k * P:(k + 1) * P], ident)
                    last.then_inc(full[b], 1)

            def up(p, a):
                if a == 0:
                    for b in range(2):
                        pe.wait_ge(empty[b], p + (base[b] + 1))
                pe.wait_ge(empty[2 + a], p + base[2 + a])
                w = []
                for m in range(2):
                    pe.wait_ge(sem(f"moe_chunk{3 * a + m}_full"), p * 16 + 16)
                    w.append(moe_slot[3 * a + m].rearrange("p (k n) -> p k n", k=KD))
                for k in range(KD):
                    for m in range(2):
                        last = pe.matmul(ps[m * CAP:(m + 1) * CAP, 2 + a, :], xT[:, k, a * CAP:(a + 1) * CAP],
                                         w[m][:, k, :], start=k == 0, stop=k == KD - 1)
                last.then_inc(full[2 + a], 1)

            def down(p, a):
                pe.wait_ge(empty[2 + a], p + (base[2 + a] + 1))
                pe.wait_ge(empty[4 + a], p + base[4 + a])
                for k in range(4):
                    last = pe.matmul(ps[:, 4 + a, k * CAP:(k + 1) * CAP], hx[0:CAP, a, k * P:(k + 1) * P],
                                     ident[0:CAP, 0:CAP], start=True, stop=True)
                last.then_inc(full[4 + a], 1)
                pe.wait_ge(empty[4 + a], p + (base[4 + a] + 1))
                pe.wait_ge(empty[6 + a], p + base[6 + a])
                pe.wait_ge(sem(f"moe_chunk{3 * a + 2}_full"), p * 16 + 16)
                w = moe_slot[3 * a + 2].rearrange("p (k n) -> p k n", k=4)
                for k in range(4):
                    for m in range(2):
                        last = pe.matmul(ps[m * CAP:(m + 1) * CAP, 6 + a, :], aT[:, a, k, :],
                                         w[:, k, m * 512:(m + 1) * 512], start=k == 0, stop=k == 3)
                last.then_inc(full[6 + a], 1)

            gathered(0)
            with pe.Fori(0, NEXP // 2 - 1) as p:
                up(p, 0)
                down(p, 0)
                up(p, 1)
                gathered(p + 1)
                down(p, 1)
            p = NEXP // 2 - 1
            up(p, 0)
            down(p, 0)
            up(p, 1)
            down(p, 1)
            for b in range(8):
                fills[b] += NEXP // 2
            filling["moe_last"] = (7, fills[7])
            pe.wait_ge(sem("over_known"), 1)
            n = pe.value_load(over[0:1, 15:16], min_val=0, max_val=OVB)
            with pe.If(n > 0):
                with pe.Fori(0, n) as b:
                    pe.wait_ge(sem("ov_x"), b * 16 + 16)
                    for k in range(KD):
                        last = pe.matmul(ps[:, 0, k * CAP:(k + 1) * CAP], gx[0:CAP, k * P:(k + 1) * P], ident[0:CAP, 0:CAP],
                                         start=True, stop=True)
                    last.then_inc(sem("ov_gt"), 1)
                    pe.wait_ge(sem("ov_xt"), b + 1)
                    pe.wait_ge(sem("ov_w"), b * 48 + 48)
                    for k in range(KD):
                        for m in range(2):
                            w = moe_slot[m].rearrange("p (k n) -> p k n", k=KD)
                            last = pe.matmul(ps[m * CAP:(m + 1) * CAP, 2, :], xT[:, k, 0:CAP], w[:, k, :],
                                             start=k == 0, stop=k == KD - 1)
                    last.then_inc(sem("ov_h"), 1)
                    pe.wait_ge(sem("ov_a"), b + 1)
                    for k in range(4):
                        last = pe.matmul(ps[:, 4, k * CAP:(k + 1) * CAP], hx[0:CAP, 0, k * P:(k + 1) * P], ident[0:CAP, 0:CAP],
                                         start=True, stop=True)
                    last.then_inc(sem("ov_at"), 1)
                    pe.wait_ge(sem("ov_ate"), b + 1)
                    w = moe_slot[2].rearrange("p (k n) -> p k n", k=4)
                    for k in range(4):
                        for m in range(2):
                            last = pe.matmul(ps[m * CAP:(m + 1) * CAP, 6, :], aT[:, 0, k, :],
                                             w[:, k, m * 512:(m + 1) * 512], start=k == 0, stop=k == 3)
                    last.then_inc(sem("ov_y"), 1)
            pe.wait_ge(sem("ov_done"), 1)

        def pe_sb(pe):
            pe.wait_ge(sem("xn3_done"), NT)
            pe_transposes(pe, "h3", xn3)
            for k in range(KD):
                emptied(pe, ("h3", k))

            def project(j):
                s = arrived(pe, ("sb", j))
                feature_major(pe, 5, ("sq", j), lambda k: quad(s, 0)[:, k, :])
                feature_major(pe, 6, ("sk", j), lambda k: quad(s, 1)[:, k, :])
                t = open_bank(pe, 7, ("sv", j))
                for i in range(NT):
                    last = gemm(pe, t[:, i * P:(i + 1) * P], lambda k: hT[:, k, i * P:(i + 1) * P],
                                lambda k: quad(s, 2)[:, k, :])
                close_bank(("sv", j), last)
                last_use(("sb", j), ("sv", j))

            def scores(u):
                j, hh, i = ZU[u]
                if hh == 0 and i == 0:
                    for x in ("sq", "sk", "sv"):
                        emptied(pe, (x, j))
                r, n = slice(64 * hh, 64 * hh + 64), P * (i + 1)
                t = open_bank(pe, u % 2, ("z", u))
                close_bank(("z", u), pe.matmul(t[:, 0:n], zq[r, j % 2, i * P:(i + 1) * P], zk[r, j % 2, 0:n],
                                               start=True, stop=True))

            project(0)
            scores(0)
            for u, (j, hh, i) in enumerate(ZU):
                if hh == 0 and i == 2 and j + 1 < KD:
                    project(j + 1)
                if u + 1 < len(ZU):
                    scores(u + 1)
                pe.wait_ge(sem("sb_weights"), u + 1)
                t = open_bank(pe, 2 + u % 2, ("zT", u))
                for k in range(i + 1):
                    last = pe.transpose(t[:, k * P:(k + 1) * P], zA[:, u % 2, k * P:(k + 1) * P], ident)
                close_bank(("zT", u), last)
                emptied(pe, ("zT", u))
                r = slice(64 * hh, 64 * hh + 64)
                t = open_bank(pe, 4, ("zO", u))
                for k in range(i + 1):
                    last = pe.matmul(t[r, 0:P], zv[:, j % 2, k, 64 * hh:64 * hh + 64], zT[:, u % 2, k * P:(k + 1) * P],
                                     start=k == 0, stop=k == i)
                close_bank(("zO", u), last)
            emptied(pe, ("zO", len(ZU) - 1))
            w = [wide(arrived(pe, ("wo", c))) for c in range(2)]
            for i in range(NT):
                for c in range(2):
                    name = ("wo", c, i)
                    t = open_bank(pe, 4 * c + i, name)
                    close_bank(name, gemm(pe, t, lambda k: sT[:, k, i * P:(i + 1) * P], lambda k: w[c][:, k, :]))
            for c in range(2):
                last_use(("wo", c), name)

        def pe_ffn(pe):
            pe.wait_ge(sem("xn4_done"), NT)
            pe_transposes(pe, "h4", xn3)
            for k in range(KD):
                emptied(pe, ("h4", k))
            for c in range(FT // 2):
                s = arrived(pe, ("fi", c))
                for x in range(2):
                    f = 2 * c + x
                    for m in range(2):
                        w = s[:, m * 2048:(m + 1) * 2048].rearrange("p (k n) -> p k n", k=KD)
                        feature_major(pe, 2 * (f % 4) + m, ("fgu", m, f), lambda k: w[:, k, x * P:(x + 1) * P])
                last_use(("fi", c), ("fgu", 1, f))
            t = {}
            for f in range(FT):
                s = arrived(pe, ("fo", f // 4)) if f % 4 == 0 else s
                emptied(pe, ("fgu", 1, f))
                w = s[:, (f % 4) * D:(f % 4 + 1) * D]
                for i in range(NT):
                    for c in range(2):
                        name = ("fo", c, i)
                        if f == 0:
                            t[c, i] = open_bank(pe, 4 * c + i, name)
                        last = pe.matmul(t[c, i], ff[:, f, i * P:(i + 1) * P], w[:, c * 512:(c + 1) * 512],
                                         start=f == 0, stop=f == FT - 1)
                        if f == FT - 1:
                            close_bank(name, last)
                        elif f % 4 == 3 and c == 1 and i == NT - 1:
                            last.then_inc(sem("fo_used"), 1)

        N_PACK = 13
        N_SMALL = 6
        pe_stages = [pe_start, pe_kv, pe_attention, pe_hgrn, pe_merge, pe_router, pe_experts, None, pe_sb, pe_ffn]

        @block.tensor
        def _(pe):
            for stage in pe_stages:
                if stage:
                    stage(pe)

        @block.sync
        def _(sp):
            def load(n):
                for view, src in chunk_list[n][1]:
                    sp.dma_start(view(slot_of(chunk_list[n][0])), src).then_inc(arrived_sem[n % NS], 16)

            for n in range(AFTER_MOE):
                if n >= NS:
                    if n - NS not in used_by:
                        break
                    filled(sp, used_by[n - NS])
                load(n)
            w = A["exp_w1"][0], A["exp_w3"][0], A["exp_w2"][0]

            def expert_part(x, e):
                kind, k = x % 3, (KD, KD, 4)[x % 3]
                src = w[kind][bass.ds(e, 1), :, :].rearrange("a (k p) n -> p (a k) n", p=P)
                sp.dma_start(moe_slot[x].rearrange("p (k n) -> p k n", k=k), src).then_inc(sem(f"moe_chunk{x}_full"), 16)

            user = [2, 2, 6, 3, 3, 7]
            first = {b: filling["moe_last"][1] - NEXP // 2 + (fills_before_moe[b] - fills_before_moe[7]) for b in (2, 3, 6, 7)}
            for x in range(6):
                if x == 0:
                    filled(sp, used_by[chunk_no[("merge", 6)]])
                elif x == 1:
                    filled(sp, used_by[chunk_no[("merge", 7)]])
                elif x == 4:
                    filled(sp, ("wout", 1, NT - 1))
                expert_part(x, x // 3)
            with sp.Fori(1, NEXP // 2) as p:
                for x in range(6):
                    sp.wait_ge(full[user[x]], p + first[user[x]])
                    expert_part(x, p * 2 + x // 3)
            sp.wait_ge(sem("over_known"), 1)
            n = sp.value_load(over[0:1, 15:16], min_val=0, max_val=OVB)
            filled(sp, "moe_last")
            with sp.If(n > 0):
                with sp.Fori(0, n) as b:
                    e = sp.value_load(over[0:1, bass.ds(b, 1)], min_val=0, max_val=NEXP - 1)
                    sp.wait_ge(sem("ov_free"), b + 1)
                    for x in range(3):
                        k = (KD, KD, 4)[x]
                        sp.dma_start(moe_slot[x].rearrange("p (k n) -> p k n", k=k),
                                     w[x][bass.ds(e, 1), :, :].rearrange("a (k p) n -> p (a k) n", p=P)).then_inc(sem("ov_w"), 16)
            sp.wait_ge(sem("ov_done"), 1)
            for n in range(AFTER_MOE, len(chunk_list)):
                if n - NS >= AFTER_MOE:
                    if chunk_list[n - NS][0][0] == "fo":
                        sp.wait_ge(sem("fo_used"), chunk_list[n - NS][0][1] + 1)
                    elif n - NS in used_by:
                        filled(sp, used_by[n - NS])
                    else:
                        break
                load(n)
            sp.wait_ge(sem("out_ready"), NT)
            sp.dma_start(out[0].rearrange("(i p) n -> p i n", p=P), xres[:, :, :]).then_inc(sem("out_stored"), 16)
            sp.wait_ge(sem("out_stored"), 16)

        def pool_start(g):
            g.dma_start(slot_dram, A["no_token"]).then_inc(sem("slots_clear"), 16)
            for c in range(2):
                emptied(g, ("rel", c))
            g.dma_start(rel_dram, relrow[:, :]).then_inc(sem("rel_stored"), 16)
            g.wait_ge(sem("rel_stored"), 16)
            g.dma_start(longb_back, bass.AP(tensor=rel_dram.tensor, offset=0,
                                            ap=[[1, P], [REL + 1, HEADS], [1, 896]])).then_inc(sem("bias_in"), 16)
            g.dma_start(bias_back, bass.AP(tensor=rel_dram.tensor, offset=T - P,
                                           ap=[[1, P], [REL + 1, HEADS], [1, T]])).then_inc(sem("bias_in"), 16)

            g.wait_ge(sem("const_in"), 16)
            g.dma_start(y_dram[MAIN:SLOTS, :].rearrange("(p a) (b n) -> p (a b) n", p=P, n=T),
                        grow(const("zeros"), (SLOTS - MAIN) // P * D // T, 1)).then_inc(sem("overflow_zero"), 16)

        def pool_attention(g):
            for u, (h, i) in enumerate(UNITS):
                n = P * (i + 1)
                g.wait_ge(sem("prob_c_scaled"), 3 * u + 2)
                for a in range(2):
                    p = prob[:, u % 2, a * T:a * T + n]
                    g.tensor_scalar(p, p, st[:, 37 + 3 * (u % 2) + a:38 + 3 * (u % 2) + a], None,
                                    ALU.mult).then_inc(sem("prob_scaled"), 1)

        def pool_merge(g):
            for j in range(KD):
                emptied(g, ("mH", j))
                emptied(g, ("mN", j))
                g.tensor_tensor(mT[:, j, :], mP[:, 2 * (j % 2), :], mP[:, 2 * (j % 2) + 1, :],
                                ALU.add).then_inc(sem("merged"), 1)

        def pool_router(g):
            g.wait_ge(sem("slots_clear"), 16)
            g.wait_ge(sem("dest_ready"), 1)
            for i in range(NT):
                for c in range(2):
                    g.indirect_dma_start(slot_dram, bass.IndirectOffsetOnAxis(ap=dest[:, i, c:c + 1], axis=0),
                                         token[:, i:i + 1], None).then_inc(sem("slots_set"), 16)
            g.wait_ge(sem("slots_set"), 16 * 2 * NT)
            g.dma_start(tabi[0:SLOTS // P, :], slot_dram.rearrange("(c p) a -> c (p a)", p=P)).then_inc(sem("slots_in"), 16)

        def pool_experts(g):
            g.wait_ge(sem("xn_stored"), 16)
            g.wait_ge(sem("slots_back"), 1)
            for p in range(NEXP // 2):
                if p:
                    g.wait_ge(full[1], fills_before_moe[1] + p)
                g.indirect_dma_start(gx, None, xn_dram, bass.IndirectOffsetOnAxis(ap=slot_token[:, p:p + 1], axis=0)
                                     ).then_inc(sem("gathered"), 16)
            n = g.value_load(over[0:1, 15:16], min_val=0, max_val=OVB)
            filled(g, "moe_last")
            with g.If(n > 0):
                with g.Fori(0, n) as b:
                    g.wait_ge(sem("ov_free"), b + 1)
                    g.dma_start(over_token[:, :], slot_dram[bass.ds(b * CAP + MAIN, CAP), :]).then_inc(sem("ov_index"), 16)
                    g.wait_ge(sem("ov_index"), b * 16 + 16)
                    g.tensor_tensor(st[:, 92:93], ones[:, 0:1], ones[:, 0:1], ALU.add)
                    g.indirect_dma_start(gx[0:CAP, :], None, xn_dram,
                                         bass.IndirectOffsetOnAxis(ap=over_token[:, 0:1], axis=0)).then_inc(sem("ov_x"), 16)
            g.wait_ge(sem("ov_done"), 1)

        def pool_combine(g):
            for x in range(2):
                g.wait_ge(sem(f"y{x}_stored"), 32 * (NEXP // 2))
            g.wait_ge(sem("overflow_zero"), 16)
            for i in range(NT):
                for c in range(2):
                    g.indirect_dma_start(yg[:, i, c, :], None, y_dram, bass.IndirectOffsetOnAxis(ap=dest[:, i, c:c + 1], axis=0)
                                         ).then_inc(sem("y_gathered"), 16)

        def pool_sb(g):
            for u, (j, hh, i) in enumerate(ZU):
                n = P * (i + 1)
                g.wait_ge(sem("sb_scan"), u + 1)
                g.tensor_tensor(zA[:, u % 2, 0:n], zA[:, u % 2, 0:n], zR[:, u % 2, 1:n + 1], ALU.mult).then_inc(sem("sb_weights"), 1)

        pool_stages = [pool_start, None, pool_attention, None, pool_merge, pool_router, pool_experts, pool_combine, pool_sb]

        @block.gpsimd
        def _(g):
            for stage in pool_stages:
                if stage:
                    stage(g)

        def act_start(a):
            a.dma_start(cst[:, :], A["shape_const"]).then_inc(sem("const_in"), 16)
            pack = [(0, 0, A["c"].rearrange("a (k p) -> (a k) p", p=P)), (0, 8, A["c_2"].rearrange("a (k p) -> (a k) p", p=P)),
                    (0, 16, A["ada_b"].rearrange("a (k p) -> (a k) p", p=P)),
                    (0, 64, A["cmp_pos_k"][0]), (0, 96, A["cmp_pos_v"][0]),
                    (1, 0, A["b_in"][:, 0:GATE_N].rearrange("a (k p) -> (a k) p", p=P)),
                    (1, BMG, A["b_in"][:, MG_H:MG_H + 2 * D].rearrange("a (k p) -> (a k) p", p=P)),
                    (1, ADAB2, A["ada_b_2"].rearrange("a (k p) -> (a k) p", p=P)),
                    (1, HGN, A["hg_norm_w"].rearrange("a (k p) -> (a k) p", p=P)),
                    (1, B1, A["cmp_b1_k"]), (1, B1 + 1, A["cmp_b1_v"]),
                    (2, 0, A["hg_lb_logits"].rearrange("a (k p) -> (a k) p", p=P)),
                    (2, 16, A["norm_g_2"][0].rearrange("a (k p) -> (a k) p", p=P))]
            assert len(pack) == N_PACK
            for b, r, src in pack:
                a.dma_start(packs[r:r + src.shape[0], b, :], src).then_inc(sem("packs_in"), 16)
            a.dma_start(xres[:, :, :], A["x"][0].rearrange("(i p) n -> p i n", p=P)).then_inc(sem("x_in"), 16)
            with nc.allow_non_contiguous_dma(reason="the small bias table, transposed"):
                a.dma_start(tab[0:BUCKETS, :], A["rel_bias"].rearrange("h b -> b h")).then_inc(sem("rel_in"), 16)
            a.dma_start(tab[BUCKETS:BUCKETS + 1, :], A["neg_row"]).then_inc(sem("rel_in"), 16)
            a.dma_start(hot, A["rel_hot"]).then_inc(sem("rel_in"), 16)
            emptied(a, "vec")
            a.activation(csil[:, :], vec[:, 0, 0:16], ACT.Silu).then_inc(sem("silu_c"), 1)
            a.wait_ge(sem("lb_diff"), 1)
            a.activation(colb[:, 0:8], colb[:, 0:8], ACT.Sigmoid).then_inc(sem("lb_sigmoid"), 1)
            for c in range(2):
                t = filled(a, ("rel", c))
                free_bank(("rel", c), a.activation(relrow[:, c * 512:(c + 1) * 512], t[0:HEADS, :], ACT.Copy))
            act_rstd(a, "x_var", "x_sd", 0, 1e-5)
            a.wait_ge(sem("rel_stored"), 16)
            for c in range(4):
                emptied(a, ("ada", 1, c))
            act_modulate(a, "h1", SC1, SH1)

        def act_rstd(a, wait, done, col, eps):
            a.wait_ge(sem(wait), 1)
            a.activation(st[:, col + 4:col + 8], st[:, col:col + 4], ACT.Sqrt).then_inc(sem(done), 1)

        def act_modulate(a, name, sc, sh):
            for k in range(KD):
                t = filled(a, (name, k))
                free_bank((name, k), a.activation(hT[:, k, :], t, ACT.Identity, bias=mod[:, sh, k:k + 1],
                                                  scale=mod[:, sc, k:k + 1]))

        def act_kv(a):
            a.wait_ge(sem("ln_done"), 4)
            for k in range(KD):
                filled(a, ("h1", k))
            def bc(src, n):
                return bass.AP(tensor=src.tensor, offset=src.offset, ap=[[0, P], [1, n]])
            with nc.allow_non_contiguous_dma(reason="24 gate columns"):
                a.dma_start(wgate, cols(A["w_in"], GATE_N, 24)).then_inc(sem("small_in"), 16)
            a.dma_start(gbias, bc(A["b_in"][0, GATE_N:MG_H], 24)).then_inc(sem("small_in"), 16)
            for v in range(2):
                a.dma_start(vbias[:, v, :], bc(A["b_in"][0, KV_N + 768 + 512 * v:KV_N + 1024 + 512 * v], 256)).then_inc(sem("small_in"), 16)
            for v, kv in enumerate("kv"):
                a.dma_start(w2cmp[:, v, :], A[f"cmp_w2_{kv}"][0]).then_inc(sem("small_in"), 16)
            a.dma_start(rows[:, ROW_A, :], bc(A["b_in"][0, I_H:G_H], D)).then_inc(sem("row_a_in"), 16)
            a.dma_start(rows[:, ROW_B, :], bc(A["ln1_b"][0, :], D)).then_inc(sem("row_b_in"), 16)
            a.wait_ge(sem("cbias_done"), 5)
            for c in range(3):
                for j in range(4 if c == 0 else 2):
                    t = filled(a, ("kvT", c, j))
                    dst = kvc[:, j // 2, j % 2, :] if c == 0 else kfull[:, c - 1, j, :]
                    free_bank(("kvT", c, j), a.activation(dst, t, ACT.Identity, bias=bin_col(KV_N + 512 * c + P * j)))
            emptied(a, "gate")
            a.activation(gates, gates, ACT.Sigmoid).then_inc(sem("gate_ready"), 1)
            for v, kv in enumerate("kv"):
                t = filled(a, ("hid", kv))
                a.activation(hsig[:, v, :], t[:, 0:GROUPS * NCMP], ACT.Sigmoid,
                             bias=vec[:, 1, B1 + v:B1 + v + 1]).then_inc(sem("hid_sigmoid"), 1)
            t = filled(a, "kcmp")
            free_bank("kcmp", a.activation(kcmpT, t[:, 0:GROUPS * NCMP], ACT.Copy))

        def act_attention(a):
            def query(h):
                t = filled(a, ("nqT", h))
                free_bank(("nqT", h), a.activation(qT[:, h % 2, :], t, ACT.Identity, scale=SCALE,
                                                   bias=colb[:, 16 + h:17 + h]))

            def exps(u):
                h, i = UNITS[u]
                n = P * (i + 1)
                a.wait_ge(sem("neg_max"), u + 1)
                for b, (o, m) in enumerate(((2 * T, NCMP), (0, n), (T, n))):
                    p = prob[:, u % 2, o:o + m]
                    c = 3 * (u % 2) + b
                    e = a.activation(p, p, ACT.Exp, bias=st[:, 18 + c:19 + c], accum_out=st[:, 24 + c:25 + c])
                e.then_inc(sem("exp_done"), 1)

            query(0)
            exps(0)
            for u, (h, i) in enumerate(UNITS):
                if i == 1 and h + 1 < HEADS:
                    query(h + 1)
                if u + 1 < len(UNITS):
                    exps(u + 1)
                t = filled(a, ("T", 1, u))
                free_bank(("T", 1, u), a.activation(probT[:, u % 2, 4:5 + i, :], t[:, 0:P * (i + 1)], ACT.Copy))
                t = filled(a, ("T", 2, u))
                free_bank(("T", 2, u), a.activation(probT[0:NCMP, u % 2, 8, :], t[0:NCMP, 0:P], ACT.Copy))
                t = filled(a, ("O", u))
                free_bank(("O", u), a.activation(oN[:, h, i * P:(i + 1) * P], t[:, 0:P], ACT.Copy))

        def act_hgrn(a):
            filled(a, ("O", len(UNITS) - 1))
            def inputs(h):
                t = filled(a, ("hq", h))
                free_bank(("hq", h), a.activation(hQ[:, h % 2, :], t, ACT.Identity, bias=bin_col(Q_H + P * h)))
                t = filled(a, ("hf", h))
                free_bank(("hf", h), a.activation(hF[:, h % 2, :], t, ACT.Sigmoid, bias=bin_col(F_H + P * h)))
            def out_gate(h):
                if h >= 2:
                    a.wait_ge(sem("hg_out"), 2 * (h - 1))
                t = filled(a, ("hg", h))
                free_bank(("hg", h), a.activation(hG[:, h % 2, :], t, ACT.Sigmoid, bias=bin_col(G_H + P * h)))

            inputs(0)
            out_gate(0)
            for h in range(HEADS):
                a.wait_ge(sem("hg_f"), h + 1)
                if h:
                    a.wait_ge(sem("hg_out"), 2 * h - 1)
                a.activation(hT2, hF[:, h % 2, :], ACT.Ln).then_inc(sem("hg_logf"), 1)
                a.wait_ge(sem("hg_b"), 2 * h + 1)
                a.activation(hEB, hB, ACT.Exp).then_inc(sem("hg_exp"), 1)
                a.activation(hT2, hB, ACT.Exp, scale=-1.0).then_inc(sem("hg_exp"), 1)
                a.wait_ge(sem("hg_b"), 2 * h + 2)
                a.activation(hKN, hKN, ACT.Exp).then_inc(sem("hg_exp"), 1)
                if h + 1 < HEADS:
                    inputs(h + 1)
                    out_gate(h + 1)
                emptied(a, ("oT", h))
                a.activation(hT2, hO, ACT.Square).then_inc(sem("hg_square"), 1)
                t = filled(a, ("ss", h))
                a.activation(hT2, t, ACT.Ln, scale=1.0 / P, bias=colb[:, 32:33]).then_inc(sem("hg_lnvar"), 1)
                a.wait_ge(sem("hg_lnvar"), h + 1)
                free_bank(("ss", h), a.activation(hT2, hT2, ACT.Exp, scale=-0.5))

        def act_merge(a):
            a.wait_ge(sem("hg_out"), 2 * HEADS)
            for j in range(KD):
                for b, (name, col) in enumerate((("mgh", MG_H), ("mgn", MG_N))):
                    if j >= 2:
                        emptied(a, (("mH", "mN")[b], j - 2))
                    t = filled(a, (name, j))
                    free_bank((name, j), a.activation(mS[:, 2 * (j % 2) + b, :], t, ACT.Sigmoid, bias=bin_col(col + P * j)))

        def bcast_row(src, n):
            return bass.AP(tensor=src.tensor, offset=src.offset, ap=[[0, P], [1, n]])

        def act_router(a):
            emptied(a, ("hi", HEADS - 1))
            a.dma_start(rows[:, ROW_A, :], bcast_row(A["ln1_g"][0, :], D)).then_inc(sem("row_a_in"), 16)
            with nc.allow_non_contiguous_dma(reason="narrow router matrices"):
                a.dma_start(rw[:, :, 0:4], cols(A["router_grp_w"], 0, 4)).then_inc(sem("router_in"), 16)
                a.dma_start(rw[:, :, 4:36], cols(A["router_exp_w"], 0, NEXP)).then_inc(sem("router_in"), 16)
            a.dma_start(rbias[:, 0:4], bcast_row(A["router_grp_b"][0, :], 4)).then_inc(sem("router_in"), 16)
            a.dma_start(rbias[:, 4:36], bcast_row(A["router_exp_b"][0, :], NEXP)).then_inc(sem("router_in"), 16)
            act_rstd(a, "x1_var", "x1_sd", 0, 0)
            act_rstd(a, "xn2_var", "xn2_sd", 0, 0)
            a.wait_ge(sem("xn2_done"), NT)
            a.dma_start(xn_dram.rearrange("(i p) n -> p i n", p=P), xn2).then_inc(sem("xn_stored"), 16)
            a.dma_start(rows[:, ROW_A, :], bcast_row(A["ln2_g"][0, :], D)).then_inc(sem("row_a_in"), 16)
            a.dma_start(rows[:, ROW_B, :], bcast_row(A["ln2_b"][0, :], D)).then_inc(sem("row_b_in"), 16)
            act_modulate(a, "h2", SC2, SH2)
            a.wait_ge(sem("group_logits"), 1)
            a.activation(gexp, gexp, ACT.Exp).then_inc(sem("group_exp"), 1)
            a.wait_ge(sem("second_logit"), 1)
            a.activation(emax2, emax2, ACT.Exp).then_inc(sem("second_exp"), 1)

        def act_experts(a):
            base = fills_before_moe

            def tokens(p):
                for b in range(2):
                    a.wait_ge(full[b], p + (base[b] + 1))
                    for k in range(4 * b, 4 * b + 4):
                        e = a.activation(xT[:, k, :], ps[:, b, (k % 4) * P:(k % 4 + 1) * P], ACT.Identity,
                                         bias=mod[:, SH2, k:k + 1], scale=mod[:, SC2, k:k + 1])
                    e.then_inc(empty[b], 1)

            def gate(p, x):
                a.wait_ge(full[2 + x], p + (base[2 + x] + 1))
                a.activation(sg[0:CAP, x, :], ps[0:CAP, 2 + x, :], ACT.Silu).then_inc(sem("moe_silu"), 1)

            def store(p, x, first=False):
                a.wait_ge(full[6 + x], p + (base[6 + x] + 1))
                if not first:
                    a.wait_ge(sem(f"y{x}_stored"), p * 32)
                a.activation(ysb[:, x, :], ps[:, 6 + x, :], ACT.Copy).then_inc(empty[6 + x], 1)
                a.wait_ge(empty[6 + x], p + (base[6 + x] + 1))
                for m in range(2):
                    a.dma_start(y_dram[bass.ds(p * (2 * CAP) + x * CAP, CAP), m * 512:(m + 1) * 512],
                                ysb[m * CAP:(m + 1) * CAP, x, :]).then_inc(sem(f"y{x}_stored"), 16)

            tokens(0)

            def pair(p, first=False, last=False):
                gate(p, 0)
                store(p, 0, first)
                gate(p, 1)
                if not last:
                    tokens(p + 1)
                store(p, 1, first)

            pair(0, first=True)
            with a.Fori(1, NEXP // 2 - 1) as p:
                pair(p)
            pair(NEXP // 2 - 1, last=True)
            for x in range(2):
                a.wait_ge(sem(f"y{x}_stored"), 32 * (NEXP // 2))
            a.wait_ge(sem("over_known"), 1)
            n = a.value_load(over[0:1, 15:16], min_val=0, max_val=OVB)
            a.wait_ge(sem("overflow_zero"), 16)
            a.activation(st[:, 90:91], st[:, 8:9], ACT.Copy).then_inc(sem("ov_free"), 1)
            with a.If(n > 0):
                with a.Fori(0, n) as b:
                    a.wait_ge(sem("ov_gt"), b + 1)
                    for k in range(KD):
                        e = a.activation(xT[:, k, 0:CAP], ps[:, 0, k * CAP:(k + 1) * CAP], ACT.Identity,
                                         bias=mod[:, SH2, k:k + 1], scale=mod[:, SC2, k:k + 1])
                    e.then_inc(sem("ov_xt"), 1)
                    a.wait_ge(sem("ov_h"), b + 1)
                    a.activation(sg[0:CAP, 0, :], ps[0:CAP, 2, :], ACT.Silu).then_inc(sem("ov_s"), 1)
                    a.wait_ge(sem("ov_y"), b + 1)
                    a.activation(ysb[:, 0, :], ps[:, 6, :], ACT.Copy).then_inc(sem("ov_ys"), 1)
                    a.wait_ge(sem("ov_ys"), b + 1)
                    for m in range(2):
                        a.dma_start(y_dram[bass.ds(b * CAP + MAIN, CAP), m * 512:(m + 1) * 512],
                                    ysb[m * CAP:(m + 1) * CAP, 0, :]).then_inc(sem("ov_stored"), 16)
                    a.wait_ge(sem("ov_stored"), b * 32 + 32)
                    a.activation(st[:, 90:91], st[:, 8:9], ACT.Copy).then_inc(sem("ov_free"), 1)
            a.activation(st[:, 91:92], st[:, 8:9], ACT.Copy).then_inc(sem("ov_done"), 1)

        def act_combine(a):
            act_rstd(a, "x2_var", "x2_sd", 0, 0)

        def act_rms(a, src, ready, name, dump):
            for i in range(NT):
                a.wait_ge(sem(ready), i + 1)
                e = a.activation(dump[:, i, :], src[:, i, :], ACT.Square, accum_out=st[:, 80 + i:81 + i])
            e.then_inc(sem(name + "_ss"), 1)
            a.wait_ge(sem(name + "_ss"), 1)
            a.activation(st[:, 84:88], st[:, 80:84], ACT.Sqrt, scale=1.0 / D, bias=colb[:, 32:33]).then_inc(sem(name + "_rms"), 1)

        def act_sb(a):
            unused = brn[:, 1, :].rearrange("p (i n) -> p i n", i=NT)
            act_rms(a, xres, "x2_ready", "x2n", unused)
            act_modulate(a, "h3", SCM, SHM)

            def inputs(j):
                t = filled(a, ("sq", j))
                free_bank(("sq", j), a.activation(zq[:, j % 2, :], t, ACT.Copy, scale=SB_SCALE))

            def sigmoids(u):
                j, hh, i = ZU[u]
                n = P * (i + 1)
                a.wait_ge(sem("sb_masked"), u + 1)
                if u >= 2:
                    filled(a, ("zT", u - 2))
                t = ps[:, u % 2, 0:n]
                a.activation(zU[:, u % 2, 0:n], t, ACT.Sigmoid, scale=-1.0)
                free_bank(("z", u), a.activation(zA[:, u % 2, 0:n], t, ACT.Sigmoid))

            inputs(0)
            sigmoids(0)
            for u, (j, hh, i) in enumerate(ZU):
                if hh == 0 and i == 2 and j + 1 < KD:
                    inputs(j + 1)
                if u + 1 < len(ZU):
                    sigmoids(u + 1)
                t = filled(a, ("zT", u))
                free_bank(("zT", u), a.activation(zT[:, u % 2, 0:P * (i + 1)], t[:, 0:P * (i + 1)], ACT.Copy))
                t = filled(a, ("zO", u))
                r = slice(64 * hh, 64 * hh + 64)
                free_bank(("zO", u), a.activation(sT[r, j, i * P:(i + 1) * P], t[r, 0:P], ACT.Copy))
            act_rms(a, yb, "y1_ready", "y1", hT4)
            act_rms(a, xres, "x3_ready", "x3n", unused)

        def act_ffn(a):
            act_modulate(a, "h4", SCF, SHF)
            for f in range(FT):
                if f >= 4:
                    emptied(a, ("fgu", 1, f - 4))
                t = filled(a, ("fgu", 0, f))
                free_bank(("fgu", 0, f), a.activation(fS[:, f % 4, :], t, ACT.Silu))
            act_rms(a, hT4, "y2_ready", "y2", brn[:, 1, :].rearrange("p (i n) -> p i n", i=NT))

        hT4 = hT[:, :, :].rearrange("p k t -> p (k t)").rearrange("p (i n) -> p i n", i=NT)

        act_stages = [act_start, act_kv, act_attention, act_hgrn, act_merge, act_router, act_experts, act_combine, act_sb, act_ffn]

        @block.scalar
        def _(a):
            for stage in act_stages:
                stage(a)

        dve_steps = [0]

        def step(v, instruction):
            dve_steps[0] += 1
            instruction.then_inc(sem("dve_step"), 1)
            v.wait_ge(sem("dve_step"), dve_steps[0])

        def dve_stats(v, src, nt=NT, eps=1e-5):
            for i in range(nt):
                for c in range(2):
                    w = v.bn_stats(bnb[:, i, c, :], src[:, i, c * 512:(c + 1) * 512])
            step(v, w)
            for i in range(nt):
                w = v.bn_aggr(mv[:, i, :], bnb[:, i, :, :])
            step(v, w)
            v.tensor_copy(st[:, 8:8 + nt], mv[:, 0:nt, 0])
            return v.tensor_scalar(st[:, 0:nt], mv[:, 0:nt, 1], eps, None, ALU.add)

        def dve_ada(v, m, c):
            name = ("ada", m, c)
            t = filled(v, name)
            b = vec[:, 0, ADAB1 + 4 * c:ADAB1 + 4 * c + 4] if m == 1 else vec[:, 1, ADAB2 + 4 * c:ADAB2 + 4 * c + 4]
            one = 0.0 if c // 2 in (0, 3) or (m, c // 2) in ((2, 2), (2, 5)) else 1.0
            dst = mod[:, 6 * (m - 1) + c // 2, 4 * (c % 2):4 * (c % 2) + 4]
            free_bank(name, v.scalar_tensor_tensor(dst, t[:, 0:4], one, b, ALU.add, ALU.add))

        def dve_start(v):
            t = filled(v, "vec")
            flat = vec[:, :, :].rearrange("p a n -> p (a n)")
            v.tensor_copy(flat[:, 0:P + 126], t[:, 0:P + 126])
            free_bank("vec", v.tensor_copy(flat[:, 2 * P:2 * P + 48], t[:, 2 * P:2 * P + 48]))
            emptied(v, "vec")
            v.tensor_tensor(colb[:, 0:8], vec[:, 2, 0:8], vec[:, 2, 8:16], ALU.subtract).then_inc(sem("lb_diff"), 1)
            v.memset(colb[:, 32:33], 1e-6)
            v.tensor_scalar(colb[:, 16:24], vec[:, 1, Q_N // P:Q_N // P + 8], SCALE, None, ALU.mult)
            v.wait_ge(sem("lb_sigmoid"), 1)
            step(v, v.tensor_scalar(colb[:, 8:16], colb[:, 0:8], -1.0, 1.0, ALU.mult, ALU.add))
            v.wait_ge(sem("x_in"), 16)
            dve_stats(v, xres).then_inc(sem("x_var"), 1)
            v.wait_ge(sem("x_sd"), 1)
            step(v, v.reciprocal(st[:, 4:8], st[:, 4:8]))
            for i in range(NT):
                v.tensor_scalar(xn[:, i, :], xres[:, i, :], st[:, 8 + i:9 + i], st[:, 4 + i:5 + i], ALU.subtract,
                                ALU.mult).then_inc(sem("ln_done"), 1)
            for c in range(4):
                dve_ada(v, 1, c)

        def dve_kv(v):
            v.wait_ge(sem("bias_in"), 32)
            for i in range(NT):
                a = 384 + CMP - 1 - P * i
                v.tensor_copy(cbias[:, :, i, :], longb[:, :, a:a + STRIDE * (NCMP - 1) + 1:STRIDE]).then_inc(sem("cbias_done"), 1)
            v.wait_ge(sem("cbias_done"), 4)
            v.tensor_scalar(cmask, cbias[:, 0, :, :], NEG / 10, None, ALU.is_gt).then_inc(sem("cbias_done"), 1)

            def cmp_blocks(a):
                for g in range(GROUPS):
                    emptied(v, ("kvT", 0, 2 * a + g))
                if a:
                    filled(v, ("hid", "k"))
                for g in range(GROUPS):
                    for half in range(2):
                        src = kvc[:, a, g, :].rearrange("p (n t) -> p t n", t=STRIDE)[:, :, half:half + NCMP]
                        pos = vec[:, 0, (POSK, POSV)[a] + STRIDE * half:(POSK, POSV)[a] + STRIDE * (half + 1)]
                        v.tensor_tensor(blocks[:, STRIDE * half:STRIDE * (half + 1), g, :], src, grow(pos, NCMP),
                                        ALU.add).then_inc(sem("blocks_ready"), 1)

            def hid_silu(a, kv):
                v.wait_ge(sem("hid_sigmoid"), a + 1)
                t = filled(v, ("hid", kv))
                free_bank(("hid", kv), v.scalar_tensor_tensor(hid[:, a, :], t[:, 0:GROUPS * NCMP],
                                                              vec[:, 1, B1 + a:B1 + a + 1], hsig[:, a, :], ALU.add, ALU.mult))

            cmp_blocks(0)
            v.wait_ge(sem("small_in"), 16 * N_SMALL)
            for c in (1, 2):
                for i2 in range(2):
                    t = filled(v, ("vtok", c, i2))
                    free_bank(("vtok", c, i2), v.tensor_tensor(
                        vfull[:, c - 1, 2 * i2:2 * i2 + 2, :], t.rearrange("p (i n) -> p i n", i=2),
                        grow(vbias[:, c - 1, :], 2, 1), ALU.add))
            t = filled(v, "gate")
            free_bank("gate", v.tensor_tensor(gates, t[:, 0:96].rearrange("p (i n) -> p i n", i=NT), grow(gbias, NT, 1), ALU.add))
            cmp_blocks(1)
            hid_silu(0, "k")
            hid_silu(1, "v")
            t = filled(v, "vcmp")
            free_bank("vcmp", v.tensor_copy(vcmp[0:NCMP, :, :], t[0:NCMP, 0:GROUPS * P].rearrange("p (g n) -> p g n", g=GROUPS)))

        def dve_attention(v):
            def bias_and_max(u):
                h, i = UNITS[u]
                n = P * (i + 1)
                if u >= 2:
                    filled(v, ("T", 2, u - 2))
                c = 3 * (u % 2)
                for b, (a, o, m, bias) in enumerate(((2, 2 * T, NCMP, cbias[:, h, i, :]),
                                                     (0, 0, n, biasT[:, h, T - n:T]), (1, T, n, biasT[:, h, T - n:T]))):
                    t = filled(v, ("S", a, u))
                    free_bank(("S", a, u), v.tensor_tensor_reduce(
                        out=prob[:, u % 2, o:o + m], in0=t[:, 0:m], in1=bias, scale=1.0, scalar=-3e38,
                        op0=ALU.add, op1=ALU.max, accum_out=st[:, 12 + c + b:13 + c + b]))
                for a in range(3):
                    emptied(v, ("S", a, u))
                v.tensor_scalar(st[:, 18 + c:21 + c], st[:, 12 + c:15 + c], -1.0, None, ALU.mult).then_inc(sem("neg_max"), 1)

            v.wait_ge(sem("gate_ready"), 1)
            bias_and_max(0)
            for u, (h, i) in enumerate(UNITS):
                if u + 1 < len(UNITS):
                    bias_and_max(u + 1)
                if i == 2:
                    dve_ada(v, *ada_at[("attn", h)])
                c = 3 * (u % 2)
                v.wait_ge(sem("exp_done"), u + 1)
                v.reciprocal(st[:, 30 + c:33 + c], st[:, 24 + c:27 + c]).then_inc(sem("prob_c_scaled"), 1)
                v.wait_ge(sem("prob_c_scaled"), 3 * u + 1)
                v.tensor_tensor(st[:, 36 + c:39 + c], st[:, 30 + c:33 + c], gates[:, i, 3 * h:3 * h + 3],
                                ALU.mult).then_inc(sem("prob_c_scaled"), 1)
                v.wait_ge(sem("prob_c_scaled"), 3 * u + 2)
                p = prob[:, u % 2, 2 * T:2 * T + NCMP]
                v.scalar_tensor_tensor(p, p, st[:, 36 + c:37 + c], cmask[:, i, :], ALU.mult,
                                       ALU.mult).then_inc(sem("prob_c_scaled"), 1)
                t = filled(v, ("T", 0, u))
                free_bank(("T", 0, u), v.tensor_copy(probT[:, u % 2, 0:i + 1, :].rearrange("p a n -> p (a n)"), t[:, 0:P * (i + 1)]))

        def dve_hgrn(v):
            filled(v, ("O", len(UNITS) - 1))
            attmask = const("attmask").bitcast(u32)
            v.memset(hAT, 0.0)
            v.wait_ge(sem("row_a_in"), 16)

            def values(h):
                t = filled(v, ("hi", h))
                free_bank(("hi", h), v.tensor_tensor(hV[:, h % 2, :, :], t.rearrange("p (i n) -> p i n", i=NT),
                                                     grow(rows[:, ROW_A, P * h:P * (h + 1)], NT, 1), ALU.add))

            for h in range(HEADS):
                f = hF[:, h % 2, :]
                emptied(v, ("hf", h))
                v.tensor_scalar(f, f, colb[:, 8 + h:9 + h], colb[:, h:h + 1], ALU.mult, ALU.add).then_inc(sem("hg_f"), 1)
                v.wait_ge(sem("hg_f"), h + 1)
                v.tensor_scalar(hK, f, -1.0, 1.0, ALU.mult, ALU.add)
                v.wait_ge(sem("hg_logf"), h + 1)
                v.tensor_tensor_scan(hB, const("reset"), hT2, 0.0, ALU.mult, ALU.add).then_inc(sem("hg_b"), 1)
                v.wait_ge(sem("hg_b"), 2 * h + 1)
                if h:
                    filled(v, ("kendT", h - 1))
                b3 = hB.rearrange("p (n c) -> p n c", c=CHUNK)
                v.tensor_tensor(hKN.rearrange("p (n c) -> p n c", c=CHUNK), b3[:, :, CHUNK - 1:CHUNK].to_broadcast([P, NCHUNK, CHUNK]),
                                b3, ALU.subtract).then_inc(sem("hg_b"), 1)
                emptied(v, ("hq", h))
                v.wait_ge(sem("hg_exp"), 3 * h + 1)
                v.tensor_tensor(hQ[:, h % 2, :], hQ[:, h % 2, :], hEB, ALU.mult)
                v.wait_ge(sem("hg_exp"), 3 * h + 2)
                if h:
                    filled(v, ("att", h - 1))
                v.tensor_tensor(hKI, hK, hT2, ALU.mult)
                v.wait_ge(sem("hg_exp"), 3 * h + 3)
                v.tensor_tensor(hKN, hKN, hK, ALU.mult).then_inc(sem("hg_kend"), 1)
                if h == 0:
                    values(0)

                def chunk_blocks(i):
                    t = filled(v, ("kendT", h))
                    if i >= 2:
                        filled(v, ("U", h, i - 2))
                    elif h:
                        filled(v, ("U", h - 1, i + 2))
                    w = v.tensor_tensor(hKX[:, i % 2, :, :], grow(t[:, i * P:(i + 1) * P], CPT, 1),
                                        grow(const("chunk"), P), ALU.mult)
                    if i < NT - 1:
                        w.then_inc(sem("hg_kblocks"), 1)
                    else:
                        free_bank(("kendT", h), w)

                chunk_blocks(0)
                chunk_blocks(1)
                t = filled(v, ("att", h))
                if h:
                    filled(v, ("oT", h - 1))
                free_bank(("att", h), v.copy_predicated(hAT.rearrange("p (i n) -> p i n", i=NT), grow(attmask, NT, 1),
                                                        t.rearrange("p (i n) -> p i n", i=NT)))
                if h + 1 < HEADS:
                    values(h + 1)
                for i in range(NT):
                    t = filled(v, ("U", h, i))
                    for c in range(CPT):
                        n = CPT * i + c
                        if n == NCHUNK - 1:
                            continue
                        u = t[:, c * P:(c + 1) * P]
                        if n == 0:
                            w = v.tensor_copy(hS[:, 1, :], u)
                        else:
                            state_ready(v, h, n)
                            w = v.scalar_tensor_tensor(hS[:, n + 1, :], hS[:, n, :], hEB[:, CHUNK * (n + 1) - 1:CHUNK * (n + 1)],
                                                       u, ALU.mult, ALU.add)
                        if c == CPT - 1 or n == NCHUNK - 2:
                            free_bank(("U", h, i), w)
                        else:
                            w.then_inc(sem("hg_state"), 1)
                    if i + 2 < NT:
                        chunk_blocks(i + 2)
                t = filled(v, ("oT", h))
                free_bank(("oT", h), v.tensor_copy(hO, t))
                dve_ada(v, *ada_at[("hg", h)])
                emptied(v, ("ss", h))
                v.tensor_tensor(hO, hO, hT2, ALU.mult).then_inc(sem("hg_out"), 1)
                v.wait_ge(sem("hg_out"), 2 * h + 1)
                v.scalar_tensor_tensor(oH[:, h, :], hO, vec[:, 1, HGN + h:HGN + h + 1], hG[:, h % 2, :], ALU.mult,
                                       ALU.mult).then_inc(sem("hg_out"), 1)

        def dve_merge(v):
            v.wait_ge(sem("hg_out"), 2 * HEADS)
            for j in range(KD):
                if j == 4:
                    for which, gain in ((GM, 1), (GF, 3), (SCM, 0), (SCF, 2)):
                        step(v, v.tensor_tensor(mod[:, which, :], mod[:, which, :], vec[:, 2, 16 + 8 * gain:24 + 8 * gain], ALU.mult))
                if j >= 4:
                    for x in (2 * j - 8, 2 * j - 7):
                        if x >= 2:
                            filled(v, ("row", x - 2))
                        g = mod[:, (G1, G2, GM, GF)[x // 2], 4 * (x % 2):4 * (x % 2) + 4]
                        v.tensor_tensor(mD[:, x % 2, :].rearrange("p (a n) -> p a n", a=4), grow(ident, 4, 1), grow(g, P),
                                        ALU.mult).then_inc(sem("gate_diag"), 1)
                    for x in (2 * j - 8, 2 * j - 7):
                        t = filled(v, ("row", x))
                        free_bank(("row", x), v.tensor_copy(rows[:, x // 2, (x % 2) * 512:(x % 2 + 1) * 512], t))
                for b, m in ((1, "mN"), (0, "mH")):
                    t = filled(v, (m, j))
                    emptied(v, (("mgh", "mgn")[b], j))
                    if j >= 2:
                        v.wait_ge(sem("merged"), j - 1)
                    free_bank((m, j), v.tensor_tensor(mP[:, 2 * (j % 2) + b, :], t, mS[:, 2 * (j % 2) + b, :], ALU.mult))
                if j < 4:
                    dve_ada(v, *ada_at[("merge", j)])
                    if j == 3:
                        emptied(v, ("ada", 2, 11))
            for i in range(NT):
                for c in range(2):
                    t = filled(v, ("wout", c, i))
                    half = slice(512 * c, 512 * (c + 1))
                    tmp = mP[:, 2 * (i % 2) + c, :]
                    if i == 0:
                        v.wait_ge(sem("merged"), KD)
                    free_bank(("wout", c, i), v.tensor_tensor(tmp, t, rows[:, ROW_G1, half], ALU.mult))
                    emptied(v, ("wout", c, i))
                    w = v.scalar_tensor_tensor(xres[:, i, half], xres[:, i, half], ALPHA, tmp, ALU.mult, ALU.add)
            step(v, w)

        def dve_layer_norm(v, src, dst, name, done=None):
            dve_stats(v, src).then_inc(sem(name + "_var"), 1)
            v.wait_ge(sem(name + "_sd"), 1)
            step(v, v.reciprocal(st[:, 4:8], st[:, 4:8]))
            for i in range(NT):
                w = v.tensor_scalar(dst[:, i, :], src[:, i, :], st[:, 8 + i:9 + i], st[:, 4 + i:5 + i], ALU.subtract, ALU.mult)
                if done:
                    w.then_inc(sem(done), 1)
            if not done:
                step(v, w)

        def dve_affine(v, done=None):
            for i in range(NT):
                v.wait_ge(sem("row_a_in"), ROW_LOADS[0])
                step(v, v.tensor_tensor(xres[:, i, :], xres[:, i, :], rows[:, ROW_A, :], ALU.mult))
                v.wait_ge(sem("row_b_in"), ROW_LOADS[1])
                w = v.tensor_tensor(xres[:, i, :], xres[:, i, :], rows[:, ROW_B, :], ALU.add)
                if done:
                    w.then_inc(sem(done), 1)
            if not done:
                step(v, w)

        ROW_LOADS = [32, 16]

        def dve_router(v):
            dve_layer_norm(v, xres, xres, "x1")
            dve_affine(v)
            dve_layer_norm(v, xres, xn2, "xn2", "xn2_done")
            step(v, v.tensor_copy(token[:, :], const("token")))
            step(v, v.memset(g8, NEG))
            v.wait_ge(sem("router_in"), 64)
            t = filled(v, "logits")
            free_bank("logits", v.tensor_tensor(lg, t[:, 0:NT * 36].rearrange("p (i n) -> p i n", i=NT), grow(rbias, NT, 1), ALU.add))
            emptied(v, "logits")
            step(v, v.tensor_copy(g8[:, :, 0:EXP_GROUPS], lg[:, :, 0:EXP_GROUPS]))
            for i in range(NT):
                w = v.max(gtop[:, i, :], g8[:, i, :])
            step(v, w)
            for i in range(NT):
                w = v.max_index(gat[:, i, :], gtop[:, i, :], g8[:, i, :])
            step(v, w)
            v.tensor_tensor(gexp, lg[:, :, 0:EXP_GROUPS], gtop[:, :, 0:1].to_broadcast([P, NT, EXP_GROUPS]),
                            ALU.subtract).then_inc(sem("group_logits"), 1)
            step(v, v.tensor_copy(idxf[:, :, 0:1], gat[:, :, 0:1]))
            step(v, v.tensor_tensor(gone, grow(const("iota")[:, 0:EXP_GROUPS], NT, 1),
                                    idxf[:, :, 0:1].to_broadcast([P, NT, EXP_GROUPS]), ALU.is_equal))
            m4 = masked.rearrange("p i (g e) -> p (i g) e", g=EXP_GROUPS)
            t4 = tmp32.rearrange("p i (g e) -> p (i g) e", g=EXP_GROUPS)
            gf = gone.rearrange("p i g -> p (i g)")
            step(v, v.tensor_scalar(t4, grow(gf, EPG), -NEG, NEG, ALU.mult, ALU.add))
            step(v, v.tensor_copy(masked, lg[:, :, EXP_GROUPS:36]))
            step(v, v.tensor_tensor(m4, m4, grow(gf, EPG), ALU.mult))
            step(v, v.tensor_tensor(masked, masked, tmp32, ALU.add))
            for i in range(NT):
                w = v.max(etop[:, i, :], masked[:, i, :])
            step(v, w)
            for i in range(NT):
                w = v.max_index(eat[:, i, :], etop[:, i, :], masked[:, i, :])
            step(v, w)
            v.tensor_tensor(emax2.unsqueeze(2), etop[:, :, 1:2], etop[:, :, 0:1], ALU.subtract).then_inc(sem("second_logit"), 1)
            step(v, v.tensor_copy(idxf[:, :, 1:3], eat[:, :, 0:2]))
            iota = grow(const("iota"), NT, 1)
            v.tensor_tensor(hot0, iota, idxf[:, :, 1:2].to_broadcast([P, NT, NEXP]), ALU.is_equal)
            step(v, v.tensor_tensor(hot1, iota, idxf[:, :, 2:3].to_broadcast([P, NT, NEXP]), ALU.is_equal))
            v.tensor_tensor(both, hot0, hot1, ALU.add).then_inc(sem("chosen"), 1)
            v.wait_ge(sem("group_exp"), 1)
            step(v, v.tensor_reduce(gsum, gexp, AX.X, ALU.add))
            v.wait_ge(sem("second_exp"), 1)
            step(v, v.tensor_scalar(st[:, 60:64], emax2, 1.0, None, ALU.add))
            step(v, v.tensor_tensor(st[:, 60:64], st[:, 60:64], gsum, ALU.mult))
            step(v, v.reciprocal(comb[:, :, 0], st[:, 60:64]))
            step(v, v.tensor_tensor(comb[:, :, 1], comb[:, :, 0], emax2, ALU.mult))
            t = filled(v, "rank")
            v.tensor_copy(rank, t[:, 0:NT * NEXP].rearrange("p (i n) -> p i n", i=NT))
            free_bank("rank", v.tensor_copy(counts, t[:, NT * NEXP:(NT + 1) * NEXP]))
            emptied(v, "rank")
            step(v, v.tensor_tensor(cmp7, grow(counts, 7), grow(const("full"), NEXP, 1), ALU.is_gt))
            step(v, v.tensor_reduce(blocks_of, cmp7, AX.X, ALU.add))
            step(v, v.tensor_tensor_scan(block_end, ones[:, 0:NEXP], blocks_of, 0.0, ALU.mult, ALU.add))
            step(v, v.tensor_tensor(tmp1, block_end, blocks_of, ALU.subtract))
            step(v, v.tensor_scalar(over0, tmp1, float(CAP), float(MAIN - CAP), ALU.mult, ALU.add))
            step(v, v.tensor_tensor(over0, over0, const("slot0"), ALU.subtract))
            step(v, v.tensor_scalar(place, rank, float(CAP), None, ALU.is_ge))
            step(v, v.tensor_tensor(place, place, grow(over0, NT, 1), ALU.mult))
            step(v, v.tensor_tensor(place, place, rank, ALU.add))
            step(v, v.tensor_tensor(place, place, grow(const("slot0"), NT, 1), ALU.add))
            v.tensor_tensor(hot0, hot0, place, ALU.mult)
            step(v, v.tensor_tensor(hot1, hot1, place, ALU.mult))
            v.tensor_reduce(slotf[:, :, 0], hot0, AX.X, ALU.add)
            step(v, v.tensor_reduce(slotf[:, :, 1], hot1, AX.X, ALU.add))
            v.tensor_copy(dest[:, :, :], slotf).then_inc(sem("dest_ready"), 1)
            step(v, v.tensor_tensor(cmp16, grow(block_end, 15, 1), grow(const("block")[:, 0:15], NEXP), ALU.is_le))
            step(v, v.tensor_reduce(overf[:, 0:15], cmp16, AX.X, ALU.add))
            step(v, v.tensor_scalar(overf[:, 0:15], overf[:, 0:15], float(NEXP - 1), None, ALU.min))
            step(v, v.tensor_copy(overf[:, 15:16], block_end[:, NEXP - 1:NEXP]))
            v.tensor_copy(over[:, :], overf).then_inc(sem("over_known"), 1)
            v.wait_ge(sem("slots_in"), 16)
            v.tensor_copy(tabf[0:SLOTS // P, :], tabi[0:SLOTS // P, :]).then_inc(sem("slots_float"), 1)
            t = filled(v, "slots")
            free_bank("slots", v.tensor_copy(slot_token[:, :], t[:, 0:SLOTS // P]))
            emptied(v, "slots")
            v.memset(st[:, 89:90], 0.0).then_inc(sem("slots_back"), 1)

        def dve_experts(v):
            base = fills_before_moe

            def gated(p, x, n):
                v.wait_ge(sem("moe_silu"), p * 2 + (x + 1))
                v.wait_ge(full[2 + x], p + (base[2 + x] + 1))
                v.tensor_tensor(hx[0:CAP, x, :], sg[0:CAP, x, :], ps[CAP:2 * CAP, 2 + x, :], ALU.mult).then_inc(empty[2 + x], 1)
                v.wait_ge(full[4 + x], p + (base[4 + x] + 1))
                v.tensor_copy(aT[:, x, :, :].rearrange("p k n -> p (k n)"), ps[:, 4 + x, 0:4 * CAP]).then_inc(empty[4 + x], 1)

            with v.Fori(0, NEXP // 2) as p:
                gated(p, 0, None)
                gated(p, 1, None)
            n = v.value_load(over[0:1, 15:16], min_val=0, max_val=OVB)
            with v.If(n > 0):
                with v.Fori(0, n) as b:
                    v.wait_ge(sem("ov_s"), b + 1)
                    v.tensor_tensor(hx[0:CAP, 0, :], sg[0:CAP, 0, :], ps[CAP:2 * CAP, 2, :], ALU.mult).then_inc(sem("ov_a"), 1)
                    v.wait_ge(sem("ov_at"), b + 1)
                    v.tensor_copy(aT[:, 0, :, :].rearrange("p k n -> p (k n)"), ps[:, 4, 0:4 * CAP]).then_inc(sem("ov_ate"), 1)
            v.wait_ge(sem("ov_done"), 1)

        def dve_combine(v):
            v.wait_ge(sem("y_gathered"), 16 * 2 * NT)
            for i in range(NT):
                y = yg[:, i, 0, :]
                step(v, v.tensor_scalar(y, y, comb[:, i, 0:1], None, ALU.mult))
                step(v, v.scalar_tensor_tensor(y, yg[:, i, 1, :], comb[:, i, 1:2], y, ALU.mult, ALU.add))
                step(v, v.tensor_tensor(y, y, rows[:, ROW_G2, :], ALU.mult))
                w = v.scalar_tensor_tensor(xres[:, i, :], xres[:, i, :], ALPHA, y, ALU.mult, ALU.add)
            step(v, w)
            dve_layer_norm(v, xres, xres, "x2")
            ROW_LOADS[:] = [48, 32]
            dve_affine(v, "x2_ready")

        def dve_rms(v, name, dst, done):
            v.wait_ge(sem(name + "_rms"), 1)
            step(v, v.reciprocal(st[:, 84:88], st[:, 84:88]))
            for i in range(NT):
                v.tensor_scalar(dst[:, i, :], xres[:, i, :], st[:, 84 + i:85 + i], None, ALU.mult).then_inc(sem(done), 1)

        def dve_residual(v, kind, y, row, name, done):
            for i in range(NT):
                for c in range(2):
                    t = filled(v, (kind, c, i))
                    free_bank((kind, c, i), v.tensor_copy(y[:, i, c * 512:(c + 1) * 512], t))
                for c in range(2):
                    emptied(v, (kind, c, i))
                v.memset(st[:, 88:89], 0.0).then_inc(sem(name + "_ready"), 1)
            v.wait_ge(sem(name + "_rms"), 1)
            step(v, v.reciprocal(st[:, 84:88], st[:, 84:88]))
            for i in range(NT):
                step(v, v.scalar_tensor_tensor(y[:, i, :], y[:, i, :], st[:, 84 + i:85 + i], rows[:, row, :], ALU.mult, ALU.mult))
                v.tensor_tensor(xres[:, i, :], xres[:, i, :], y[:, i, :], ALU.add).then_inc(sem(done), 1)

        def dve_sb(v):
            dve_rms(v, "x2n", xn3, "xn3_done")

            def keys(j):
                t = filled(v, ("sk", j))
                free_bank(("sk", j), v.tensor_copy(zk[:, j % 2, :], t))
                t = filled(v, ("sv", j))
                free_bank(("sv", j), v.tensor_copy(zv[:, j % 2, :, :].rearrange("p i n -> p (i n)"), t))

            def mask(u):
                i = ZU[u][2]
                t = filled(v, ("z", u))
                t = t[:, i * P:(i + 1) * P]
                v.tensor_tensor(t, t, const("sbmask"), ALU.add).then_inc(sem("sb_masked"), 1)

            for n in range(1, NT + 1):
                for a in range(2):
                    w = v.memset(zR[:, a, n * P:n * P + 1], 1.0)
            step(v, w)
            keys(0)
            mask(0)
            for u, (j, hh, i) in enumerate(ZU):
                if hh == 0 and i == 2 and j + 1 < KD:
                    keys(j + 1)
                if u + 1 < len(ZU):
                    mask(u + 1)
                n = P * (i + 1)
                emptied(v, ("z", u))
                if u >= 2:
                    v.wait_ge(sem("sb_weights"), u - 1)
                step(v, v.memset(zR[:, u % 2, n:n + 1], 1.0))
                v.tensor_tensor_scan(zR[:, u % 2, 0:n][:, ::-1], zU[:, u % 2, 0:n][:, ::-1], const("zeros")[:, 0:n], 1.0,
                                     ALU.mult, ALU.add).then_inc(sem("sb_scan"), 1)
            dve_residual(v, "wo", yb, ROW_GM, "y1", "x3_ready")

        def dve_ffn(v):
            dve_rms(v, "x3n", xn3, "xn4_done")
            for f in range(FT):
                emptied(v, ("fgu", 0, f))
                t = filled(v, ("fgu", 1, f))
                free_bank(("fgu", 1, f), v.tensor_tensor(ff[:, f, :], fS[:, f % 4, :], t, ALU.mult))
            dve_residual(v, "fo", hT4, ROW_GF, "y2", "out_ready")

        dve_stages = [dve_start, dve_kv, dve_attention, dve_hgrn, dve_merge, dve_router, dve_experts, dve_combine, dve_sb, dve_ffn]

        @block.vector
        def _(v):
            for stage in dve_stages:
                stage(v)


_OUT = (1, T, D)


def kernel(**inputs):
    import concourse.bacc as bacc
    from concourse.bass_utils import run_bass_kernel_spmd

    nc = bacc.Bacc("TRN2", target_bir_lowering=False, num_devices=1)
    arrays, io = {}, {}
    given = {k: v for k, v in inputs.items() if v.size and not k.startswith(("sg_", "sc_", "cb_"))}
    for name, a in {**given, **shape_constants()}.items():
        a = np.ascontiguousarray(a)
        arrays[f"in_{name}"] = a
        io[name] = nc.dram_tensor(f"in_{name}", a.shape, mybir.dt.from_np(a.dtype), kind="ExternalInput").ap()
    out = nc.dram_tensor("out", _OUT, mybir.dt.float32, kind="ExternalOutput").ap()
    block_kernel(nc, io, out)
    return run_bass_kernel_spmd(nc, [arrays], core_ids=[0]).results[0]["out"]
```

```python
import math
from contextlib import ExitStack

import numpy as np
import concourse.bass as bass
from concourse import mybir

P = 128
T = 512
D = 1024
NT = T // P
KD = D // P
HEADS = 8
GROUPS = 2
REP = HEADS // GROUPS
CHUNK = 32
NCHUNK = T // CHUNK
CPT = P // CHUNK
CMP = 32
STRIDE = 16
NCMP = T // STRIDE - CMP // STRIDE + 1
BUCKETS = 32
MAX_DIST = 128
NEXP = 32
EXP_GROUPS = 4
EPG = NEXP // EXP_GROUPS
DE = 512
CAP = 64
OVB = (2 * T - 1) // CAP
MAIN = NEXP * CAP
SLOTS = 24 * P
SB_HEADS = 16
DFF = 2816
FT = DFF // P
ALPHA = 2 ** 0.25
NEG = -1e30
SCALE = P ** -0.5
SB_SCALE = 64 ** -0.5
Q_H, F_H, I_H, G_H, Q_N, KV_N, GATE_N = 0, 1024, 2048, 3072, 4096, 5120, 6656
MG_H = GATE_N + 3 * HEADS
MG_N = MG_H + D
REL = 2 * T - 1

_at, _c = {}, 0
for _name, _n in (("ident", P), ("ones", P), ("before", P), ("sbmask", P), ("chunk", CPT), ("reset", T),
                  ("zeros", T), ("attmask", P), ("iota", NEXP), ("slot0", NEXP), ("token", NT),
                  ("full", 7), ("block", 16)):
    _at[_name] = (_c, _n)
    _c += _n
NCONST = _c


def shape_constants():
    p = np.arange(P)
    c = np.zeros((P, NCONST), np.float32)

    def put(name, value):
        a, n = _at[name]
        c[:, a:a + n] = value

    put("ident", np.eye(P))
    put("ones", 1.0)
    put("before", p[:, None] < p[None, :])
    put("sbmask", np.where(p[None, :] < p[:, None], 0.0, NEG))
    put("chunk", p[:, None] // CHUNK == np.arange(CPT)[None])
    put("reset", (np.arange(T) % CHUNK != 0)[None])
    put("attmask", (p[:, None] // CHUNK == p[None] // CHUNK) & (p[:, None] <= p[None]))
    put("iota", np.arange(NEXP)[None])
    put("slot0", CAP * np.arange(NEXP)[None])
    put("token", p[:, None] + P * np.arange(NT)[None])
    put("full", CAP * np.arange(1, 8)[None])
    put("block", np.arange(16)[None])
    dist = np.arange(REL) - (T - 1)
    n = np.maximum(dist, 0)
    nf = np.maximum(n, 1).astype(np.float32)
    half = BUCKETS // 2
    large = half + (np.log(nf / half) / math.log(MAX_DIST / half) * (BUCKETS - half)).astype(np.int32)
    bucket = np.where(n < half, n, np.minimum(large, BUCKETS - 1))
    bucket = np.where(dist < 0, BUCKETS, bucket)
    hot = np.zeros((BUCKETS + 1, REL + 1), np.float32)
    hot[bucket, np.arange(REL)] = 1.0
    return {"shape_const": c, "rel_hot": hot, "neg_row": np.full((1, HEADS), NEG, np.float32),
            "no_token": np.zeros((SLOTS, 1), np.int32)}


def block_kernel(nc, io, out):
    f32, f32r, i32, u32 = mybir.dt.float32, mybir.dt.float32r, mybir.dt.int32, mybir.dt.uint32
    ACT, ALU, AX = mybir.ActivationFunctionType, mybir.AluOpType, mybir.AxisListType
    ctx = ExitStack()
    with ctx:
        rounded = {}

        def sb(name, shape, dt=f32):
            return ctx.enter_context(nc.sbuf_tensor(name, shape, dt))

        def sb_both(name, shape):
            t = sb(name, shape)
            size = 4 * int(np.prod(shape[1:]))
            rounded[name] = nc.alloc_sbuf_tensor_at(name + "_rounded", shape, f32r, offset=nc.sbuf_base - size)
            return t

        sems = {}

        def sem(name):
            if name not in sems:
                sems[name] = ctx.enter_context(nc.semaphore(name))
            return sems[name]

        NS = 3
        ring = sb_both("ring", [P, NS + 1, 4096])
        xres = sb("xres", [P, NT, D])
        hT = sb_both("hT", [P, KD, T])
        brn = sb_both("brn", [P, 2, 4096])
        scr = sb_both("scr", [P, FT * T])
        rows = sb_both("rows", [P, 6, D])
        cst = sb("cst", [P, NCONST])
        vec = sb("vec", [P, 3, P])
        mod = sb("mod", [P, 12, KD])
        csil = sb("csil", [P, 2 * KD])
        colb = sb("colb", [P, 40])
        st = sb("st", [P, 96])
        bnb = sb("bnb", [P, NT, 2, 6])
        mv = sb("mv", [P, NT, 2])
        comb = sb("comb", [P, NT, 2])
        dest = sb("dest", [P, NT, 2], i32)
        token = sb("token", [P, NT], i32)
        slot_token = sb("slot_token", [P, SLOTS // P], i32)
        over = sb("over", [P, 16], i32)
        over_token = sb("over_token", [CAP, 1], i32)
        ps = ctx.enter_context(nc.psum_tensor("ps", [P, 8, 512], f32))
        rel_dram = nc.dram_tensor("rel_scratch", (HEADS, REL + 1), f32).ap()
        xn_dram = nc.dram_tensor("xn_scratch", (T, D), f32).ap()
        slot_dram = nc.dram_tensor("slot_scratch", (SLOTS, 1), i32).ap()
        y_dram = nc.dram_tensor("y_scratch", (SLOTS, D), f32).ap()

        def const(name):
            a, n = _at[name]
            return cst[:, a:a + n]

        def grow(ap, n, at=2):
            ap = ap.unsqueeze(at)
            shape = list(ap.shape)
            shape[at] = n
            return ap.to_broadcast(shape)

        ident, ones = const("ident"), const("ones")
        oH = brn[:, 0, :].rearrange("p (k t) -> p k t", k=KD)
        oN = brn[:, 1, :].rearrange("p (k t) -> p k t", k=KD)
        SH1, SC1, G1, SH2, SC2, G2, SHM, SCM, GM, SHF, SCF, GF = range(12)
        ROW_G1, ROW_G2, ROW_GM, ROW_GF, ROW_A, ROW_B = range(6)

        full = [sem(f"bank{b}_full") for b in range(8)]
        empty = [sem(f"bank{b}_empty") for b in range(8)]
        fills = [0] * 8
        filling = {}

        def open_bank(pe, b, name):
            if fills[b]:
                pe.wait_ge(empty[b], fills[b])
            fills[b] += 1
            filling[name] = (b, fills[b])
            return ps[:, b, :]

        def close_bank(name, instruction):
            instruction.then_inc(full[filling[name][0]], 1)

        def filled(eng, name):
            b, n = filling[name]
            eng.wait_ge(full[b], n)
            return ps[:, b, :]

        def emptied(eng, name):
            b, n = filling[name]
            eng.wait_ge(empty[b], n)

        def free_bank(name, instruction):
            instruction.then_inc(empty[filling[name][0]], 1)

        arrived_sem = [sem(f"chunk_slot{s}_full") for s in range(NS)]
        chunk_no = {}
        used_by = {}

        chunk_list = []

        def plan(name, parts):
            chunk_no[name] = len(chunk_list)
            chunk_list.append((name, parts))

        def slot_of(name):
            return ring[:, chunk_no[name] % NS, :]

        arrived_at = {}

        def arrived(pe, name):
            n = chunk_no[name]
            pe.wait_ge(arrived_sem[n % NS], arrived_at[name])
            return slot_of(name)

        def last_use(name, fill):
            used_by[chunk_no[name]] = fill

        NPIECE = 4
        piece_no = {}
        piece_used = {}

        def single(ap):
            whole = rounded[ap.tensor.name]
            return bass.AP(tensor=whole[:, 0:1].tensor, offset=ap.offset, ap=ap.ap)

        def as_float(ap):
            return single(ap).bitcast(f32)

        def piece_high(q):
            return ring[:, NS, (q % NPIECE) * 1024:(q % NPIECE + 1) * 1024]

        def piece_low(chunk, j):
            return slot_of(chunk)[:, j * 1024:(j + 1) * 1024]

        def pe_piece(pe, chunk, j):
            q = piece_no[chunk, j] = len(piece_no)
            pe.wait_ge(sem("piece_split"), q + 1)
            return single(piece_high(q)), single(piece_low(chunk, j))

        def used(eng, entry):
            if entry[0] == "pieces":
                eng.wait_ge(sem("pieces_used"), entry[1])
            else:
                filled(eng, entry)

        counted_pieces = [0]

        def count_piece(chunk, j, instruction):
            instruction.then_inc(sem("pieces_used"), 1)
            counted_pieces[0] += 1
            piece_used[piece_no[chunk, j]] = ("pieces", counted_pieces[0])

        def act_round(a, chunk, j):
            q = piece_no[chunk, j]
            arrived(a, chunk)
            if q >= NPIECE:
                used(a, piece_used[q - NPIECE])
            a.activation(single(piece_high(q)), piece_low(chunk, j), ACT.Copy).then_inc(sem("piece_rounded"), 1)

        def dve_rest(v, chunk, j):
            v.wait_ge(sem("piece_rounded"), piece_no[chunk, j] + 1)
            low = piece_low(chunk, j)
            v.tensor_tensor(single(low), low, as_float(piece_high(piece_no[chunk, j])), ALU.subtract).then_inc(sem("piece_split"), 1)

        def triple(pe, dst, lhs, rhs, start, stop):
            pe.matmul(dst, lhs[0], rhs[0], start=start, stop=False)
            pe.matmul(dst, lhs[0], rhs[1], start=False, stop=False)
            return pe.matmul(dst, lhs[1], rhs[0], start=False, stop=stop)

        def cols(w, a, n):
            return w[0, :, a:a + n].rearrange("(k p) n -> p k n", p=P)

        def plan_wide(name, w, a):
            plan(name, [(lambda s: s.rearrange("p (k n) -> p k n", k=KD), cols(w, a, 512))])

        def plan_quad(name, quad):
            plan(name, [((lambda s, j=j: s[:, j * 1024:(j + 1) * 1024].rearrange("p (k n) -> p k n", k=KD)),
                         cols(w, a, P)) for j, (w, a) in enumerate(quad)])

        def wide(s):
            return s.rearrange("p (k n) -> p k n", k=KD)

        def quad(s, j):
            return s[:, j * 1024:(j + 1) * 1024].rearrange("p (k n) -> p k n", k=KD)

        A = io
        ada_todo = [(1, c) for c in (4, 5, 6, 7, 8, 9, 10, 11)] + [(2, c) for c in range(12)]
        ada_at = {("attn", h): ada_todo[h] for h in range(8)}
        for h in range(8):
            ada_at[("hg", h)] = ada_todo[8 + h]
        for j in range(4):
            ada_at[("merge", j)] = ada_todo[16 + j]

        def plan_ada(m, c):
            plan_wide(("ada", m, c), A["ada_w"] if m == 1 else A["ada_w_2"], 512 * c)

        for c in range(4):
            plan_ada(1, c)
        for c in range(3):
            plan_wide(("kv", c), A["w_in"], KV_N + 512 * c)
        for kv in ("k", "v"):
            plan(("cmp", kv), [(lambda s: s.rearrange("p (t n) -> p t n", t=CMP),
                                A[f"cmp_w1_{kv}"][0].rearrange("(t p) n -> p t n", p=P))])
        for h in range(8):
            if h in (0, 1, 3, 5):
                j = (h + 1) // 2
                plan(("nq", j), [(lambda s: s[:, 0:2048].rearrange("p (k n) -> p k n", k=KD),
                                  cols(A["w_in"], Q_N + 256 * j, 256))])
            plan_ada(*ada_at[("attn", h)])

        def plan_head(h):
            w = A["w_in"]
            plan_quad(("hg", h), [(w, Q_H + P * h), (w, F_H + P * h), (w, G_H + P * h), (w, I_H + P * h)])

        plan_head(0)
        for h in range(8):
            if h < 7:
                plan_head(h + 1)
            plan_ada(*ada_at[("hg", h)])
        for j in range(8):
            plan_quad(("merge", j), [(A["w_in"], MG_H + P * j), (A["w_in"], MG_N + P * j),
                                     (A["w_br_hg"], P * j), (A["w_br_nsa"], P * j)])
            if j < 4:
                plan_ada(*ada_at[("merge", j)])
        for c in range(2):
            plan_wide(("wout", c), A["w_out"], 512 * c)
        AFTER_MOE = len(chunk_list)
        for j in range(KD):
            w = A["sb_w_qkv_2"]
            plan_quad(("sb", j), [(w, P * j), (w, D + P * j), (w, 2 * D + P * j)])
        for c in range(2):
            plan_wide(("wo", c), A["sb_w_o_2"], 512 * c)
        for c in range(FT // 2):
            w = A["ffn_w_in_2"]
            plan_quad(("fi", c), [(w, m * DFF + (2 * c + x) * P) for x in range(2) for m in range(2)])
        for c in range(-(-FT // 4)):
            n = min(4, FT - 4 * c)
            plan(("fo", c), [((lambda s, n=n: s[:, 0:n * D].rearrange("p (k n) -> p k n", k=n)),
                              A["ffn_w_out_2"][0, 4 * P * c:4 * P * c + n * P, :].rearrange("(k p) n -> p k n", p=P))])
        count = [0] * NS
        for name, parts in chunk_list:
            s = chunk_no[name] % NS
            count[s] += 16 * len(parts)
            arrived_at[name] = count[s]

        class Cut:

            def __init__(self, base=0):
                self.at = base

            def __call__(self, n):
                a, self.at = self.at, self.at + n
                assert self.at <= FT * T, self.at
                return scr[:, a:a + n]

        cut = Cut()
        bias_back = cut(HEADS * T).rearrange("p (h j) -> p h j", h=HEADS)
        biasT = bias_back[:, :, ::-1]
        cbias = cut(HEADS * NT * NCMP).rearrange("p (h i n) -> p h i n", h=HEADS, i=NT)
        cmask = cut(NT * NCMP).rearrange("p (i n) -> p i n", i=NT)
        gates = sb("gates", [P, NT, 24])[:, :, :]
        kcmpT = sb("kcmpT", [P, GROUPS * NCMP])[:, :]
        vcmp = cut(GROUPS * P).rearrange("p (g n) -> p g n", g=GROUPS)
        w2cmp = cut(2 * P).rearrange("p (a n) -> p a n", a=2)
        attn_base = cut.at
        qT = cut(2 * T).rearrange("p (a n) -> p a n", a=2)
        SW = 2 * T + 32
        prob = cut(2 * SW).rearrange("p (a n) -> p a n", a=2)
        probT = cut(2 * 9 * P).rearrange("p (a k n) -> p a k n", a=2, k=9)
        dg = rows[:, 1, 0:6 * P].rearrange("p (a b n) -> p a b n", a=2, b=3)
        kfull = brn[:, 0, 0:2048].rearrange("p (a g t) -> p a g t", a=2, g=GROUPS)
        vfull = brn[:, 0, 2048:4096].rearrange("p (a i n) -> p a i n", a=2, i=NT)
        kvc = brn[:, 1, 0:2048].rearrange("p (a g t) -> p a g t", a=2, g=GROUPS)
        cut2 = Cut(attn_base)
        blocks = cut2(CMP * GROUPS * NCMP).rearrange("p (t g n) -> p t g n", t=CMP, g=GROUPS)
        hid = cut2(2 * GROUPS * NCMP).rearrange("p (a n) -> p a n", a=2)
        hsig = cut2(2 * GROUPS * NCMP).rearrange("p (a n) -> p a n", a=2)
        wgate = cut2(KD * 24).rearrange("p (k n) -> p k n", k=KD)
        vbias = cut2(T).rearrange("p (a n) -> p a n", a=2)
        gbias = cut2(24)
        tab = sb("tab", [P, HEADS])
        xn = scr[:, attn_base:attn_base + NT * D].rearrange("p (i n) -> p i n", i=NT)
        longb_back = brn[:, :, :].rearrange("p a n -> p (a n)")[:, 0:HEADS * 896].rearrange("p (h j) -> p h j", h=HEADS)
        longb = longb_back[:, :, ::-1]
        hot = hT[0:BUCKETS + 1, 0:2, :].rearrange("p a n -> p (a n)")
        relrow = hT[0:HEADS, 2:4, :].rearrange("p a n -> p (a n)")
        packs = rows[:, 0:1, 0:3 * P].rearrange("p a (b n) -> p (a b) n", b=3)

        h1_high = rows[:, 0:4, :].rearrange("p a n -> p (a n)").rearrange("p (k t) -> p k t", k=KD)
        b0T, b1T = oH, oN

        block = ctx.enter_context(nc.Block())

        c_col = lambda k: vec[:, 0, k:k + 1]
        ADAB1 = 16
        POSK, POSV = 64, 96
        BIN, BMG, ADAB2, HGN, B1 = 0, 52, 68, 116, 124

        def bin_col(a):
            j = a // P if a < GATE_N else BMG + (a - MG_H) // P
            return vec[:, 1, j:j + 1]

        def gemm(pe, dst, lhs, rhs, n=KD, start=True):
            for k in range(n):
                last = pe.matmul(dst, lhs(k), rhs(k), start=start and k == 0, stop=k == n - 1)
            return last

        def pe_ada(pe, m, c, bank):
            name = ("ada", m, c)
            pe.wait_ge(sem("ada_added"), 4 * (list(ada_at.values()).index((m, c)) + 1))
            acc = slot_of(name)[:, 0:512]
            dst = open_bank(pe, bank, name)
            for j in range(4):
                last = pe.matmul(dst[:, j:j + 1], acc[:, j * P:(j + 1) * P], ones[:, 0:1], start=True, stop=True)
            close_bank(name, last)
            last_use(name, name)

        def pe_ada_whole(pe, m, c, bank):
            name = ("ada", m, c)
            s = wide(arrived(pe, name))
            dst = open_bank(pe, bank, name)
            for j in range(4):
                last = gemm(pe, dst[:, j:j + 1], lambda k: s[:, k, j * P:(j + 1) * P],
                            lambda k: csil[:, (m - 1) * KD + k:(m - 1) * KD + k + 1])
            close_bank(name, last)
            last_use(name, name)

        def pe_start(pe):
            pe.wait_ge(sem("const_in"), 16)
            pe.wait_ge(sem("packs_in"), 16 * N_PACK)
            t = open_bank(pe, 7, "vec")
            for b, n in ((0, P), (1, 126), (2, 48)):
                last = pe.transpose(t[:, b * P:b * P + n], packs[0:n, b, :], ident[0:n, 0:n])
            close_bank("vec", last)
            pe.wait_ge(sem("rel_in"), 48)
            for c in range(2):
                t = open_bank(pe, 5 + c, ("rel", c))
                close_bank(("rel", c), pe.matmul(t[0:HEADS, :], tab[0:BUCKETS + 1, :],
                                                 hot[:, c * 512:(c + 1) * 512], start=True, stop=True))
            pe.wait_ge(sem("silu_c"), 1)
            for c in range(4):
                pe_ada_whole(pe, 1, c, c % 2)
            pe.wait_ge(sem("ln_done"), 4)
            pe_transposes(pe, "h1", xn)

        def pe_transposes(pe, name, src):
            for k in range(KD):
                t = open_bank(pe, 2 + k % 4, (name, k))
                for i in range(NT):
                    last = pe.transpose(t[:, i * P:(i + 1) * P], src[:, i, k * P:(k + 1) * P], ident)
                close_bank((name, k), last)

        def feature_major(pe, bank, name, w, src=None):
            t = open_bank(pe, bank, name)
            close_bank(name, gemm(pe, t, w, lambda k: (src if src is not None else hT)[:, k, :]))

        def feature_major3(pe, bank, name, chunk, j, high, low):
            wh, wl = (quad(x, 0) for x in pe_piece(pe, chunk, j))
            t = open_bank(pe, bank, name)
            for k in range(KD):
                last = triple(pe, t, (wh[:, k, :], wl[:, k, :]), (single(high[:, k, :]), single(low[:, k, :])),
                              k == 0, k == KD - 1)
            close_bank(name, last)
            piece_used[piece_no[chunk, j]] = name

        def token_major3(pe, bank, name, chunk, j, high, low):
            wh, wl = (quad(x, 0) for x in pe_piece(pe, chunk, j))
            t = open_bank(pe, bank, name)
            for i in range(NT):
                rows_ = slice(i * P, (i + 1) * P)
                for k in range(KD):
                    last = triple(pe, t[:, rows_], (single(high[:, k, rows_]), single(low[:, k, rows_])),
                                  (wh[:, k, :], wl[:, k, :]), k == 0, k == KD - 1)
            close_bank(name, last)
            piece_used[piece_no[chunk, j]] = name

        def pe_kv(pe):
            for k in range(KD):
                emptied(pe, ("h1", k))
            for c in range(3):
                s = wide(arrived(pe, ("kv", c)))
                nf = 4 if c == 0 else 2
                for j in range(nf):
                    feature_major(pe, j, ("kvT", c, j), lambda k: s[:, k, j * P:(j + 1) * P])
                name = ("kvT", c, nf - 1)
                if c:
                    for i2 in range(2):
                        name = ("vtok", c, i2)
                        t = open_bank(pe, 4 + i2, name)
                        for i in (2 * i2, 2 * i2 + 1):
                            last = gemm(pe, t[:, (i % 2) * 256:(i % 2) * 256 + 256],
                                        lambda k: hT[:, k, i * P:(i + 1) * P], lambda k: s[:, k, 256:512])
                        close_bank(name, last)
                last_use(("kv", c), name)
            pe.wait_ge(sem("small_in"), 16 * N_SMALL)
            t = open_bank(pe, 6, "gate")
            for i in range(NT):
                last = gemm(pe, t[:, i * 24:(i + 1) * 24], lambda k: hT[:, k, i * P:(i + 1) * P],
                            lambda k: wgate[:, k, :])
            close_bank("gate", last)
            for a, kv in enumerate("kv"):
                s = arrived(pe, ("cmp", kv)).rearrange("p (t n) -> p t n", t=CMP)
                pe.wait_ge(sem("blocks_ready"), 4 * (a + 1))
                name = ("hid", kv)
                t = open_bank(pe, 7, name)
                last = gemm(pe, t[:, 0:GROUPS * NCMP], lambda k: s[:, k, :],
                            lambda k: blocks[:, k, :, :].rearrange("p g n -> p (g n)"), n=CMP)
                close_bank(name, last)
                last_use(("cmp", kv), name)
            emptied(pe, ("hid", "v"))
            t = open_bank(pe, 0, "kcmp")
            close_bank("kcmp", pe.matmul(t[:, 0:GROUPS * NCMP], w2cmp[:, 0, :], hid[:, 0, :], start=True, stop=True))
            t = open_bank(pe, 1, "vcmp")
            for g in range(GROUPS):
                last = pe.matmul(t[0:NCMP, g * P:(g + 1) * P], hid[:, 1, g * NCMP:(g + 1) * NCMP],
                                 w2cmp[:, 1, :], start=True, stop=True)
            close_bank("vcmp", last)

        UNITS = [(h, i) for h in range(HEADS) for i in range(NT)]

        def pe_attention(pe):
            emptied(pe, "kcmp")
            emptied(pe, "vcmp")
            for c in (1, 2):
                for j in range(2):
                    emptied(pe, ("kvT", c, j))
                    emptied(pe, ("vtok", c, j))

            def query(h):
                s = arrived(pe, ("nq", h // 2))[:, 0:2048].rearrange("p (k n) -> p k n", k=KD)
                feature_major(pe, 7, ("nqT", h), lambda k: s[:, k, (h % 2) * P:(h % 2 + 1) * P])
                if h % 2:
                    last_use(("nq", h // 2), ("nqT", h))

            def scores(u):
                h, i = UNITS[u]
                if i == 0:
                    emptied(pe, ("nqT", h))
                n = P * (i + 1)
                for a in range(2):
                    name = ("S", a, u)
                    t = open_bank(pe, 2 * a + u % 2, name)
                    close_bank(name, pe.matmul(t[:, 0:n], qT[:, h % 2, i * P:(i + 1) * P], kfull[:, a, h // REP, 0:n],
                                               start=True, stop=True))

            def compressed(u):
                t = open_bank(pe, 4, ("C", u))
                if u < len(UNITS):
                    h, i = UNITS[u]
                    last = pe.matmul(t[:, 0:NCMP], qT[:, h % 2, i * P:(i + 1) * P],
                                     kcmpT[:, h // REP * NCMP:(h // REP + 1) * NCMP], start=True, stop=True)
                if u:
                    pe.wait_ge(sem("diag_ready"), u)
                    last = pe.matmul(t[0:NCMP, P:2 * P], prob[:, (u - 1) % 2, 2 * T:2 * T + NCMP], dg[:, (u - 1) % 2, 0, :],
                                     start=True, stop=True)
                close_bank(("C", u), last)

            def transposes(u):
                for a in range(2):
                    t = open_bank(pe, 5 + a, ("T", a, u))
                    for j in range(UNITS[u][1] + 1):
                        last = pe.matmul(t[:, j * P:(j + 1) * P], prob[:, u % 2, a * T + j * P:a * T + (j + 1) * P],
                                         dg[:, u % 2, 1 + a, :], start=True, stop=True)
                    close_bank(("T", a, u), last)

            query(0)
            for u in range(2):
                scores(u)
                compressed(u)
            transposes(0)
            for u, (h, i) in enumerate(UNITS):
                if i == 1 and h + 1 < HEADS:
                    query(h + 1)
                if i == 2:
                    pe_ada(pe, *ada_at[("attn", h)], 7)
                if u + 2 < len(UNITS):
                    scores(u + 2)
                if u + 1 < len(UNITS):
                    compressed(u + 2)
                    transposes(u + 1)
                t = open_bank(pe, 7, ("O", u))
                emptied(pe, ("C", u + 1))
                g = h // REP
                pe.matmul(t[:, 0:P], vcmp[0:NCMP, g, :], probT[0:NCMP, u % 2, 8, :], start=True, stop=False)
                for a in range(2):
                    emptied(pe, ("T", a, u))
                    for j in range(i + 1):
                        last = pe.matmul(t[:, 0:P], vfull[:, a, j, g * P:(g + 1) * P], probT[:, u % 2, 4 * a + j, :],
                                         start=False, stop=a == 1 and j == i)
                close_bank(("O", u), last)

        def state_ready(eng, h, n):
            i, c = (n - 1) // CPT, (n - 1) % CPT
            if c == CPT - 1 or n == NCHUNK - 1:
                emptied(eng, ("U", h, i))
            else:
                eng.wait_ge(sem("hg_state"), 11 * h + 3 * i + c + 1)

        def pe_hgrn(pe):
            def project(h, which):
                if which < 3:
                    feature_major3(pe, which, (("hq", "hf", "hg")[which], h), ("hg", h), which, h1_high, hT)
                else:
                    token_major3(pe, 3, ("hi", h), ("hg", h), 3, h1_high, hT)
                    last_use(("hg", h), ("hi", h))

            pe.wait_ge(sem("h1_split"), KD)
            for which in range(4):
                project(0, which)
            for h in range(HEADS):
                more = h + 1 < HEADS
                if more:
                    project(h + 1, 0)
                    project(h + 1, 1)
                pe.wait_ge(sem("hg_kend"), h + 1)
                t = open_bank(pe, 4, ("kendT", h))
                for i in range(NT):
                    last = pe.transpose(t[:, i * P:(i + 1) * P], hKN[:, i * P:(i + 1) * P], ident)
                close_bank(("kendT", h), last)
                t = open_bank(pe, 5, ("att", h))
                for i in range(NT):
                    c = slice(i * P, (i + 1) * P)
                    last = pe.matmul(t[:, c], hKI[:, c], hQ[:, h % 2, c], start=True, stop=True)
                close_bank(("att", h), last)
                if more:
                    project(h + 1, 2)
                    project(h + 1, 3)
                emptied(pe, ("hi", h))
                for i in range(NT):
                    if i < NT - 1:
                        pe.wait_ge(sem("hg_kblocks"), (NT - 1) * h + i + 1)
                    else:
                        emptied(pe, ("kendT", h))
                    t = open_bank(pe, 6 + i % 2, ("U", h, i))
                    for c in range(CPT):
                        last = pe.matmul(t[:, c * P:(c + 1) * P], hKX[:, i % 2, c, :], hV[:, h % 2, i, :],
                                         start=True, stop=True)
                    close_bank(("U", h, i), last)
                emptied(pe, ("att", h))
                t = open_bank(pe, 4, ("oT", h))
                for i in range(NT):
                    c = slice(i * P, (i + 1) * P)
                    last = pe.matmul(t[:, c], hV[:, h % 2, i, :], hAT[:, c], start=True, stop=False,
                                     skip_group_check=True)
                    for n in range(CPT * i, CPT * (i + 1)):
                        if n:
                            state_ready(pe, h, n)
                            last = pe.matmul(t[:, n * CHUNK:(n + 1) * CHUNK], hS[:, n, :],
                                             hQ[:, h % 2, n * CHUNK:(n + 1) * CHUNK], start=False,
                                             stop=n == CPT * (i + 1) - 1, skip_group_check=True)
                close_bank(("oT", h), last)
                pe_ada(pe, *ada_at[("hg", h)], 6)
                pe.wait_ge(sem("hg_square"), h + 1)
                t = open_bank(pe, 5, ("ss", h))
                close_bank(("ss", h), pe.matmul(t, ones, hT2[:, :], start=True, stop=True))

        def pe_merge(pe):
            for j in range(KD):
                b = 4 * (j % 2)
                c = ("merge", j)
                feature_major3(pe, b, ("mgh", j), c, 0, h1_high, hT)
                feature_major3(pe, b + 1, ("mgn", j), c, 1, h1_high, hT)
                s = arrived(pe, c)
                feature_major(pe, b + 3, ("mN", j), lambda k: quad(s, 3)[:, k, :], oN)
                if j == 0:
                    pe.wait_ge(sem("hg_out"), 2 * HEADS)
                feature_major(pe, b + 2, ("mH", j), lambda k: quad(s, 2)[:, k, :], oH)
                last_use(c, ("mH", j))
                if j < 4:
                    pe_ada(pe, *ada_at[("merge", j)], 7 - b)
            for c in range(2):
                out_projection(pe, "wout", c, mT_high, mT, ("wout_split", 1))
                if c == 0:
                    for x in range(8):
                        pe.wait_ge(sem("gate_diag"), x + 1)
                        t = open_bank(pe, 4 + x % 4, ("row", x))
                        close_bank(("row", x), pe.matmul(t, ones, mD[:, x % 2, :], start=True, stop=True))

        def out_projection(pe, kind, c, high, low, ready):
            t = {}
            for j in range(4):
                wh, wl = (x.rearrange("p (k n) -> p k n", k=2) for x in pe_piece(pe, (kind, c), j))
                for k in (2 * j, 2 * j + 1):
                    if c == 0:
                        pe.wait_ge(sem(ready[0]), ready[1] * (k + 1))
                    for i in range(NT):
                        if k == 0:
                            t[i] = open_bank(pe, 4 * c + i, (kind, c, i))
                        cut_ = slice(i * P, (i + 1) * P)
                        last = triple(pe, t[i], (single(high[:, k, cut_]), single(low[:, k, cut_])),
                                      (wh[:, k % 2, :], wl[:, k % 2, :]), k == 0, k == KD - 1)
                        if k == KD - 1:
                            close_bank((kind, c, i), last)
                if j < 3:
                    count_piece((kind, c), j, last)
                else:
                    piece_used[piece_no[(kind, c), j]] = (kind, c, NT - 1)
            last_use((kind, c), (kind, c, NT - 1))

        cut3 = Cut()
        hQ = cut3(2 * T).rearrange("p (a n) -> p a n", a=2)
        hF = cut3(2 * T).rearrange("p (a n) -> p a n", a=2)
        hG = cut3(2 * T).rearrange("p (a n) -> p a n", a=2)
        hV = cut3(2 * T).rearrange("p (a i n) -> p a i n", a=2, i=NT)
        hK, hB, hEB, hT2, hKI, hKN, hAT, hO = (cut3(T) for _ in range(8))
        hKX = cut3(2 * CPT * P).rearrange("p (a c n) -> p a c n", a=2, c=CPT)
        hS = cut3(NCHUNK * P).rearrange("p (c n) -> p c n", c=NCHUNK)
        cut4 = Cut()
        mT = cut4(KD * T).rearrange("p (k t) -> p k t", k=KD)
        mS = cut4(4 * T).rearrange("p (a n) -> p a n", a=4)
        mT_high = oH
        mD = cut4(2 * T).rearrange("p (a n) -> p a n", a=2)
        mP = cut4(4 * T).rearrange("p (a n) -> p a n", a=4)

        cut5 = Cut()
        xn2 = cut5(NT * D).rearrange("p (i n) -> p i n", i=NT)
        lg = cut5(NT * 36).rearrange("p (i n) -> p i n", i=NT)
        g8, gtop, etop = (cut5(NT * 8).rearrange("p (i n) -> p i n", i=NT) for _ in range(3))
        gat, eat = (cut5(NT * 8).rearrange("p (i n) -> p i n", i=NT).bitcast(u32) for _ in range(2))
        gexp, gone = (cut5(NT * EXP_GROUPS).rearrange("p (i n) -> p i n", i=NT) for _ in range(2))
        gsum, emax2 = (cut5(NT) for _ in range(2))
        masked, hot0, hot1, both, rank, place, tmp32 = (cut5(NT * NEXP).rearrange("p (i n) -> p i n", i=NT) for _ in range(7))
        counts, blocks_of, block_end, over0, tmp1 = (cut5(NEXP) for _ in range(5))
        cmp7 = cut5(NEXP * 7).rearrange("p (e n) -> p e n", e=NEXP)
        cmp16 = cut5(15 * NEXP).rearrange("p (b e) -> p b e", b=15)
        idxf = cut5(NT * 3).rearrange("p (i n) -> p i n", i=NT)
        slotf = cut5(NT * 2).rearrange("p (i n) -> p i n", i=NT)
        overf = cut5(16)
        tabi = cut5(P).bitcast(i32)
        tabf = cut5(P)
        assert cut5.at <= 9216
        cut5.at = 9216
        rw = cut5(KD * 36).rearrange("p (k n) -> p k n", k=KD)
        rbias = cut5(36)
        cut6 = Cut()
        gx = cut6(D)
        xT = cut6(KD * P).rearrange("p (k n) -> p k n", k=KD)
        sg = cut6(2 * DE).rearrange("p (a n) -> p a n", a=2)
        hx = cut6(2 * DE).rearrange("p (a n) -> p a n", a=2)
        aT = cut6(2 * 4 * CAP).rearrange("p (a k n) -> p a k n", a=2, k=4)
        ysb = cut6(2 * 512).rearrange("p (a n) -> p a n", a=2)
        cut6.at = max(cut6.at, 0)
        yg = scr[:, 0:2 * NT * D].rearrange("p (i a n) -> p i a n", i=NT, a=2)
        w0 = chunk_no[("wout", 0)]
        moe_slot = [ring[:, (w0 - 1) % NS, :], ring[:, w0 % NS, :], ring[:, (w0 + 1) % NS, :], ring[:, NS, :],
                    brn[:, 0, :], brn[:, 1, :]]
        cut7 = Cut()
        zq, zk = (cut7(2 * T).rearrange("p (a n) -> p a n", a=2) for _ in range(2))
        zv = cut7(2 * T).rearrange("p (a i n) -> p a i n", a=2, i=NT)
        zT = cut7(2 * T).rearrange("p (a n) -> p a n", a=2)
        zA, zU = (cut7(3 * T).rearrange("p (a n) -> p a n", a=3) for _ in range(2))
        zR = cut7(3 * (T + 4)).rearrange("p (a n) -> p a n", a=3)
        Z_BANK = (0, 1, 7)
        yb = scr[:, 0:NT * D].rearrange("p (i n) -> p i n", i=NT)
        xn3 = brn[:, 1, :].rearrange("p (i n) -> p i n", i=NT)
        h_low = b0T
        sT, sT_high = oN, b0T
        ff = scr[:, :].rearrange("p (f t) -> p f t", f=FT)
        fS = brn[:, 1, 0:2048].rearrange("p (a n) -> p a n", a=4)
        ffh = brn[:, 1, 2048:4096].rearrange("p (a n) -> p a n", a=4)
        ZU = [(j, hh, i) for j in range(KD) for hh in range(2) for i in range(NT)]

        def pe_router(pe):
            pe.wait_ge(sem("xn2_done"), NT)
            pe_transposes(pe, "h2", xn2)
            for k in range(KD):
                emptied(pe, ("h2", k))
            pe.wait_ge(sem("router_in"), 64)
            t = open_bank(pe, 0, "logits")
            for i in range(NT):
                last = gemm(pe, t[:, i * 36:(i + 1) * 36], lambda k: hT[:, k, i * P:(i + 1) * P], lambda k: rw[:, k, :])
            close_bank("logits", last)
            pe.wait_ge(sem("chosen"), 1)
            t = open_bank(pe, 1, "rank")
            for i in range(NT + 1):
                for j in range(min(i + 1, NT)):
                    last = pe.matmul(t[:, i * NEXP:(i + 1) * NEXP], const("before") if j == i else ones, both[:, j, :],
                                     start=j == 0, stop=j == min(i, NT - 1))
            close_bank("rank", last)
            pe.wait_ge(sem("slots_float"), 1)
            t = open_bank(pe, 0, "slots")
            close_bank("slots", pe.transpose(t[:, 0:SLOTS // P], tabf[0:SLOTS // P, :], ident[0:SLOTS // P, 0:SLOTS // P]))

        fills_before_moe = [0] * 8

        def pe_experts(pe):
            base = fills_before_moe
            base[:] = fills

            def gathered(p):
                pe.wait_ge(sem("gathered"), 16 * (p + 1) if isinstance(p, int) else p * 16 + 16)
                for b in range(2):
                    pe.wait_ge(empty[b], p + base[b])
                    for k in range(4 * b, 4 * b + 4):
                        last = pe.transpose(ps[:, b, (k % 4) * P:(k % 4 + 1) * P], gx[:, k * P:(k + 1) * P], ident)
                    last.then_inc(full[b], 1)

            def up(p, a):
                if a == 0:
                    for b in range(2):
                        pe.wait_ge(empty[b], p + (base[b] + 1))
                pe.wait_ge(empty[2 + a], p + base[2 + a])
                w = []
                for m in range(2):
                    pe.wait_ge(sem(f"moe_chunk{3 * a + m}_full"), p * 16 + 16)
                    w.append(moe_slot[3 * a + m].rearrange("p (k n) -> p k n", k=KD))
                for k in range(KD):
                    for m in range(2):
                        last = pe.matmul(ps[m * CAP:(m + 1) * CAP, 2 + a, :], xT[:, k, a * CAP:(a + 1) * CAP],
                                         w[m][:, k, :], start=k == 0, stop=k == KD - 1)
                last.then_inc(full[2 + a], 1)

            def down(p, a):
                pe.wait_ge(empty[2 + a], p + (base[2 + a] + 1))
                pe.wait_ge(empty[4 + a], p + base[4 + a])
                for k in range(4):
                    last = pe.matmul(ps[:, 4 + a, k * CAP:(k + 1) * CAP], hx[0:CAP, a, k * P:(k + 1) * P],
                                     ident[0:CAP, 0:CAP], start=True, stop=True)
                last.then_inc(full[4 + a], 1)
                pe.wait_ge(empty[4 + a], p + (base[4 + a] + 1))
                pe.wait_ge(empty[6 + a], p + base[6 + a])
                pe.wait_ge(sem(f"moe_chunk{3 * a + 2}_full"), p * 16 + 16)
                w = moe_slot[3 * a + 2].rearrange("p (k n) -> p k n", k=4)
                for k in range(4):
                    for m in range(2):
                        last = pe.matmul(ps[m * CAP:(m + 1) * CAP, 6 + a, :], aT[:, a, k, :],
                                         w[:, k, m * 512:(m + 1) * 512], start=k == 0, stop=k == 3)
                last.then_inc(full[6 + a], 1)

            gathered(0)
            with pe.Fori(0, NEXP // 2 - 1) as p:
                up(p, 0)
                down(p, 0)
                up(p, 1)
                gathered(p + 1)
                down(p, 1)
            p = NEXP // 2 - 1
            up(p, 0)
            down(p, 0)
            up(p, 1)
            down(p, 1)
            for b in range(8):
                fills[b] += NEXP // 2
            filling["moe_last"] = (7, fills[7])
            pe.wait_ge(sem("over_known"), 1)
            n = pe.value_load(over[0:1, 15:16], min_val=0, max_val=OVB)
            with pe.If(n > 0):
                with pe.Fori(0, n) as b:
                    pe.wait_ge(sem("ov_x"), b * 16 + 16)
                    for k in range(KD):
                        last = pe.matmul(ps[:, 0, k * CAP:(k + 1) * CAP], gx[0:CAP, k * P:(k + 1) * P], ident[0:CAP, 0:CAP],
                                         start=True, stop=True)
                    last.then_inc(sem("ov_gt"), 1)
                    pe.wait_ge(sem("ov_xt"), b + 1)
                    pe.wait_ge(sem("ov_w"), b * 48 + 48)
                    for k in range(KD):
                        for m in range(2):
                            w = moe_slot[m].rearrange("p (k n) -> p k n", k=KD)
                            last = pe.matmul(ps[m * CAP:(m + 1) * CAP, 2, :], xT[:, k, 0:CAP], w[:, k, :],
                                             start=k == 0, stop=k == KD - 1)
                    last.then_inc(sem("ov_h"), 1)
                    pe.wait_ge(sem("ov_a"), b + 1)
                    for k in range(4):
                        last = pe.matmul(ps[:, 4, k * CAP:(k + 1) * CAP], hx[0:CAP, 0, k * P:(k + 1) * P], ident[0:CAP, 0:CAP],
                                         start=True, stop=True)
                    last.then_inc(sem("ov_at"), 1)
                    pe.wait_ge(sem("ov_ate"), b + 1)
                    w = moe_slot[2].rearrange("p (k n) -> p k n", k=4)
                    for k in range(4):
                        for m in range(2):
                            last = pe.matmul(ps[m * CAP:(m + 1) * CAP, 6, :], aT[:, 0, k, :],
                                             w[:, k, m * 512:(m + 1) * 512], start=k == 0, stop=k == 3)
                    last.then_inc(sem("ov_y"), 1)
            pe.wait_ge(sem("ov_done"), 1)

        def pe_sb(pe):
            pe.wait_ge(sem("xn3_done"), NT)
            pe_transposes(pe, "h3", xn3)
            pe.wait_ge(sem("h3_split"), KD)

            def project(j, which):
                if which < 2:
                    feature_major3(pe, 5 + which, (("sq", "sk")[which], j), ("sb", j), which, hT, h_low)
                else:
                    token_major3(pe, 5, ("sv", j), ("sb", j), 2, hT, h_low)
                    last_use(("sb", j), ("sv", j))

            def scores(u):
                j, hh, i = ZU[u]
                if hh == 0 and i == 0:
                    emptied(pe, ("sq", j))
                    emptied(pe, ("sk", j))
                r, n = slice(64 * hh, 64 * hh + 64), P * (i + 1)
                t = open_bank(pe, Z_BANK[u % 3], ("z", u))
                close_bank(("z", u), pe.matmul(t[:, 0:n], zq[r, j % 2, i * P:(i + 1) * P], zk[r, j % 2, 0:n],
                                               start=True, stop=True))

            def transposes(u):
                pe.wait_ge(sem("sb_weights"), u + 1)
                t = open_bank(pe, 2 + u % 2, ("zT", u))
                for k in range(ZU[u][2] + 1):
                    last = pe.transpose(t[:, k * P:(k + 1) * P], zA[:, u % 3, k * P:(k + 1) * P], ident)
                close_bank(("zT", u), last)

            for which in range(3):
                project(0, which)
            for u in range(3):
                scores(u)
            transposes(0)
            for u, (j, hh, i) in enumerate(ZU):
                if 3 <= u % 8 < 6 and j + 1 < KD:
                    project(j + 1, u % 8 - 3)
                if u + 3 < len(ZU):
                    scores(u + 3)
                if u + 1 < len(ZU):
                    transposes(u + 1)
                if hh == 0 and i == 0:
                    emptied(pe, ("sv", j))
                emptied(pe, ("zT", u))
                r = slice(64 * hh, 64 * hh + 64)
                t = open_bank(pe, 4, ("zO", u))
                for k in range(i + 1):
                    last = pe.matmul(t[r, 0:P], zv[:, j % 2, k, 64 * hh:64 * hh + 64], zT[:, u % 2, k * P:(k + 1) * P],
                                     start=k == 0, stop=k == i)
                close_bank(("zO", u), last)
            emptied(pe, ("zO", len(ZU) - 1))
            for c in range(2):
                out_projection(pe, "wo", c, sT_high, sT, ("wo_split", 1))

        def pe_ffn(pe):
            pe.wait_ge(sem("xn4_done"), NT)
            pe_transposes(pe, "h4", xn3)
            pe.wait_ge(sem("h4_split"), KD)
            for f in range(FT):
                for m in range(2):
                    feature_major3(pe, 2 * (f % 4) + m, ("fgu", m, f), ("fi", f // 2), 2 * (f % 2) + m, hT, h_low)
                last_use(("fi", f // 2), ("fgu", 1, f))
            t = {}
            for f in range(FT):
                wh, wl = pe_piece(pe, ("fo", f // 4), f % 4)
                pe.wait_ge(sem("ff_split"), f + 1)
                for i in range(NT):
                    for c in range(2):
                        name = ("fo", c, i)
                        if f == 0:
                            t[c, i] = open_bank(pe, 4 * c + i, name)
                        tok, half = slice(i * P, (i + 1) * P), slice(c * 512, (c + 1) * 512)
                        last = triple(pe, t[c, i], (single(ffh[:, f % 4, tok]), single(ff[:, f, tok])),
                                      (wh[:, half], wl[:, half]), f == 0, f == FT - 1)
                        if f == FT - 1:
                            close_bank(name, last)
                if f < FT - 1:
                    count_piece(("fo", f // 4), f % 4, last)
                    last_use(("fo", f // 4), ("pieces", counted_pieces[0]))
                else:
                    piece_used[piece_no[("fo", f // 4), f % 4]] = name

        N_PACK = 13
        N_SMALL = 6
        pe_stages = [pe_start, pe_kv, pe_attention, pe_hgrn, pe_merge, pe_router, pe_experts, None, pe_sb, pe_ffn]

        @block.tensor
        def _(pe):
            for stage in pe_stages:
                if stage:
                    stage(pe)

        @block.sync
        def _(sp):
            def load(n):
                for view, src in chunk_list[n][1]:
                    sp.dma_start(view(slot_of(chunk_list[n][0])), src).then_inc(arrived_sem[n % NS], 16)

            for n in range(AFTER_MOE):
                if n >= NS:
                    used(sp, used_by[n - NS])
                load(n)
            w = A["exp_w1"][0], A["exp_w3"][0], A["exp_w2"][0]

            def expert_part(x, e):
                kind, k = x % 3, (KD, KD, 4)[x % 3]
                src = w[kind][bass.ds(e, 1), :, :].rearrange("a (k p) n -> p (a k) n", p=P)
                sp.dma_start(moe_slot[x].rearrange("p (k n) -> p k n", k=k), src).then_inc(sem(f"moe_chunk{x}_full"), 16)

            user = [2, 2, 6, 3, 3, 7]
            first = {b: filling["moe_last"][1] - NEXP // 2 + (fills_before_moe[b] - fills_before_moe[7]) for b in (2, 3, 6, 7)}
            for x in range(6):
                if x == 0:
                    filled(sp, used_by[chunk_no[("merge", 7)]])
                elif x == 1:
                    filled(sp, ("wout", 1, NT - 1))
                expert_part(x, x // 3)
            with sp.Fori(1, NEXP // 2) as p:
                for x in range(6):
                    sp.wait_ge(full[user[x]], p + first[user[x]])
                    expert_part(x, p * 2 + x // 3)
            sp.wait_ge(sem("over_known"), 1)
            n = sp.value_load(over[0:1, 15:16], min_val=0, max_val=OVB)
            filled(sp, "moe_last")
            with sp.If(n > 0):
                with sp.Fori(0, n) as b:
                    e = sp.value_load(over[0:1, bass.ds(b, 1)], min_val=0, max_val=NEXP - 1)
                    sp.wait_ge(sem("ov_free"), b + 1)
                    for x in range(3):
                        k = (KD, KD, 4)[x]
                        sp.dma_start(moe_slot[x].rearrange("p (k n) -> p k n", k=k),
                                     w[x][bass.ds(e, 1), :, :].rearrange("a (k p) n -> p (a k) n", p=P)).then_inc(sem("ov_w"), 16)
            sp.wait_ge(sem("ov_done"), 1)
            for n in range(AFTER_MOE, len(chunk_list)):
                if n - NS >= AFTER_MOE:
                    used(sp, used_by[n - NS])
                load(n)
            sp.wait_ge(sem("out_ready"), NT)
            sp.dma_start(out[0].rearrange("(i p) n -> p i n", p=P), xres[:, :, :]).then_inc(sem("out_stored"), 16)
            sp.wait_ge(sem("out_stored"), 16)

        def pool_start(g):
            g.dma_start(slot_dram, A["no_token"]).then_inc(sem("slots_clear"), 16)
            for c in range(2):
                emptied(g, ("rel", c))
            g.dma_start(rel_dram, relrow[:, :]).then_inc(sem("rel_stored"), 16)
            g.wait_ge(sem("rel_stored"), 16)
            g.dma_start(longb_back, bass.AP(tensor=rel_dram.tensor, offset=0,
                                            ap=[[1, P], [REL + 1, HEADS], [1, 896]])).then_inc(sem("bias_in"), 16)
            g.dma_start(bias_back, bass.AP(tensor=rel_dram.tensor, offset=T - P,
                                           ap=[[1, P], [REL + 1, HEADS], [1, T]])).then_inc(sem("bias_in"), 16)

            g.wait_ge(sem("const_in"), 16)
            g.dma_start(y_dram[MAIN:SLOTS, :].rearrange("(p a) (b n) -> p (a b) n", p=P, n=T),
                        grow(const("zeros"), (SLOTS - MAIN) // P * D // T, 1)).then_inc(sem("overflow_zero"), 16)

        def pool_ada(g, key):
            m, c = ada_at[key]
            n = 4 * list(ada_at).index(key)
            s = wide(arrived(g, ("ada", m, c)))
            col = csil[:, (m - 1) * KD:m * KD]
            g.tensor_tensor(s, s, grow(col, 512), ALU.mult).then_inc(sem("ada_added"), 1)
            for x, half in enumerate((4, 2, 1)):
                g.wait_ge(sem("ada_added"), n + x + 1)
                g.tensor_tensor(s[:, 0:half, :], s[:, 0:half, :], s[:, half:2 * half, :], ALU.add).then_inc(sem("ada_added"), 1)

        def pool_attention(g):
            g.wait_ge(sem("silu_c"), 1)
            for h in range(HEADS):
                pool_ada(g, ("attn", h))

        def pool_hgrn(g):
            for h in range(HEADS):
                pool_ada(g, ("hg", h))

        def pool_merge(g):
            for j in range(KD):
                if j < 4:
                    pool_ada(g, ("merge", j))
                emptied(g, ("mH", j))
                emptied(g, ("mN", j))
                g.tensor_tensor(mT[:, j, :], mP[:, 2 * (j % 2), :], mP[:, 2 * (j % 2) + 1, :],
                                ALU.add).then_inc(sem("merged"), 1)

        def pool_router(g):
            g.wait_ge(sem("slots_clear"), 16)
            g.wait_ge(sem("dest_ready"), 1)
            for i in range(NT):
                for c in range(2):
                    g.indirect_dma_start(slot_dram, bass.IndirectOffsetOnAxis(ap=dest[:, i, c:c + 1], axis=0),
                                         token[:, i:i + 1], None).then_inc(sem("slots_set"), 16)
            g.wait_ge(sem("slots_set"), 16 * 2 * NT)
            g.dma_start(tabi[0:SLOTS // P, :], slot_dram.rearrange("(c p) a -> c (p a)", p=P)).then_inc(sem("slots_in"), 16)

        def pool_experts(g):
            g.wait_ge(sem("xn_stored"), 16)
            g.wait_ge(sem("slots_back"), 1)
            for p in range(NEXP // 2):
                if p:
                    g.wait_ge(full[1], fills_before_moe[1] + p)
                g.indirect_dma_start(gx, None, xn_dram, bass.IndirectOffsetOnAxis(ap=slot_token[:, p:p + 1], axis=0)
                                     ).then_inc(sem("gathered"), 16)
            n = g.value_load(over[0:1, 15:16], min_val=0, max_val=OVB)
            filled(g, "moe_last")
            with g.If(n > 0):
                with g.Fori(0, n) as b:
                    g.wait_ge(sem("ov_free"), b + 1)
                    g.dma_start(over_token[:, :], slot_dram[bass.ds(b * CAP + MAIN, CAP), :]).then_inc(sem("ov_index"), 16)
                    g.wait_ge(sem("ov_index"), b * 16 + 16)
                    g.tensor_tensor(st[:, 92:93], ones[:, 0:1], ones[:, 0:1], ALU.add)
                    g.indirect_dma_start(gx[0:CAP, :], None, xn_dram,
                                         bass.IndirectOffsetOnAxis(ap=over_token[:, 0:1], axis=0)).then_inc(sem("ov_x"), 16)
            g.wait_ge(sem("ov_done"), 1)

        def pool_combine(g):
            for x in range(2):
                g.wait_ge(sem(f"y{x}_stored"), 32 * (NEXP // 2))
            g.wait_ge(sem("overflow_zero"), 16)
            for i in range(NT):
                for c in range(2):
                    g.indirect_dma_start(yg[:, i, c, :], None, y_dram, bass.IndirectOffsetOnAxis(ap=dest[:, i, c:c + 1], axis=0)
                                         ).then_inc(sem("y_gathered"), 16)

        def pool_sb(g):
            for u, (j, hh, i) in enumerate(ZU):
                n = P * (i + 1)
                g.wait_ge(sem("sb_scan"), u + 1)
                g.tensor_tensor(zA[:, u % 3, 0:n], zA[:, u % 3, 0:n], zR[:, u % 3, 1:n + 1], ALU.mult).then_inc(sem("sb_weights"), 1)

        pool_stages = [pool_start, None, pool_attention, pool_hgrn, pool_merge, pool_router, pool_experts, pool_combine, pool_sb]

        @block.gpsimd
        def _(g):
            for stage in pool_stages:
                if stage:
                    stage(g)

        def act_start(a):
            a.dma_start(cst[:, :], A["shape_const"]).then_inc(sem("const_in"), 16)
            pack = [(0, 0, A["c"].rearrange("a (k p) -> (a k) p", p=P)), (0, 8, A["c_2"].rearrange("a (k p) -> (a k) p", p=P)),
                    (0, 16, A["ada_b"].rearrange("a (k p) -> (a k) p", p=P)),
                    (0, 64, A["cmp_pos_k"][0]), (0, 96, A["cmp_pos_v"][0]),
                    (1, 0, A["b_in"][:, 0:GATE_N].rearrange("a (k p) -> (a k) p", p=P)),
                    (1, BMG, A["b_in"][:, MG_H:MG_H + 2 * D].rearrange("a (k p) -> (a k) p", p=P)),
                    (1, ADAB2, A["ada_b_2"].rearrange("a (k p) -> (a k) p", p=P)),
                    (1, HGN, A["hg_norm_w"].rearrange("a (k p) -> (a k) p", p=P)),
                    (1, B1, A["cmp_b1_k"]), (1, B1 + 1, A["cmp_b1_v"]),
                    (2, 0, A["hg_lb_logits"].rearrange("a (k p) -> (a k) p", p=P)),
                    (2, 16, A["norm_g_2"][0].rearrange("a (k p) -> (a k) p", p=P))]
            assert len(pack) == N_PACK
            for b, r, src in pack:
                a.dma_start(packs[r:r + src.shape[0], b, :], src).then_inc(sem("packs_in"), 16)
            a.dma_start(xres[:, :, :], A["x"][0].rearrange("(i p) n -> p i n", p=P)).then_inc(sem("x_in"), 16)
            with nc.allow_non_contiguous_dma(reason="the small bias table, transposed"):
                a.dma_start(tab[0:BUCKETS, :], A["rel_bias"].rearrange("h b -> b h")).then_inc(sem("rel_in"), 16)
            a.dma_start(tab[BUCKETS:BUCKETS + 1, :], A["neg_row"]).then_inc(sem("rel_in"), 16)
            a.dma_start(hot, A["rel_hot"]).then_inc(sem("rel_in"), 16)
            emptied(a, "vec")
            a.activation(csil[:, :], vec[:, 0, 0:16], ACT.Silu).then_inc(sem("silu_c"), 1)
            a.wait_ge(sem("lb_diff"), 1)
            a.activation(colb[:, 0:8], colb[:, 0:8], ACT.Sigmoid).then_inc(sem("lb_sigmoid"), 1)
            for c in range(2):
                t = filled(a, ("rel", c))
                free_bank(("rel", c), a.activation(relrow[:, c * 512:(c + 1) * 512], t[0:HEADS, :], ACT.Copy))
            act_rstd(a, "x_var", "x_sd", 0, 1e-5)
            a.wait_ge(sem("rel_stored"), 16)
            for c in range(4):
                emptied(a, ("ada", 1, c))
            act_modulate(a, "h1", SC1, SH1)

        def act_rstd(a, wait, done, col, eps):
            a.wait_ge(sem(wait), 1)
            a.activation(st[:, col + 4:col + 8], st[:, col:col + 4], ACT.Sqrt).then_inc(sem(done), 1)

        def act_modulate(a, name, sc, sh):
            for k in range(KD):
                t = filled(a, (name, k))
                free_bank((name, k), a.activation(hT[:, k, :], t, ACT.Identity, bias=mod[:, sh, k:k + 1],
                                                  scale=mod[:, sc, k:k + 1]))

        def act_high_part(a, name):
            for k in range(KD):
                emptied(a, (name, k))
                a.activation(single(hT[:, k, :]), h_low[:, k, :], ACT.Copy).then_inc(sem(name + "_rounded"), 1)

        def act_kv(a):
            a.wait_ge(sem("ln_done"), 4)
            for k in range(KD):
                filled(a, ("h1", k))
            def bc(src, n):
                return bass.AP(tensor=src.tensor, offset=src.offset, ap=[[0, P], [1, n]])
            with nc.allow_non_contiguous_dma(reason="24 gate columns"):
                a.dma_start(wgate, cols(A["w_in"], GATE_N, 24)).then_inc(sem("small_in"), 16)
            a.dma_start(gbias, bc(A["b_in"][0, GATE_N:MG_H], 24)).then_inc(sem("small_in"), 16)
            for v in range(2):
                a.dma_start(vbias[:, v, :], bc(A["b_in"][0, KV_N + 768 + 512 * v:KV_N + 1024 + 512 * v], 256)).then_inc(sem("small_in"), 16)
            for v, kv in enumerate("kv"):
                a.dma_start(w2cmp[:, v, :], A[f"cmp_w2_{kv}"][0]).then_inc(sem("small_in"), 16)
            a.dma_start(rows[:, ROW_A, :], bc(A["b_in"][0, I_H:G_H], D)).then_inc(sem("row_a_in"), 16)
            a.dma_start(rows[:, ROW_B, :], bc(A["ln1_b"][0, :], D)).then_inc(sem("row_b_in"), 16)
            a.wait_ge(sem("cbias_done"), 5)
            for c in range(3):
                for j in range(4 if c == 0 else 2):
                    t = filled(a, ("kvT", c, j))
                    dst = kvc[:, j // 2, j % 2, :] if c == 0 else kfull[:, c - 1, j, :]
                    free_bank(("kvT", c, j), a.activation(dst, t, ACT.Identity, bias=bin_col(KV_N + 512 * c + P * j)))
            emptied(a, "gate")
            a.activation(gates, gates, ACT.Sigmoid).then_inc(sem("gate_ready"), 1)
            for v, kv in enumerate("kv"):
                t = filled(a, ("hid", kv))
                a.activation(hsig[:, v, :], t[:, 0:GROUPS * NCMP], ACT.Sigmoid,
                             bias=vec[:, 1, B1 + v:B1 + v + 1]).then_inc(sem("hid_sigmoid"), 1)
            t = filled(a, "kcmp")
            free_bank("kcmp", a.activation(kcmpT, t[:, 0:GROUPS * NCMP], ACT.Copy))

        def act_attention(a):
            def query(h):
                t = filled(a, ("nqT", h))
                free_bank(("nqT", h), a.activation(qT[:, h % 2, :], t, ACT.Identity, scale=SCALE,
                                                   bias=colb[:, 16 + h:17 + h]))

            def exps(u):
                h, i = UNITS[u]
                n = P * (i + 1)
                a.wait_ge(sem("neg_max"), u + 1)
                for b, (o, m) in enumerate(((2 * T, NCMP), (0, n), (T, n))):
                    p = prob[:, u % 2, o:o + m]
                    c = 3 * (u % 2) + b
                    e = a.activation(p, p, ACT.Exp, bias=st[:, 18 + c:19 + c], accum_out=st[:, 24 + c:25 + c])
                e.then_inc(sem("exp_done"), 1)

            query(0)
            exps(0)
            exps(1)
            for u, (h, i) in enumerate(UNITS):
                t = filled(a, ("T", 1, u))
                free_bank(("T", 1, u), a.activation(probT[:, u % 2, 4:5 + i, :], t[:, 0:P * (i + 1)], ACT.Copy))
                if i == 1 and h + 1 < HEADS:
                    query(h + 1)
                if u + 2 < len(UNITS):
                    exps(u + 2)
                t = filled(a, ("O", u))
                free_bank(("O", u), a.activation(oN[:, h, i * P:(i + 1) * P], t[:, 0:P], ACT.Copy))

        def act_hgrn(a):
            filled(a, ("O", len(UNITS) - 1))
            for k in range(KD):
                a.activation(single(h1_high[:, k, :]), hT[:, k, :], ACT.Copy).then_inc(sem("h1_rounded"), 1)

            def weights(h):
                for j in range(4):
                    act_round(a, ("hg", h), j)

            weights(0)

            def inputs(h):
                t = filled(a, ("hq", h))
                free_bank(("hq", h), a.activation(hQ[:, h % 2, :], t, ACT.Identity, bias=bin_col(Q_H + P * h)))
                t = filled(a, ("hf", h))
                free_bank(("hf", h), a.activation(hF[:, h % 2, :], t, ACT.Sigmoid, bias=bin_col(F_H + P * h)))
            def out_gate(h):
                if h >= 2:
                    a.wait_ge(sem("hg_out"), 2 * (h - 1))
                t = filled(a, ("hg", h))
                free_bank(("hg", h), a.activation(hG[:, h % 2, :], t, ACT.Sigmoid, bias=bin_col(G_H + P * h)))

            inputs(0)
            out_gate(0)
            weights(1)
            for h in range(HEADS):
                a.wait_ge(sem("hg_f"), h + 1)
                if h:
                    a.wait_ge(sem("hg_out"), 2 * h - 1)
                a.activation(hT2, hF[:, h % 2, :], ACT.Ln).then_inc(sem("hg_logf"), 1)
                a.wait_ge(sem("hg_b"), 2 * h + 1)
                a.activation(hEB, hB, ACT.Exp).then_inc(sem("hg_exp"), 1)
                a.activation(hT2, hB, ACT.Exp, scale=-1.0).then_inc(sem("hg_exp"), 1)
                a.wait_ge(sem("hg_b"), 2 * h + 2)
                a.activation(hKN, hKN, ACT.Exp).then_inc(sem("hg_exp"), 1)
                if h + 1 < HEADS:
                    inputs(h + 1)
                    out_gate(h + 1)
                if h + 2 < HEADS:
                    weights(h + 2)
                emptied(a, ("oT", h))
                a.activation(hT2, hO, ACT.Square).then_inc(sem("hg_square"), 1)
                t = filled(a, ("ss", h))
                a.activation(hT2, t, ACT.Ln, scale=1.0 / P, bias=colb[:, 32:33]).then_inc(sem("hg_lnvar"), 1)
                a.wait_ge(sem("hg_lnvar"), h + 1)
                free_bank(("ss", h), a.activation(hT2, hT2, ACT.Exp, scale=-0.5))

        def act_merge(a):
            a.wait_ge(sem("hg_out"), 2 * HEADS)
            def weights(j):
                for x in range(2):
                    act_round(a, ("merge", j), x)

            weights(0)
            weights(1)
            for j in range(KD):
                for b, (name, col) in enumerate((("mgh", MG_H), ("mgn", MG_N))):
                    if j >= 2:
                        emptied(a, (("mH", "mN")[b], j - 2))
                    t = filled(a, (name, j))
                    free_bank((name, j), a.activation(mS[:, 2 * (j % 2) + b, :], t, ACT.Sigmoid, bias=bin_col(col + P * j)))
                if j + 2 < KD:
                    weights(j + 2)
            act_output_split(a, "wout", mT, mT_high, "merged")

        def act_output_split(a, kind, src, high, ready):
            for j in range(4):
                act_round(a, (kind, 0), j)
                for k in (2 * j, 2 * j + 1):
                    if ready == "merged":
                        a.wait_ge(sem(ready), KD)
                        filled(a, ("mH", KD - 1))
                    a.activation(single(high[:, k, :]), src[:, k, :], ACT.Copy).then_inc(sem(kind + "_rounded"), 1)
            for j in range(4):
                act_round(a, (kind, 1), j)

        def dve_output_split(v, kind, src, high):
            for j in range(4):
                dve_rest(v, (kind, 0), j)
                for k in (2 * j, 2 * j + 1):
                    v.wait_ge(sem(kind + "_rounded"), k + 1)
                    v.tensor_tensor(single(src[:, k, :]), src[:, k, :], as_float(high[:, k, :]), ALU.subtract).then_inc(sem(kind + "_split"), 1)

        def bcast_row(src, n):
            return bass.AP(tensor=src.tensor, offset=src.offset, ap=[[0, P], [1, n]])

        def act_router(a):
            emptied(a, ("hi", HEADS - 1))
            a.dma_start(rows[:, ROW_A, :], bcast_row(A["ln1_g"][0, :], D)).then_inc(sem("row_a_in"), 16)
            with nc.allow_non_contiguous_dma(reason="narrow router matrices"):
                a.dma_start(rw[:, :, 0:4], cols(A["router_grp_w"], 0, 4)).then_inc(sem("router_in"), 16)
                a.dma_start(rw[:, :, 4:36], cols(A["router_exp_w"], 0, NEXP)).then_inc(sem("router_in"), 16)
            a.dma_start(rbias[:, 0:4], bcast_row(A["router_grp_b"][0, :], 4)).then_inc(sem("router_in"), 16)
            a.dma_start(rbias[:, 4:36], bcast_row(A["router_exp_b"][0, :], NEXP)).then_inc(sem("router_in"), 16)
            act_rstd(a, "x1_var", "x1_sd", 0, 0)
            act_rstd(a, "xn2_var", "xn2_sd", 0, 0)
            a.wait_ge(sem("xn2_done"), NT)
            a.dma_start(xn_dram.rearrange("(i p) n -> p i n", p=P), xn2).then_inc(sem("xn_stored"), 16)
            a.dma_start(rows[:, ROW_A, :], bcast_row(A["ln2_g"][0, :], D)).then_inc(sem("row_a_in"), 16)
            a.dma_start(rows[:, ROW_B, :], bcast_row(A["ln2_b"][0, :], D)).then_inc(sem("row_b_in"), 16)
            act_modulate(a, "h2", SC2, SH2)
            a.wait_ge(sem("group_logits"), 1)
            a.activation(gexp, gexp, ACT.Exp).then_inc(sem("group_exp"), 1)
            a.wait_ge(sem("second_logit"), 1)
            a.activation(emax2, emax2, ACT.Exp).then_inc(sem("second_exp"), 1)

        def act_experts(a):
            base = fills_before_moe

            def tokens(p):
                for b in range(2):
                    a.wait_ge(full[b], p + (base[b] + 1))
                    for k in range(4 * b, 4 * b + 4):
                        e = a.activation(xT[:, k, :], ps[:, b, (k % 4) * P:(k % 4 + 1) * P], ACT.Identity,
                                         bias=mod[:, SH2, k:k + 1], scale=mod[:, SC2, k:k + 1])
                    e.then_inc(empty[b], 1)

            def gate(p, x):
                a.wait_ge(full[2 + x], p + (base[2 + x] + 1))
                a.activation(sg[0:CAP, x, :], ps[0:CAP, 2 + x, :], ACT.Silu).then_inc(sem("moe_silu"), 1)

            def store(p, x, first=False):
                a.wait_ge(full[6 + x], p + (base[6 + x] + 1))
                if not first:
                    a.wait_ge(sem(f"y{x}_stored"), p * 32)
                a.activation(ysb[:, x, :], ps[:, 6 + x, :], ACT.Copy).then_inc(empty[6 + x], 1)
                a.wait_ge(empty[6 + x], p + (base[6 + x] + 1))
                for m in range(2):
                    a.dma_start(y_dram[bass.ds(p * (2 * CAP) + x * CAP, CAP), m * 512:(m + 1) * 512],
                                ysb[m * CAP:(m + 1) * CAP, x, :]).then_inc(sem(f"y{x}_stored"), 16)

            tokens(0)

            def pair(p, first=False, last=False):
                gate(p, 0)
                store(p, 0, first)
                gate(p, 1)
                if not last:
                    tokens(p + 1)
                store(p, 1, first)

            pair(0, first=True)
            with a.Fori(1, NEXP // 2 - 1) as p:
                pair(p)
            pair(NEXP // 2 - 1, last=True)
            for x in range(2):
                a.wait_ge(sem(f"y{x}_stored"), 32 * (NEXP // 2))
            a.wait_ge(sem("over_known"), 1)
            n = a.value_load(over[0:1, 15:16], min_val=0, max_val=OVB)
            a.wait_ge(sem("overflow_zero"), 16)
            a.activation(st[:, 90:91], st[:, 8:9], ACT.Copy).then_inc(sem("ov_free"), 1)
            with a.If(n > 0):
                with a.Fori(0, n) as b:
                    a.wait_ge(sem("ov_gt"), b + 1)
                    for k in range(KD):
                        e = a.activation(xT[:, k, 0:CAP], ps[:, 0, k * CAP:(k + 1) * CAP], ACT.Identity,
                                         bias=mod[:, SH2, k:k + 1], scale=mod[:, SC2, k:k + 1])
                    e.then_inc(sem("ov_xt"), 1)
                    a.wait_ge(sem("ov_h"), b + 1)
                    a.activation(sg[0:CAP, 0, :], ps[0:CAP, 2, :], ACT.Silu).then_inc(sem("ov_s"), 1)
                    a.wait_ge(sem("ov_y"), b + 1)
                    a.activation(ysb[:, 0, :], ps[:, 6, :], ACT.Copy).then_inc(sem("ov_ys"), 1)
                    a.wait_ge(sem("ov_ys"), b + 1)
                    for m in range(2):
                        a.dma_start(y_dram[bass.ds(b * CAP + MAIN, CAP), m * 512:(m + 1) * 512],
                                    ysb[m * CAP:(m + 1) * CAP, 0, :]).then_inc(sem("ov_stored"), 16)
                    a.wait_ge(sem("ov_stored"), b * 32 + 32)
                    a.activation(st[:, 90:91], st[:, 8:9], ACT.Copy).then_inc(sem("ov_free"), 1)
            a.activation(st[:, 91:92], st[:, 8:9], ACT.Copy).then_inc(sem("ov_done"), 1)

        def act_combine(a):
            act_rstd(a, "x2_var", "x2_sd", 0, 0)

        def act_rms(a, src, ready, name, dump):
            for i in range(NT):
                a.wait_ge(sem(ready), i + 1)
                e = a.activation(dump[:, i, :], src[:, i, :], ACT.Square, accum_out=st[:, 80 + i:81 + i])
            e.then_inc(sem(name + "_ss"), 1)
            a.wait_ge(sem(name + "_ss"), 1)
            a.activation(st[:, 84:88], st[:, 80:84], ACT.Sqrt, scale=1.0 / D, bias=colb[:, 32:33]).then_inc(sem(name + "_rms"), 1)

        def act_sb(a):
            unused = brn[:, 0, :].rearrange("p (i n) -> p i n", i=NT)
            act_rms(a, xres, "x2_ready", "x2n", unused)
            act_high_part(a, "h3")

            def weights(j, which):
                act_round(a, ("sb", j), which)

            for which in range(3):
                weights(0, which)

            def inputs(j):
                t = filled(a, ("sq", j))
                free_bank(("sq", j), a.activation(zq[:, j % 2, :], t, ACT.Copy, scale=SB_SCALE))

            def sigmoids(u):
                j, hh, i = ZU[u]
                n = P * (i + 1)
                a.wait_ge(sem("sb_masked"), u + 1)
                if u >= 3:
                    filled(a, ("zT", u - 3))
                t = ps[:, Z_BANK[u % 3], 0:n]
                a.activation(zU[:, u % 3, 0:n], t, ACT.Sigmoid, scale=-1.0)
                free_bank(("z", u), a.activation(zA[:, u % 3, 0:n], t, ACT.Sigmoid))

            def output(u):
                j, hh, i = ZU[u]
                t = filled(a, ("zO", u))
                r = slice(64 * hh, 64 * hh + 64)
                free_bank(("zO", u), a.activation(sT[r, j, i * P:(i + 1) * P], t[r, 0:P], ACT.Copy))

            inputs(0)
            sigmoids(0)
            sigmoids(1)
            for u, (j, hh, i) in enumerate(ZU):
                if u % 8 == 4 and j + 1 < KD:
                    inputs(j + 1)
                if u + 2 < len(ZU):
                    sigmoids(u + 2)
                t = filled(a, ("zT", u))
                free_bank(("zT", u), a.activation(zT[:, u % 2, 0:P * (i + 1)], t[:, 0:P * (i + 1)], ACT.Copy))
                if u:
                    output(u - 1)
                if u % 8 < 3 and j + 1 < KD:
                    weights(j + 1, u % 8)
            output(len(ZU) - 1)
            emptied(a, ("zO", len(ZU) - 1))
            act_output_split(a, "wo", sT, sT_high, "")
            act_rms(a, yb, "y1_ready", "y1", hT4)
            act_rms(a, xres, "x3_ready", "x3n", unused)

        def ffn_pieces(f, split):
            if f < FT:
                for m in range(2):
                    split(("fi", f // 2), 2 * (f % 2) + m)
            else:
                for j in range(2):
                    split(("fo", 0), 2 * (f - FT) + j)

        def act_ffn(a):
            act_high_part(a, "h4")
            for f in range(2):
                ffn_pieces(f, lambda chunk, j: act_round(a, chunk, j))
            for f in range(FT):
                if f >= 4:
                    emptied(a, ("fgu", 1, f - 4))
                t = filled(a, ("fgu", 0, f))
                free_bank(("fgu", 0, f), a.activation(fS[:, f % 4, :], t, ACT.Silu))
                ffn_pieces(f + 2, lambda chunk, j: act_round(a, chunk, j))

            def hidden(f):
                if f < FT:
                    emptied(a, ("fgu", 1, f))
                    a.activation(single(ffh[:, f % 4, :]), ff[:, f, :], ACT.Copy).then_inc(sem("ff_rounded"), 1)

            for f in range(4):
                hidden(f)
            for f in range(FT - 4):
                act_round(a, ("fo", (f + 4) // 4), f % 4)
                hidden(f + 4)
            act_rms(a, hT4, "y2_ready", "y2", brn[:, 0, :].rearrange("p (i n) -> p i n", i=NT))

        hT4 = hT[:, :, :].rearrange("p k t -> p (k t)").rearrange("p (i n) -> p i n", i=NT)

        act_stages = [act_start, act_kv, act_attention, act_hgrn, act_merge, act_router, act_experts, act_combine, act_sb, act_ffn]

        @block.scalar
        def _(a):
            for stage in act_stages:
                stage(a)

        dve_steps = [0]

        def step(v, instruction):
            dve_steps[0] += 1
            instruction.then_inc(sem("dve_step"), 1)
            v.wait_ge(sem("dve_step"), dve_steps[0])

        def dve_stats(v, src, nt=NT, eps=1e-5):
            for i in range(nt):
                for c in range(2):
                    w = v.bn_stats(bnb[:, i, c, :], src[:, i, c * 512:(c + 1) * 512])
            step(v, w)
            for i in range(nt):
                w = v.bn_aggr(mv[:, i, :], bnb[:, i, :, :])
            step(v, w)
            v.tensor_copy(st[:, 8:8 + nt], mv[:, 0:nt, 0])
            return v.tensor_scalar(st[:, 0:nt], mv[:, 0:nt, 1], eps, None, ALU.add)

        def dve_ada(v, m, c):
            name = ("ada", m, c)
            t = filled(v, name)
            b = vec[:, 0, ADAB1 + 4 * c:ADAB1 + 4 * c + 4] if m == 1 else vec[:, 1, ADAB2 + 4 * c:ADAB2 + 4 * c + 4]
            one = 0.0 if c // 2 in (0, 3) or (m, c // 2) in ((2, 2), (2, 5)) else 1.0
            dst = mod[:, 6 * (m - 1) + c // 2, 4 * (c % 2):4 * (c % 2) + 4]
            free_bank(name, v.scalar_tensor_tensor(dst, t[:, 0:4], one, b, ALU.add, ALU.add))

        def dve_start(v):
            t = filled(v, "vec")
            flat = vec[:, :, :].rearrange("p a n -> p (a n)")
            v.tensor_copy(flat[:, 0:P + 126], t[:, 0:P + 126])
            free_bank("vec", v.tensor_copy(flat[:, 2 * P:2 * P + 48], t[:, 2 * P:2 * P + 48]))
            emptied(v, "vec")
            v.tensor_tensor(colb[:, 0:8], vec[:, 2, 0:8], vec[:, 2, 8:16], ALU.subtract).then_inc(sem("lb_diff"), 1)
            v.memset(colb[:, 32:33], 1e-6)
            v.tensor_scalar(colb[:, 16:24], vec[:, 1, Q_N // P:Q_N // P + 8], SCALE, None, ALU.mult)
            v.wait_ge(sem("lb_sigmoid"), 1)
            step(v, v.tensor_scalar(colb[:, 8:16], colb[:, 0:8], -1.0, 1.0, ALU.mult, ALU.add))
            v.wait_ge(sem("x_in"), 16)
            dve_stats(v, xres).then_inc(sem("x_var"), 1)
            v.wait_ge(sem("x_sd"), 1)
            step(v, v.reciprocal(st[:, 4:8], st[:, 4:8]))
            for i in range(NT):
                v.tensor_scalar(xn[:, i, :], xres[:, i, :], st[:, 8 + i:9 + i], st[:, 4 + i:5 + i], ALU.subtract,
                                ALU.mult).then_inc(sem("ln_done"), 1)
            for c in range(4):
                dve_ada(v, 1, c)

        def dve_kv(v):
            v.wait_ge(sem("bias_in"), 32)
            for i in range(NT):
                a = 384 + CMP - 1 - P * i
                v.tensor_copy(cbias[:, :, i, :], longb[:, :, a:a + STRIDE * (NCMP - 1) + 1:STRIDE]).then_inc(sem("cbias_done"), 1)
            v.wait_ge(sem("cbias_done"), 4)
            v.tensor_scalar(cmask, cbias[:, 0, :, :], NEG / 10, None, ALU.is_gt).then_inc(sem("cbias_done"), 1)

            def cmp_blocks(a):
                for g in range(GROUPS):
                    emptied(v, ("kvT", 0, 2 * a + g))
                if a:
                    filled(v, ("hid", "k"))
                for g in range(GROUPS):
                    for half in range(2):
                        src = kvc[:, a, g, :].rearrange("p (n t) -> p t n", t=STRIDE)[:, :, half:half + NCMP]
                        pos = vec[:, 0, (POSK, POSV)[a] + STRIDE * half:(POSK, POSV)[a] + STRIDE * (half + 1)]
                        v.tensor_tensor(blocks[:, STRIDE * half:STRIDE * (half + 1), g, :], src, grow(pos, NCMP),
                                        ALU.add).then_inc(sem("blocks_ready"), 1)

            def hid_silu(a, kv):
                v.wait_ge(sem("hid_sigmoid"), a + 1)
                t = filled(v, ("hid", kv))
                free_bank(("hid", kv), v.scalar_tensor_tensor(hid[:, a, :], t[:, 0:GROUPS * NCMP],
                                                              vec[:, 1, B1 + a:B1 + a + 1], hsig[:, a, :], ALU.add, ALU.mult))

            cmp_blocks(0)
            v.wait_ge(sem("small_in"), 16 * N_SMALL)
            for c in (1, 2):
                for i2 in range(2):
                    t = filled(v, ("vtok", c, i2))
                    free_bank(("vtok", c, i2), v.tensor_tensor(
                        vfull[:, c - 1, 2 * i2:2 * i2 + 2, :], t.rearrange("p (i n) -> p i n", i=2),
                        grow(vbias[:, c - 1, :], 2, 1), ALU.add))
            t = filled(v, "gate")
            free_bank("gate", v.tensor_tensor(gates, t[:, 0:96].rearrange("p (i n) -> p i n", i=NT), grow(gbias, NT, 1), ALU.add))
            cmp_blocks(1)
            hid_silu(0, "k")
            hid_silu(1, "v")
            t = filled(v, "vcmp")
            free_bank("vcmp", v.tensor_copy(vcmp[0:NCMP, :, :], t[0:NCMP, 0:GROUPS * P].rearrange("p (g n) -> p g n", g=GROUPS)))

        def dve_attention(v):
            def add_and_max(u, b, scores, o, m, bias):
                c = 12 + 3 * (u % 2) + b
                return v.tensor_tensor_reduce(out=prob[:, u % 2, o:o + m], in0=scores, in1=bias, scale=1.0, scalar=-3e38,
                                              op0=ALU.add, op1=ALU.max, accum_out=st[:, c:c + 1])

            def full_scores(u):
                h, i = UNITS[u]
                n = P * (i + 1)
                for a in range(2):
                    t = filled(v, ("S", a, u))
                    free_bank(("S", a, u), add_and_max(u, 1 + a, t[:, 0:n], a * T, n, biasT[:, h, T - n:T]))

            def compressed(u):
                t = filled(v, ("C", u))
                if u:
                    w = v.tensor_copy(probT[0:NCMP, (u - 1) % 2, 8, :], t[0:NCMP, P:2 * P])
                if u < len(UNITS):
                    h, i = UNITS[u]
                    w = add_and_max(u, 0, t[:, 0:NCMP], 2 * T, NCMP, cbias[:, h, i, :])
                free_bank(("C", u), w)
                if u < len(UNITS):
                    for a in range(2):
                        emptied(v, ("S", a, u))
                    emptied(v, ("C", u))
                    c = 3 * (u % 2)
                    v.tensor_scalar(st[:, 18 + c:21 + c], st[:, 12 + c:15 + c], -1.0, None, ALU.mult).then_inc(sem("neg_max"), 1)

            def diagonals(u):
                h, i = UNITS[u]
                c = 3 * (u % 2)
                v.wait_ge(sem("exp_done"), u + 1)
                p = prob[:, u % 2, 2 * T:2 * T + NCMP]
                v.tensor_tensor(p, p, cmask[:, i, :], ALU.mult)
                step(v, v.reciprocal(st[:, 30 + c:33 + c], st[:, 24 + c:27 + c]))
                step(v, v.tensor_tensor(st[:, 36 + c:39 + c], st[:, 30 + c:33 + c], gates[:, i, 3 * h:3 * h + 3], ALU.mult))
                v.tensor_tensor(dg[:, u % 2, :, :], grow(ident, 3, 1), grow(st[:, 36 + c:39 + c], P), ALU.mult).then_inc(sem("diag_ready"), 1)

            v.wait_ge(sem("gate_ready"), 1)
            full_scores(0)
            compressed(0)
            full_scores(1)
            diagonals(0)
            compressed(1)
            for u, (h, i) in enumerate(UNITS):
                t = filled(v, ("T", 0, u))
                free_bank(("T", 0, u), v.tensor_copy(probT[:, u % 2, 0:i + 1, :].rearrange("p a n -> p (a n)"), t[:, 0:P * (i + 1)]))
                if i == 2:
                    dve_ada(v, *ada_at[("attn", h)])
                if u + 1 < len(UNITS):
                    diagonals(u + 1)
                if u + 2 < len(UNITS):
                    full_scores(u + 2)
                if u + 1 < len(UNITS):
                    compressed(u + 2)

        def dve_hgrn(v):
            filled(v, ("O", len(UNITS) - 1))
            attmask = const("attmask").bitcast(u32)
            for k in range(KD):
                v.wait_ge(sem("h1_rounded"), k + 1)
                v.tensor_tensor(single(hT[:, k, :]), hT[:, k, :], as_float(h1_high[:, k, :]), ALU.subtract).then_inc(sem("h1_split"), 1)

            def weights(h):
                for j in range(4):
                    dve_rest(v, ("hg", h), j)

            weights(0)
            weights(1)
            v.memset(hAT, 0.0)
            v.wait_ge(sem("row_a_in"), 16)

            def values(h):
                t = filled(v, ("hi", h))
                free_bank(("hi", h), v.tensor_tensor(hV[:, h % 2, :, :], t.rearrange("p (i n) -> p i n", i=NT),
                                                     grow(rows[:, ROW_A, P * h:P * (h + 1)], NT, 1), ALU.add))

            for h in range(HEADS):
                f = hF[:, h % 2, :]
                emptied(v, ("hf", h))
                v.tensor_scalar(f, f, colb[:, 8 + h:9 + h], colb[:, h:h + 1], ALU.mult, ALU.add).then_inc(sem("hg_f"), 1)
                v.wait_ge(sem("hg_f"), h + 1)
                v.tensor_scalar(hK, f, -1.0, 1.0, ALU.mult, ALU.add)
                v.wait_ge(sem("hg_logf"), h + 1)
                v.tensor_tensor_scan(hB, const("reset"), hT2, 0.0, ALU.mult, ALU.add).then_inc(sem("hg_b"), 1)
                v.wait_ge(sem("hg_b"), 2 * h + 1)
                if h:
                    filled(v, ("kendT", h - 1))
                b3 = hB.rearrange("p (n c) -> p n c", c=CHUNK)
                v.tensor_tensor(hKN.rearrange("p (n c) -> p n c", c=CHUNK), b3[:, :, CHUNK - 1:CHUNK].to_broadcast([P, NCHUNK, CHUNK]),
                                b3, ALU.subtract).then_inc(sem("hg_b"), 1)
                emptied(v, ("hq", h))
                v.wait_ge(sem("hg_exp"), 3 * h + 1)
                v.tensor_tensor(hQ[:, h % 2, :], hQ[:, h % 2, :], hEB, ALU.mult)
                v.wait_ge(sem("hg_exp"), 3 * h + 2)
                if h:
                    filled(v, ("att", h - 1))
                v.tensor_tensor(hKI, hK, hT2, ALU.mult)
                v.wait_ge(sem("hg_exp"), 3 * h + 3)
                v.tensor_tensor(hKN, hKN, hK, ALU.mult).then_inc(sem("hg_kend"), 1)
                if h == 0:
                    values(0)

                def chunk_blocks(i):
                    t = filled(v, ("kendT", h))
                    if i >= 2:
                        filled(v, ("U", h, i - 2))
                    elif h:
                        filled(v, ("U", h - 1, i + 2))
                    w = v.tensor_tensor(hKX[:, i % 2, :, :], grow(t[:, i * P:(i + 1) * P], CPT, 1),
                                        grow(const("chunk"), P), ALU.mult)
                    if i < NT - 1:
                        w.then_inc(sem("hg_kblocks"), 1)
                    else:
                        free_bank(("kendT", h), w)

                chunk_blocks(0)
                chunk_blocks(1)
                t = filled(v, ("att", h))
                if h:
                    filled(v, ("oT", h - 1))
                free_bank(("att", h), v.copy_predicated(hAT.rearrange("p (i n) -> p i n", i=NT), grow(attmask, NT, 1),
                                                        t.rearrange("p (i n) -> p i n", i=NT)))
                if h + 1 < HEADS:
                    values(h + 1)
                for i in range(NT):
                    t = filled(v, ("U", h, i))
                    for c in range(CPT):
                        n = CPT * i + c
                        if n == NCHUNK - 1:
                            continue
                        u = t[:, c * P:(c + 1) * P]
                        if n == 0:
                            w = v.tensor_copy(hS[:, 1, :], u)
                        else:
                            state_ready(v, h, n)
                            w = v.scalar_tensor_tensor(hS[:, n + 1, :], hS[:, n, :], hEB[:, CHUNK * (n + 1) - 1:CHUNK * (n + 1)],
                                                       u, ALU.mult, ALU.add)
                        if c == CPT - 1 or n == NCHUNK - 2:
                            free_bank(("U", h, i), w)
                        else:
                            w.then_inc(sem("hg_state"), 1)
                    if i + 2 < NT:
                        chunk_blocks(i + 2)
                if h + 2 < HEADS:
                    weights(h + 2)
                t = filled(v, ("oT", h))
                free_bank(("oT", h), v.tensor_copy(hO, t))
                dve_ada(v, *ada_at[("hg", h)])
                emptied(v, ("ss", h))
                v.tensor_tensor(hO, hO, hT2, ALU.mult).then_inc(sem("hg_out"), 1)
                v.wait_ge(sem("hg_out"), 2 * h + 1)
                v.scalar_tensor_tensor(oH[:, h, :], hO, vec[:, 1, HGN + h:HGN + h + 1], hG[:, h % 2, :], ALU.mult,
                                       ALU.mult).then_inc(sem("hg_out"), 1)

        def dve_merge(v):
            def weights(j):
                for x in range(2):
                    dve_rest(v, ("merge", j), x)

            weights(0)
            weights(1)
            v.wait_ge(sem("hg_out"), 2 * HEADS)
            for j in range(KD):
                for b, m in ((1, "mN"), (0, "mH")):
                    t = filled(v, (m, j))
                    emptied(v, (("mgh", "mgn")[b], j))
                    if j >= 2:
                        v.wait_ge(sem("merged"), j - 1)
                    free_bank((m, j), v.tensor_tensor(mP[:, 2 * (j % 2) + b, :], t, mS[:, 2 * (j % 2) + b, :], ALU.mult))
                if j + 2 < KD:
                    weights(j + 2)
                if j < 4:
                    dve_ada(v, *ada_at[("merge", j)])
            emptied(v, ("ada", 2, 11))
            for which, gain in ((GM, 1), (GF, 3), (SCM, 0), (SCF, 2)):
                step(v, v.tensor_tensor(mod[:, which, :], mod[:, which, :], vec[:, 2, 16 + 8 * gain:24 + 8 * gain], ALU.mult))
            dve_output_split(v, "wout", mT, mT_high)
            for x in range(8):
                if x >= 2:
                    filled(v, ("row", x - 2))
                g = mod[:, (G1, G2, GM, GF)[x // 2], 4 * (x % 2):4 * (x % 2) + 4]
                v.tensor_tensor(mD[:, x % 2, :].rearrange("p (a n) -> p a n", a=4), grow(ident, 4, 1), grow(g, P),
                                ALU.mult).then_inc(sem("gate_diag"), 1)
                if x:
                    t = filled(v, ("row", x - 1))
                    free_bank(("row", x - 1), v.tensor_copy(rows[:, (x - 1) // 2, ((x - 1) % 2) * 512:((x - 1) % 2 + 1) * 512], t))
            t = filled(v, ("row", 7))
            free_bank(("row", 7), v.tensor_copy(rows[:, 3, 512:1024], t))
            emptied(v, ("row", 7))
            for j in range(4):
                dve_rest(v, ("wout", 1), j)
            for c in range(2):
                for i in range(NT):
                    t = filled(v, ("wout", c, i))
                    half = slice(512 * c, 512 * (c + 1))
                    tmp = mP[:, i, :]
                    free_bank(("wout", c, i), v.tensor_tensor(tmp, t, rows[:, ROW_G1, half], ALU.mult))
                    emptied(v, ("wout", c, i))
                    w = v.scalar_tensor_tensor(xres[:, i, half], xres[:, i, half], ALPHA, tmp, ALU.mult, ALU.add)
            step(v, w)

        def dve_layer_norm(v, src, dst, name, done=None):
            dve_stats(v, src).then_inc(sem(name + "_var"), 1)
            v.wait_ge(sem(name + "_sd"), 1)
            step(v, v.reciprocal(st[:, 4:8], st[:, 4:8]))
            for i in range(NT):
                w = v.tensor_scalar(dst[:, i, :], src[:, i, :], st[:, 8 + i:9 + i], st[:, 4 + i:5 + i], ALU.subtract, ALU.mult)
                if done:
                    w.then_inc(sem(done), 1)
            if not done:
                step(v, w)

        def dve_affine(v, done=None):
            for i in range(NT):
                v.wait_ge(sem("row_a_in"), ROW_LOADS[0])
                step(v, v.tensor_tensor(xres[:, i, :], xres[:, i, :], rows[:, ROW_A, :], ALU.mult))
                v.wait_ge(sem("row_b_in"), ROW_LOADS[1])
                w = v.tensor_tensor(xres[:, i, :], xres[:, i, :], rows[:, ROW_B, :], ALU.add)
                if done:
                    w.then_inc(sem(done), 1)
            if not done:
                step(v, w)

        ROW_LOADS = [32, 16]

        def dve_router(v):
            dve_layer_norm(v, xres, xres, "x1")
            dve_affine(v)
            dve_layer_norm(v, xres, xn2, "xn2", "xn2_done")
            step(v, v.tensor_copy(token[:, :], const("token")))
            step(v, v.memset(g8, NEG))
            v.wait_ge(sem("router_in"), 64)
            t = filled(v, "logits")
            free_bank("logits", v.tensor_tensor(lg, t[:, 0:NT * 36].rearrange("p (i n) -> p i n", i=NT), grow(rbias, NT, 1), ALU.add))
            emptied(v, "logits")
            step(v, v.tensor_copy(g8[:, :, 0:EXP_GROUPS], lg[:, :, 0:EXP_GROUPS]))
            for i in range(NT):
                w = v.max(gtop[:, i, :], g8[:, i, :])
            step(v, w)
            for i in range(NT):
                w = v.max_index(gat[:, i, :], gtop[:, i, :], g8[:, i, :])
            step(v, w)
            v.tensor_tensor(gexp, lg[:, :, 0:EXP_GROUPS], gtop[:, :, 0:1].to_broadcast([P, NT, EXP_GROUPS]),
                            ALU.subtract).then_inc(sem("group_logits"), 1)
            step(v, v.tensor_copy(idxf[:, :, 0:1], gat[:, :, 0:1]))
            step(v, v.tensor_tensor(gone, grow(const("iota")[:, 0:EXP_GROUPS], NT, 1),
                                    idxf[:, :, 0:1].to_broadcast([P, NT, EXP_GROUPS]), ALU.is_equal))
            m4 = masked.rearrange("p i (g e) -> p (i g) e", g=EXP_GROUPS)
            t4 = tmp32.rearrange("p i (g e) -> p (i g) e", g=EXP_GROUPS)
            gf = gone.rearrange("p i g -> p (i g)")
            step(v, v.tensor_scalar(t4, grow(gf, EPG), -NEG, NEG, ALU.mult, ALU.add))
            step(v, v.tensor_copy(masked, lg[:, :, EXP_GROUPS:36]))
            step(v, v.tensor_tensor(m4, m4, grow(gf, EPG), ALU.mult))
            step(v, v.tensor_tensor(masked, masked, tmp32, ALU.add))
            for i in range(NT):
                w = v.max(etop[:, i, :], masked[:, i, :])
            step(v, w)
            for i in range(NT):
                w = v.max_index(eat[:, i, :], etop[:, i, :], masked[:, i, :])
            step(v, w)
            v.tensor_tensor(emax2.unsqueeze(2), etop[:, :, 1:2], etop[:, :, 0:1], ALU.subtract).then_inc(sem("second_logit"), 1)
            step(v, v.tensor_copy(idxf[:, :, 1:3], eat[:, :, 0:2]))
            iota = grow(const("iota"), NT, 1)
            v.tensor_tensor(hot0, iota, idxf[:, :, 1:2].to_broadcast([P, NT, NEXP]), ALU.is_equal)
            step(v, v.tensor_tensor(hot1, iota, idxf[:, :, 2:3].to_broadcast([P, NT, NEXP]), ALU.is_equal))
            v.tensor_tensor(both, hot0, hot1, ALU.add).then_inc(sem("chosen"), 1)
            v.wait_ge(sem("group_exp"), 1)
            step(v, v.tensor_reduce(gsum, gexp, AX.X, ALU.add))
            v.wait_ge(sem("second_exp"), 1)
            step(v, v.tensor_scalar(st[:, 60:64], emax2, 1.0, None, ALU.add))
            step(v, v.tensor_tensor(st[:, 60:64], st[:, 60:64], gsum, ALU.mult))
            step(v, v.reciprocal(comb[:, :, 0], st[:, 60:64]))
            step(v, v.tensor_tensor(comb[:, :, 1], comb[:, :, 0], emax2, ALU.mult))
            t = filled(v, "rank")
            v.tensor_copy(rank, t[:, 0:NT * NEXP].rearrange("p (i n) -> p i n", i=NT))
            free_bank("rank", v.tensor_copy(counts, t[:, NT * NEXP:(NT + 1) * NEXP]))
            emptied(v, "rank")
            step(v, v.tensor_tensor(cmp7, grow(counts, 7), grow(const("full"), NEXP, 1), ALU.is_gt))
            step(v, v.tensor_reduce(blocks_of, cmp7, AX.X, ALU.add))
            step(v, v.tensor_tensor_scan(block_end, ones[:, 0:NEXP], blocks_of, 0.0, ALU.mult, ALU.add))
            step(v, v.tensor_tensor(tmp1, block_end, blocks_of, ALU.subtract))
            step(v, v.tensor_scalar(over0, tmp1, float(CAP), float(MAIN - CAP), ALU.mult, ALU.add))
            step(v, v.tensor_tensor(over0, over0, const("slot0"), ALU.subtract))
            step(v, v.tensor_scalar(place, rank, float(CAP), None, ALU.is_ge))
            step(v, v.tensor_tensor(place, place, grow(over0, NT, 1), ALU.mult))
            step(v, v.tensor_tensor(place, place, rank, ALU.add))
            step(v, v.tensor_tensor(place, place, grow(const("slot0"), NT, 1), ALU.add))
            v.tensor_tensor(hot0, hot0, place, ALU.mult)
            step(v, v.tensor_tensor(hot1, hot1, place, ALU.mult))
            v.tensor_reduce(slotf[:, :, 0], hot0, AX.X, ALU.add)
            step(v, v.tensor_reduce(slotf[:, :, 1], hot1, AX.X, ALU.add))
            v.tensor_copy(dest[:, :, :], slotf).then_inc(sem("dest_ready"), 1)
            step(v, v.tensor_tensor(cmp16, grow(block_end, 15, 1), grow(const("block")[:, 0:15], NEXP), ALU.is_le))
            step(v, v.tensor_reduce(overf[:, 0:15], cmp16, AX.X, ALU.add))
            step(v, v.tensor_scalar(overf[:, 0:15], overf[:, 0:15], float(NEXP - 1), None, ALU.min))
            step(v, v.tensor_copy(overf[:, 15:16], block_end[:, NEXP - 1:NEXP]))
            v.tensor_copy(over[:, :], overf).then_inc(sem("over_known"), 1)
            v.wait_ge(sem("slots_in"), 16)
            v.tensor_copy(tabf[0:SLOTS // P, :], tabi[0:SLOTS // P, :]).then_inc(sem("slots_float"), 1)
            t = filled(v, "slots")
            free_bank("slots", v.tensor_copy(slot_token[:, :], t[:, 0:SLOTS // P]))
            emptied(v, "slots")
            v.memset(st[:, 89:90], 0.0).then_inc(sem("slots_back"), 1)

        def dve_experts(v):
            base = fills_before_moe

            def gated(p, x, n):
                v.wait_ge(sem("moe_silu"), p * 2 + (x + 1))
                v.wait_ge(full[2 + x], p + (base[2 + x] + 1))
                v.tensor_tensor(hx[0:CAP, x, :], sg[0:CAP, x, :], ps[CAP:2 * CAP, 2 + x, :], ALU.mult).then_inc(empty[2 + x], 1)
                v.wait_ge(full[4 + x], p + (base[4 + x] + 1))
                v.tensor_copy(aT[:, x, :, :].rearrange("p k n -> p (k n)"), ps[:, 4 + x, 0:4 * CAP]).then_inc(empty[4 + x], 1)

            with v.Fori(0, NEXP // 2) as p:
                gated(p, 0, None)
                gated(p, 1, None)
            n = v.value_load(over[0:1, 15:16], min_val=0, max_val=OVB)
            with v.If(n > 0):
                with v.Fori(0, n) as b:
                    v.wait_ge(sem("ov_s"), b + 1)
                    v.tensor_tensor(hx[0:CAP, 0, :], sg[0:CAP, 0, :], ps[CAP:2 * CAP, 2, :], ALU.mult).then_inc(sem("ov_a"), 1)
                    v.wait_ge(sem("ov_at"), b + 1)
                    v.tensor_copy(aT[:, 0, :, :].rearrange("p k n -> p (k n)"), ps[:, 4, 0:4 * CAP]).then_inc(sem("ov_ate"), 1)
            v.wait_ge(sem("ov_done"), 1)

        def dve_combine(v):
            v.wait_ge(sem("y_gathered"), 16 * 2 * NT)
            for i in range(NT):
                y = yg[:, i, 0, :]
                step(v, v.tensor_scalar(y, y, comb[:, i, 0:1], None, ALU.mult))
                step(v, v.scalar_tensor_tensor(y, yg[:, i, 1, :], comb[:, i, 1:2], y, ALU.mult, ALU.add))
                step(v, v.tensor_tensor(y, y, rows[:, ROW_G2, :], ALU.mult))
                w = v.scalar_tensor_tensor(xres[:, i, :], xres[:, i, :], ALPHA, y, ALU.mult, ALU.add)
            step(v, w)
            dve_layer_norm(v, xres, xres, "x2")
            ROW_LOADS[:] = [48, 32]
            dve_affine(v, "x2_ready")

        def dve_rms(v, name, dst, done):
            v.wait_ge(sem(name + "_rms"), 1)
            step(v, v.reciprocal(st[:, 84:88], st[:, 84:88]))
            for i in range(NT):
                v.tensor_scalar(dst[:, i, :], xres[:, i, :], st[:, 84 + i:85 + i], None, ALU.mult).then_inc(sem(done), 1)

        def dve_residual(v, kind, y, row, name, done):
            for i in range(NT):
                for c in range(2):
                    t = filled(v, (kind, c, i))
                    free_bank((kind, c, i), v.tensor_copy(y[:, i, c * 512:(c + 1) * 512], t))
                for c in range(2):
                    emptied(v, (kind, c, i))
                v.memset(st[:, 88:89], 0.0).then_inc(sem(name + "_ready"), 1)
            v.wait_ge(sem(name + "_rms"), 1)
            step(v, v.reciprocal(st[:, 84:88], st[:, 84:88]))
            for i in range(NT):
                step(v, v.scalar_tensor_tensor(y[:, i, :], y[:, i, :], st[:, 84 + i:85 + i], rows[:, row, :], ALU.mult, ALU.mult))
                v.tensor_tensor(xres[:, i, :], xres[:, i, :], y[:, i, :], ALU.add).then_inc(sem(done), 1)

        def dve_low_part(v, name, sc, sh):
            for k in range(KD + 1):
                if k < KD:
                    t = filled(v, (name, k))
                    free_bank((name, k), v.tensor_scalar(h_low[:, k, :], t, mod[:, sc, k:k + 1], mod[:, sh, k:k + 1],
                                                         ALU.mult, ALU.add))
                if k:
                    low = h_low[:, k - 1, :]
                    v.wait_ge(sem(name + "_rounded"), k)
                    v.tensor_tensor(single(low), low, as_float(hT[:, k - 1, :]), ALU.subtract).then_inc(sem(name + "_split"), 1)

        def dve_sb(v):
            dve_rms(v, "x2n", xn3, "xn3_done")
            dve_low_part(v, "h3", SCM, SHM)
            for which in range(3):
                dve_rest(v, ("sb", 0), which)

            def keys(j):
                t = filled(v, ("sk", j))
                free_bank(("sk", j), v.tensor_copy(zk[:, j % 2, :], t))

            def values(j):
                t = filled(v, ("sv", j))
                free_bank(("sv", j), v.tensor_copy(zv[:, j % 2, :, :].rearrange("p i n -> p (i n)"), t))

            def mask(u):
                i = ZU[u][2]
                t = filled(v, ("z", u))
                t = t[:, i * P:(i + 1) * P]
                v.tensor_tensor(t, t, const("sbmask"), ALU.add).then_inc(sem("sb_masked"), 1)

            for n in range(1, NT + 1):
                for a in range(3):
                    w = v.memset(zR[:, a, n * P:n * P + 1], 1.0)
            step(v, w)
            keys(0)
            values(0)
            mask(0)
            mask(1)
            for u, (j, hh, i) in enumerate(ZU):
                if u % 8 == 5 and j + 1 < KD:
                    keys(j + 1)
                if u % 8 == 6 and j + 1 < KD:
                    values(j + 1)
                n = P * (i + 1)
                emptied(v, ("z", u))
                if u >= 3:
                    v.wait_ge(sem("sb_weights"), u - 2)
                step(v, v.memset(zR[:, u % 3, n:n + 1], 1.0))
                v.tensor_tensor_scan(zR[:, u % 3, 0:n][:, ::-1], zU[:, u % 3, 0:n][:, ::-1], const("zeros")[:, 0:n], 1.0,
                                     ALU.mult, ALU.add).then_inc(sem("sb_scan"), 1)
                if u + 2 < len(ZU):
                    mask(u + 2)
                if 0 < u % 8 < 4 and j + 1 < KD:
                    dve_rest(v, ("sb", j + 1), u % 8 - 1)
            dve_output_split(v, "wo", sT, sT_high)
            for j in range(4):
                dve_rest(v, ("wo", 1), j)
            dve_residual(v, "wo", yb, ROW_GM, "y1", "x3_ready")

        def dve_ffn(v):
            dve_rms(v, "x3n", xn3, "xn4_done")
            dve_low_part(v, "h4", SCF, SHF)
            for f in range(2):
                ffn_pieces(f, lambda chunk, j: dve_rest(v, chunk, j))
            for f in range(FT):
                emptied(v, ("fgu", 0, f))
                t = filled(v, ("fgu", 1, f))
                free_bank(("fgu", 1, f), v.tensor_tensor(ff[:, f, :], fS[:, f % 4, :], t, ALU.mult))
                ffn_pieces(f + 2, lambda chunk, j: dve_rest(v, chunk, j))

            def hidden(f):
                v.wait_ge(sem("ff_rounded"), f + 1)
                v.tensor_tensor(single(ff[:, f, :]), ff[:, f, :], as_float(ffh[:, f % 4, :]), ALU.subtract).then_inc(sem("ff_split"), 1)

            for f in range(4):
                hidden(f)
            for f in range(FT - 4):
                dve_rest(v, ("fo", (f + 4) // 4), f % 4)
                hidden(f + 4)
            dve_residual(v, "fo", hT4, ROW_GF, "y2", "out_ready")

        dve_stages = [dve_start, dve_kv, dve_attention, dve_hgrn, dve_merge, dve_router, dve_experts, dve_combine, dve_sb, dve_ffn]

        @block.vector
        def _(v):
            for stage in dve_stages:
                stage(v)


_OUT = (1, T, D)


def kernel(**inputs):
    import concourse.bacc as bacc
    from concourse.bass_utils import run_bass_kernel_spmd

    nc = bacc.Bacc("TRN2", target_bir_lowering=False, num_devices=1)
    arrays, io = {}, {}
    given = {k: v for k, v in inputs.items() if v.size and not k.startswith(("sg_", "sc_", "cb_"))}
    for name, a in {**given, **shape_constants()}.items():
        a = np.ascontiguousarray(a)
        arrays[f"in_{name}"] = a
        io[name] = nc.dram_tensor(f"in_{name}", a.shape, mybir.dt.from_np(a.dtype), kind="ExternalInput").ap()
    out = nc.dram_tensor("out", _OUT, mybir.dt.float32, kind="ExternalOutput").ap()
    block_kernel(nc, io, out)
    return run_bass_kernel_spmd(nc, [arrays], core_ids=[0]).results[0]["out"]
```

```python
import math
from contextlib import ExitStack

import numpy as np
import concourse.bass as bass
from concourse import mybir

P = 128
T = 512
D = 1024
NT = T // P
KD = D // P
HEADS = 8
GROUPS = 2
REP = HEADS // GROUPS
CHUNK = 32
NCHUNK = T // CHUNK
CPT = P // CHUNK
CMP = 32
STRIDE = 16
NCMP = T // STRIDE - CMP // STRIDE + 1
BUCKETS = 32
MAX_DIST = 128
NEXP = 32
EXP_GROUPS = 4
EPG = NEXP // EXP_GROUPS
DE = 512
CAP = 64
OVB = (2 * T - 1) // CAP
MAIN = NEXP * CAP
SLOTS = 24 * P
SB_HEADS = 16
DFF = 2816
FT = DFF // P
ALPHA = 2 ** 0.25
NEG = -1e30
SCALE = P ** -0.5
SB_SCALE = 64 ** -0.5
Q_H, F_H, I_H, G_H, Q_N, KV_N, GATE_N = 0, 1024, 2048, 3072, 4096, 5120, 6656
MG_H = GATE_N + 3 * HEADS
MG_N = MG_H + D
REL = 2 * T - 1

_at, _c = {}, 0
for _name, _n in (("ident", P), ("ones", P), ("before", P), ("sbmask", P), ("chunk", CPT), ("reset", T),
                  ("zeros", T), ("attmask", P), ("iota", NEXP), ("slot0", NEXP), ("token", NT),
                  ("full", 7), ("block", 16)):
    _at[_name] = (_c, _n)
    _c += _n
NCONST = _c


def shape_constants():
    p = np.arange(P)
    c = np.zeros((P, NCONST), np.float32)

    def put(name, value):
        a, n = _at[name]
        c[:, a:a + n] = value

    put("ident", np.eye(P))
    put("ones", 1.0)
    put("before", p[:, None] < p[None, :])
    put("sbmask", np.where(p[None, :] < p[:, None], 0.0, NEG))
    put("chunk", p[:, None] // CHUNK == np.arange(CPT)[None])
    put("reset", (np.arange(T) % CHUNK != 0)[None])
    put("attmask", (p[:, None] // CHUNK == p[None] // CHUNK) & (p[:, None] <= p[None]))
    put("iota", np.arange(NEXP)[None])
    put("slot0", CAP * np.arange(NEXP)[None])
    put("token", p[:, None] + P * np.arange(NT)[None])
    put("full", CAP * np.arange(1, 8)[None])
    put("block", np.arange(16)[None])
    dist = np.arange(REL) - (T - 1)
    n = np.maximum(dist, 0)
    nf = np.maximum(n, 1).astype(np.float32)
    half = BUCKETS // 2
    large = half + (np.log(nf / half) / math.log(MAX_DIST / half) * (BUCKETS - half)).astype(np.int32)
    bucket = np.where(n < half, n, np.minimum(large, BUCKETS - 1))
    bucket = np.where(dist < 0, BUCKETS, bucket)
    hot = np.zeros((BUCKETS + 1, REL + 1), np.float32)
    hot[bucket, np.arange(REL)] = 1.0
    return {"shape_const": c, "rel_hot": hot, "neg_row": np.full((1, HEADS), NEG, np.float32),
            "no_token": np.zeros((SLOTS, 1), np.int32)}


def block_kernel(nc, io, out):
    f32, f32r, i32, u32 = mybir.dt.float32, mybir.dt.float32r, mybir.dt.int32, mybir.dt.uint32
    ACT, ALU, AX = mybir.ActivationFunctionType, mybir.AluOpType, mybir.AxisListType
    ctx = ExitStack()
    with ctx:
        rounded = {}

        def sb(name, shape, dt=f32):
            return ctx.enter_context(nc.sbuf_tensor(name, shape, dt))

        def sb_both(name, shape):
            t = sb(name, shape)
            size = 4 * int(np.prod(shape[1:]))
            rounded[name] = nc.alloc_sbuf_tensor_at(name + "_rounded", shape, f32r, offset=nc.sbuf_base - size)
            return t

        sems = {}

        def sem(name):
            if name not in sems:
                sems[name] = ctx.enter_context(nc.semaphore(name))
            return sems[name]

        NS = 3
        ring = sb_both("ring", [P, NS + 1, 4096])
        xres = sb("xres", [P, NT, D])
        hT = sb_both("hT", [P, KD, T])
        brn = sb_both("brn", [P, 2, 4096])
        scr = sb_both("scr", [P, FT * T])
        rows = sb_both("rows", [P, 6, D])
        cst = sb("cst", [P, NCONST])
        vec = sb("vec", [P, 3, P])
        mod = sb("mod", [P, 12, KD])
        csil = sb("csil", [P, 2 * KD])
        colb = sb("colb", [P, 40])
        st = sb("st", [P, 96])
        bnb = sb("bnb", [P, NT, 2, 6])
        mv = sb("mv", [P, NT, 2])
        comb = sb("comb", [P, NT, 2])
        dest = sb("dest", [P, NT, 2], i32)
        token = sb("token", [P, NT], i32)
        slot_token = sb("slot_token", [P, SLOTS // P], i32)
        over = sb("over", [P, 16], i32)
        over_token = sb("over_token", [CAP, 1], i32)
        ps = ctx.enter_context(nc.psum_tensor("ps", [P, 8, 512], f32))
        rel_dram = nc.dram_tensor("rel_scratch", (HEADS, REL + 1), f32).ap()
        xn_dram = nc.dram_tensor("xn_scratch", (T, D), f32).ap()
        slot_dram = nc.dram_tensor("slot_scratch", (SLOTS, 1), i32).ap()
        y_dram = nc.dram_tensor("y_scratch", (SLOTS, D), f32).ap()

        def const(name):
            a, n = _at[name]
            return cst[:, a:a + n]

        def grow(ap, n, at=2):
            ap = ap.unsqueeze(at)
            shape = list(ap.shape)
            shape[at] = n
            return ap.to_broadcast(shape)

        ident, ones = const("ident"), const("ones")
        oH = brn[:, 0, :].rearrange("p (k t) -> p k t", k=KD)
        oN = brn[:, 1, :].rearrange("p (k t) -> p k t", k=KD)
        SH1, SC1, G1, SH2, SC2, G2, SHM, SCM, GM, SHF, SCF, GF = range(12)
        ROW_G1, ROW_G2, ROW_GM, ROW_GF, ROW_A, ROW_B = range(6)

        full = [sem(f"bank{b}_full") for b in range(8)]
        empty = [sem(f"bank{b}_empty") for b in range(8)]
        fills = [0] * 8
        filling = {}

        def open_bank(pe, b, name):
            if fills[b]:
                pe.wait_ge(empty[b], fills[b])
            fills[b] += 1
            filling[name] = (b, fills[b])
            return ps[:, b, :]

        def close_bank(name, instruction):
            instruction.then_inc(full[filling[name][0]], 1)

        def filled(eng, name):
            b, n = filling[name]
            eng.wait_ge(full[b], n)
            return ps[:, b, :]

        def emptied(eng, name):
            b, n = filling[name]
            eng.wait_ge(empty[b], n)

        def free_bank(name, instruction):
            instruction.then_inc(empty[filling[name][0]], 1)

        arrived_sem = [sem(f"chunk_slot{s}_full") for s in range(NS)]
        chunk_no = {}
        used_by = {}

        chunk_list = []

        def plan(name, parts):
            chunk_no[name] = len(chunk_list)
            chunk_list.append((name, parts))

        def slot_of(name):
            return ring[:, chunk_no[name] % NS, :]

        arrived_at = {}

        def arrived(pe, name):
            n = chunk_no[name]
            pe.wait_ge(arrived_sem[n % NS], arrived_at[name])
            return slot_of(name)

        def last_use(name, fill):
            used_by[chunk_no[name]] = fill

        NPIECE = 4
        piece_no = {}
        piece_used = {}

        def single(ap):
            whole = rounded[ap.tensor.name]
            return bass.AP(tensor=whole[:, 0:1].tensor, offset=ap.offset, ap=ap.ap)

        def as_float(ap):
            return single(ap).bitcast(f32)

        def piece_high(q):
            return ring[:, NS, (q % NPIECE) * 1024:(q % NPIECE + 1) * 1024]

        def piece_low(chunk, j):
            return slot_of(chunk)[:, j * 1024:(j + 1) * 1024]

        def pe_piece(pe, chunk, j):
            q = piece_no[chunk, j] = len(piece_no)
            pe.wait_ge(sem("piece_split"), q + 1)
            return single(piece_high(q)), single(piece_low(chunk, j))

        def used(eng, entry):
            if entry[0] == "pieces":
                eng.wait_ge(sem("pieces_used"), entry[1])
            else:
                filled(eng, entry)

        counted_pieces = [0]

        def count_piece(chunk, j, instruction):
            instruction.then_inc(sem("pieces_used"), 1)
            counted_pieces[0] += 1
            piece_used[piece_no[chunk, j]] = ("pieces", counted_pieces[0])

        def act_round(a, chunk, j):
            q = piece_no[chunk, j]
            arrived(a, chunk)
            if q >= NPIECE:
                used(a, piece_used[q - NPIECE])
            a.activation(single(piece_high(q)), piece_low(chunk, j), ACT.Copy).then_inc(sem("piece_rounded"), 1)

        def dve_rest(v, chunk, j):
            v.wait_ge(sem("piece_rounded"), piece_no[chunk, j] + 1)
            low = piece_low(chunk, j)
            v.tensor_tensor(single(low), low, as_float(piece_high(piece_no[chunk, j])), ALU.subtract).then_inc(sem("piece_split"), 1)

        def triple(pe, dst, lhs, rhs, start, stop):
            pe.matmul(dst, lhs[0], rhs[0], start=start, stop=False)
            pe.matmul(dst, lhs[0], rhs[1], start=False, stop=False)
            return pe.matmul(dst, lhs[1], rhs[0], start=False, stop=stop)

        def cols(w, a, n):
            return w[0, :, a:a + n].rearrange("(k p) n -> p k n", p=P)

        def plan_wide(name, w, a):
            plan(name, [(lambda s: s.rearrange("p (k n) -> p k n", k=KD), cols(w, a, 512))])

        def plan_quad(name, quad):
            plan(name, [((lambda s, j=j: s[:, j * 1024:(j + 1) * 1024].rearrange("p (k n) -> p k n", k=KD)),
                         cols(w, a, P)) for j, (w, a) in enumerate(quad)])

        def wide(s):
            return s.rearrange("p (k n) -> p k n", k=KD)

        def quad(s, j):
            return s[:, j * 1024:(j + 1) * 1024].rearrange("p (k n) -> p k n", k=KD)

        A = io
        ada_todo = [(1, c) for c in (4, 5, 6, 7, 8, 9, 10, 11)] + [(2, c) for c in range(12)]
        ada_at = {("attn", h): ada_todo[h] for h in range(8)}
        for h in range(8):
            ada_at[("hg", h)] = ada_todo[8 + h]
        for j in range(4):
            ada_at[("merge", j)] = ada_todo[16 + j]

        def plan_ada(m, c):
            plan_wide(("ada", m, c), A["ada_w"] if m == 1 else A["ada_w_2"], 512 * c)

        for c in range(4):
            plan_ada(1, c)
        for c in range(3):
            plan_quad(("kv", c), [(A["w_in"], KV_N + 512 * c + P * j) for j in range(4)])
        for kv in ("k", "v"):
            plan(("cmp", kv), [(lambda s: s.rearrange("p (t n) -> p t n", t=CMP),
                                A[f"cmp_w1_{kv}"][0].rearrange("(t p) n -> p t n", p=P))])
        for h in range(8):
            if h in (0, 1, 3, 5):
                j = (h + 1) // 2
                plan_quad(("nq", j), [(A["w_in"], Q_N + 256 * j + P * x) for x in range(2)])
            plan_ada(*ada_at[("attn", h)])

        def plan_head(h):
            w = A["w_in"]
            plan_quad(("hg", h), [(w, Q_H + P * h), (w, F_H + P * h), (w, G_H + P * h), (w, I_H + P * h)])

        plan_head(0)
        for h in range(8):
            if h < 7:
                plan_head(h + 1)
            plan_ada(*ada_at[("hg", h)])
        for j in range(8):
            plan_quad(("merge", j), [(A["w_in"], MG_H + P * j), (A["w_in"], MG_N + P * j),
                                     (A["w_br_hg"], P * j), (A["w_br_nsa"], P * j)])
            if j < 4:
                plan_ada(*ada_at[("merge", j)])
        for c in range(2):
            plan_wide(("wout", c), A["w_out"], 512 * c)
        AFTER_MOE = len(chunk_list)
        for j in range(KD):
            w = A["sb_w_qkv_2"]
            plan_quad(("sb", j), [(w, P * j), (w, D + P * j), (w, 2 * D + P * j)])
        for c in range(2):
            plan_wide(("wo", c), A["sb_w_o_2"], 512 * c)
        for c in range(FT // 2):
            w = A["ffn_w_in_2"]
            plan_quad(("fi", c), [(w, m * DFF + (2 * c + x) * P) for x in range(2) for m in range(2)])
        for c in range(-(-FT // 4)):
            n = min(4, FT - 4 * c)
            plan(("fo", c), [((lambda s, n=n: s[:, 0:n * D].rearrange("p (k n) -> p k n", k=n)),
                              A["ffn_w_out_2"][0, 4 * P * c:4 * P * c + n * P, :].rearrange("(k p) n -> p k n", p=P))])
        count = [0] * NS
        for name, parts in chunk_list:
            s = chunk_no[name] % NS
            count[s] += 16 * len(parts)
            arrived_at[name] = count[s]

        class Cut:

            def __init__(self, base=0):
                self.at = base

            def __call__(self, n):
                a, self.at = self.at, self.at + n
                assert self.at <= FT * T, self.at
                return scr[:, a:a + n]

        cut = Cut()
        bias_back = cut(HEADS * T).rearrange("p (h j) -> p h j", h=HEADS)
        biasT = bias_back[:, :, ::-1]
        cbias = cut(HEADS * NT * NCMP).rearrange("p (h i n) -> p h i n", h=HEADS, i=NT)
        cmask = cut(NT * NCMP).rearrange("p (i n) -> p i n", i=NT)
        gates = sb("gates", [P, NT, 24])[:, :, :]
        kcmpT = sb("kcmpT", [P, GROUPS * NCMP])[:, :]
        vcmp = cut(GROUPS * P).rearrange("p (g n) -> p g n", g=GROUPS)
        w2cmp = cut(2 * P).rearrange("p (a n) -> p a n", a=2)
        attn_base = cut.at
        qT = cut(2 * T).rearrange("p (a n) -> p a n", a=2)
        SW = 2 * T + 32
        prob = cut(2 * SW).rearrange("p (a n) -> p a n", a=2)
        probT = cut(2 * 9 * P).rearrange("p (a k n) -> p a k n", a=2, k=9)
        dg = rows[:, 4, 0:6 * P].rearrange("p (a b n) -> p a b n", a=2, b=3)
        kfull = brn[:, 0, 0:2048].rearrange("p (a g t) -> p a g t", a=2, g=GROUPS)
        vfull = brn[:, 0, 2048:4096].rearrange("p (a i n) -> p a i n", a=2, i=NT)
        kvc = brn[:, 1, 0:2048].rearrange("p (a g t) -> p a g t", a=2, g=GROUPS)
        cut2 = Cut(attn_base)
        blocks = cut2(CMP * GROUPS * NCMP).rearrange("p (t g n) -> p t g n", t=CMP, g=GROUPS)
        hid = cut2(2 * GROUPS * NCMP).rearrange("p (a n) -> p a n", a=2)
        hsig = cut2(2 * GROUPS * NCMP).rearrange("p (a n) -> p a n", a=2)
        wgate = rows[:, 4, 6 * P:6 * P + KD * 24].rearrange("p (k n) -> p k n", k=KD)
        vtmp = cut2(2 * T).rearrange("p (a n) -> p a n", a=2)
        gbias = cut2(1)[0:24, :]
        wgate_high = cut2(KD * 24).rearrange("p (k n) -> p k n", k=KD)
        gT = cut2(T)[0:24, :]
        tab = sb("tab", [P, HEADS])
        xn = scr[:, attn_base:attn_base + NT * D].rearrange("p (i n) -> p i n", i=NT)
        hot = hT[0:BUCKETS + 1, 0:2, :].rearrange("p a n -> p (a n)")
        relrow = hT[0:HEADS, 2:4, :].rearrange("p a n -> p (a n)")
        packs = rows[:, 0:1, 0:3 * P].rearrange("p a (b n) -> p (a b) n", b=3)

        h1_high = rows[:, 0:4, :].rearrange("p a n -> p (a n)").rearrange("p (k t) -> p k t", k=KD)
        b0T = oH

        block = ctx.enter_context(nc.Block())

        c_col = lambda k: vec[:, 0, k:k + 1]
        ADAB1 = 16
        POSK, POSV = 64, 96
        BIN, BMG, ADAB2, HGN, B1 = 0, 52, 68, 116, 124

        def bin_col(a):
            j = a // P if a < GATE_N else BMG + (a - MG_H) // P
            return vec[:, 1, j:j + 1]

        def gemm(pe, dst, lhs, rhs, n=KD, start=True):
            for k in range(n):
                last = pe.matmul(dst, lhs(k), rhs(k), start=start and k == 0, stop=k == n - 1)
            return last

        def pe_ada(pe, m, c, bank):
            name = ("ada", m, c)
            if m == 1 and c < 4:
                pe.wait_ge(sem("start_ada_added"), 3 * (c + 1))
            else:
                pe.wait_ge(sem("ada_added"), 4 * (list(ada_at.values()).index((m, c)) + 1))
            acc = slot_of(name)[:, 0:512]
            dst = open_bank(pe, bank, name)
            for j in range(4):
                last = pe.matmul(dst[:, j:j + 1], acc[:, j * P:(j + 1) * P], ones[:, 0:1], start=True, stop=True)
            close_bank(name, last)
            last_use(name, name)

        def pe_start(pe):
            pe.wait_ge(sem("const_in"), 16)
            pe.wait_ge(sem("packs_in"), 16 * N_PACK)
            t = open_bank(pe, 7, "vec")
            for b, n in ((0, P), (1, 126), (2, 48)):
                last = pe.transpose(t[:, b * P:b * P + n], packs[0:n, b, :], ident[0:n, 0:n])
            close_bank("vec", last)
            pe.wait_ge(sem("rel_in"), 48)
            for c in range(2):
                t = open_bank(pe, 5 + c, ("rel", c))
                close_bank(("rel", c), pe.matmul(t[0:HEADS, :], tab[0:BUCKETS + 1, :],
                                                 hot[:, c * 512:(c + 1) * 512], start=True, stop=True))
            t = open_bank(pe, 4, "cbias")
            distances = (NT - 1) * P // STRIDE + NCMP
            for c in range(4):
                for m in range(distances * c // 4, distances * (c + 1) // 4):
                    y = T - CMP - STRIDE * (NCMP - 1) + STRIDE * m
                    last = pe.matmul(t[:, m * HEADS:(m + 1) * HEADS], hot[:, y:y + P], tab[0:BUCKETS + 1, :], start=True, stop=True)
                if c == 3:
                    close_bank("cbias", last)
                pe_ada(pe, 1, c, c % 2)
            pe.wait_ge(sem("ln_done"), 4)
            pe_transposes(pe, "h1", xn)

        def pe_transposes(pe, name, src):
            for k in range(KD):
                t = open_bank(pe, 2 + k % 4, (name, k))
                for i in range(NT):
                    last = pe.transpose(t[:, i * P:(i + 1) * P], src[:, i, k * P:(k + 1) * P], ident)
                close_bank((name, k), last)

        def feature_major(pe, bank, name, w, src=None):
            t = open_bank(pe, bank, name)
            close_bank(name, gemm(pe, t, w, lambda k: (src if src is not None else hT)[:, k, :]))

        parts = {}

        def feature_major3(pe, bank, name, chunk, j, high, low, halves=(0, 1)):
            if 0 in halves:
                parts[name] = [quad(x, 0) for x in pe_piece(pe, chunk, j)]
                open_bank(pe, bank, name)
            wh, wl = parts[name]
            for k in range(4 * halves[0], 4 * halves[-1] + 4):
                last = triple(pe, ps[:, bank, :], (wh[:, k, :], wl[:, k, :]), (single(high[:, k, :]), single(low[:, k, :])),
                              k == 0, k == KD - 1)
            if 1 in halves:
                close_bank(name, last)
                piece_used[piece_no[chunk, j]] = name

        def transpose_512(pe, bank, name, src):
            t = open_bank(pe, bank, name)
            for i in range(NT):
                last = pe.transpose(t[:, i * P:(i + 1) * P], src[:, i * P:(i + 1) * P], ident)
            close_bank(name, last)

        def pe_kv(pe):
            for k in range(KD):
                emptied(pe, ("h1", k))
            pe.wait_ge(sem("h1_split"), KD)
            for c in range(3):
                for j in range(4):
                    feature_major3(pe, j, ("kvT", c, j), ("kv", c), j, h1_high, hT)
                last_use(("kv", c), ("kvT", c, 3))
                if c:
                    for g in range(GROUPS):
                        emptied(pe, ("kvT", c, 2 + g))
                        transpose_512(pe, 4 + g, ("vtok", c, g), vtmp[:, g, :])
            pe.wait_ge(sem("wgate_split"), 1)
            t = open_bank(pe, 6, "gate")
            for k in range(KD):
                last = triple(pe, t[0:24, :], (single(wgate_high[:, k, :]), single(wgate[:, k, :])),
                              (single(h1_high[:, k, :]), single(hT[:, k, :])), k == 0, k == KD - 1)
            close_bank("gate", last)
            emptied(pe, "gate")
            t = open_bank(pe, 6, "gateT")
            for i in range(NT):
                last = pe.transpose(t[:, i * 24:(i + 1) * 24], gT[:, i * P:(i + 1) * P], ident[0:24, 0:24])
            close_bank("gateT", last)
            pe.wait_ge(sem("small_in"), 16 * N_SMALL)
            for a, kv in enumerate("kv"):
                s = arrived(pe, ("cmp", kv)).rearrange("p (t n) -> p t n", t=CMP)
                pe.wait_ge(sem("blocks_ready"), 4 * (a + 1))
                name = ("hid", kv)
                t = open_bank(pe, 7, name)
                last = gemm(pe, t[:, 0:GROUPS * NCMP], lambda k: s[:, k, :],
                            lambda k: blocks[:, k, :, :].rearrange("p g n -> p (g n)"), n=CMP)
                close_bank(name, last)
                last_use(("cmp", kv), name)
            emptied(pe, ("hid", "v"))
            t = open_bank(pe, 0, "kcmp")
            close_bank("kcmp", pe.matmul(t[:, 0:GROUPS * NCMP], w2cmp[:, 0, :], hid[:, 0, :], start=True, stop=True))
            t = open_bank(pe, 1, "vcmp")
            for g in range(GROUPS):
                last = pe.matmul(t[0:NCMP, g * P:(g + 1) * P], hid[:, 1, g * NCMP:(g + 1) * NCMP],
                                 w2cmp[:, 1, :], start=True, stop=True)
            close_bank("vcmp", last)

        UNITS = [(h, i) for h in range(HEADS) for i in range(NT)]

        def pe_attention(pe):
            emptied(pe, "kcmp")
            emptied(pe, "vcmp")
            for c in (1, 2):
                for j in range(2):
                    emptied(pe, ("kvT", c, j))
                    emptied(pe, ("vtok", c, j))

            def query(h):
                feature_major3(pe, 7, ("nqT", h), ("nq", h // 2), h % 2, h1_high, hT)
                if h % 2:
                    last_use(("nq", h // 2), ("nqT", h))

            def scores(u):
                h, i = UNITS[u]
                if i == 0:
                    emptied(pe, ("nqT", h))
                n = P * (i + 1)
                for a in range(2):
                    name = ("S", a, u)
                    t = open_bank(pe, 2 * a + u % 2, name)
                    close_bank(name, pe.matmul(t[:, 0:n], qT[:, h % 2, i * P:(i + 1) * P], kfull[:, a, h // REP, 0:n],
                                               start=True, stop=True))

            def compressed(u):
                t = open_bank(pe, 4, ("C", u))
                if u < len(UNITS):
                    h, i = UNITS[u]
                    last = pe.matmul(t[:, 0:NCMP], qT[:, h % 2, i * P:(i + 1) * P],
                                     kcmpT[:, h // REP * NCMP:(h // REP + 1) * NCMP], start=True, stop=True)
                if u:
                    pe.wait_ge(sem("diag_ready"), u)
                    last = pe.matmul(t[0:NCMP, P:2 * P], prob[:, (u - 1) % 2, 2 * T:2 * T + NCMP], dg[:, (u - 1) % 2, 0, :],
                                     start=True, stop=True)
                close_bank(("C", u), last)

            def transposes(u):
                for a in range(2):
                    t = open_bank(pe, 5 + a, ("T", a, u))
                    for j in range(UNITS[u][1] + 1):
                        last = pe.matmul(t[:, j * P:(j + 1) * P], prob[:, u % 2, a * T + j * P:a * T + (j + 1) * P],
                                         dg[:, u % 2, 1 + a, :], start=True, stop=True)
                    close_bank(("T", a, u), last)

            query(0)
            for u in range(2):
                scores(u)
                compressed(u)
            transposes(0)
            for u, (h, i) in enumerate(UNITS):
                if i == 1 and h + 1 < HEADS:
                    query(h + 1)
                if i == 2:
                    pe_ada(pe, *ada_at[("attn", h)], 7)
                if u + 2 < len(UNITS):
                    scores(u + 2)
                if u + 1 < len(UNITS):
                    compressed(u + 2)
                    transposes(u + 1)
                t = open_bank(pe, 7, ("O", u))
                emptied(pe, ("C", u + 1))
                g = h // REP
                pe.matmul(t[:, 0:P], vcmp[0:NCMP, g, :], probT[0:NCMP, u % 2, 8, :], start=True, stop=False)
                for a in range(2):
                    emptied(pe, ("T", a, u))
                    for j in range(i + 1):
                        last = pe.matmul(t[:, 0:P], vfull[:, a, j, g * P:(g + 1) * P], probT[:, u % 2, 4 * a + j, :],
                                         start=False, stop=a == 1 and j == i)
                close_bank(("O", u), last)

        def state_ready(eng, h, n):
            i, c = (n - 1) // CPT, (n - 1) % CPT
            if c == CPT - 1 or n == NCHUNK - 1:
                emptied(eng, ("U", h, i))
            else:
                eng.wait_ge(sem("hg_state"), 11 * h + 3 * i + c + 1)

        def pe_hgrn(pe):
            def project(h, which, halves=(0, 1)):
                feature_major3(pe, which, (("hq", "hf", "hg", "hi")[which], h), ("hg", h), which, h1_high, hT, halves)
                if which == 3 and 1 in halves:
                    last_use(("hg", h), ("hi", h))

            def transpose_values(h):
                emptied(pe, ("hi", h))
                transpose_512(pe, 3, ("hiT", h), hVT[:, h % 2, :])

            for which in range(4):
                project(0, which)
            for h in range(HEADS):
                more = h + 1 < HEADS
                if more:
                    project(h + 1, 0)
                transpose_values(h)
                if more:
                    project(h + 1, 1)
                pe.wait_ge(sem("hg_kend"), h + 1)
                t = open_bank(pe, 4, ("kendT", h))
                for i in range(NT):
                    last = pe.transpose(t[:, i * P:(i + 1) * P], hKN[:, i * P:(i + 1) * P], ident)
                close_bank(("kendT", h), last)
                t = open_bank(pe, 5, ("att", h))
                for i in range(NT):
                    c = slice(i * P, (i + 1) * P)
                    last = pe.matmul(t[:, c], hKI[:, c], hQ[:, h % 2, c], start=True, stop=True)
                close_bank(("att", h), last)
                if more:
                    project(h + 1, 2)
                emptied(pe, ("hiT", h))
                for i in range(NT):
                    if i == 2 and more:
                        project(h + 1, 3, (0,))
                    if i < NT - 1:
                        pe.wait_ge(sem("hg_kblocks"), (NT - 1) * h + i + 1)
                    else:
                        emptied(pe, ("kendT", h))
                    t = open_bank(pe, 6 + i % 2, ("U", h, i))
                    for c in range(CPT):
                        last = pe.matmul(t[:, c * P:(c + 1) * P], hKX[:, i % 2, c, :], hV[:, h % 2, i, :],
                                         start=True, stop=True)
                    close_bank(("U", h, i), last)
                emptied(pe, ("att", h))
                t = open_bank(pe, 4, ("oT", h))
                for i in range(NT):
                    c = slice(i * P, (i + 1) * P)
                    last = pe.matmul(t[:, c], hV[:, h % 2, i, :], hAT[:, c], start=True, stop=False,
                                     skip_group_check=True)
                    for n in range(CPT * i, CPT * (i + 1)):
                        if n:
                            state_ready(pe, h, n)
                            last = pe.matmul(t[:, n * CHUNK:(n + 1) * CHUNK], hS[:, n, :],
                                             hQ[:, h % 2, n * CHUNK:(n + 1) * CHUNK], start=False,
                                             stop=n == CPT * (i + 1) - 1, skip_group_check=True)
                close_bank(("oT", h), last)
                if more:
                    project(h + 1, 3, (1,))
                pe_ada(pe, *ada_at[("hg", h)], 6)
                pe.wait_ge(sem("hg_square"), h + 1)
                t = open_bank(pe, 5, ("ss", h))
                close_bank(("ss", h), pe.matmul(t, ones, hT2[:, :], start=True, stop=True))

        def pe_merge(pe):
            for j in range(KD):
                b = 4 * (j % 2)
                c = ("merge", j)
                feature_major3(pe, b, ("mgh", j), c, 0, h1_high, hT)
                feature_major3(pe, b + 1, ("mgn", j), c, 1, h1_high, hT)
                s = arrived(pe, c)
                feature_major(pe, b + 3, ("mN", j), lambda k: quad(s, 3)[:, k, :], oN)
                if j == 0:
                    pe.wait_ge(sem("hg_out"), 2 * HEADS)
                feature_major(pe, b + 2, ("mH", j), lambda k: quad(s, 2)[:, k, :], oH)
                last_use(c, ("mH", j))
                if j < 4:
                    pe_ada(pe, *ada_at[("merge", j)], 7 - b)
            for c in range(2):
                out_projection(pe, "wout", c, mT_high, mT, ("wout_split", 1))
                if c == 0:
                    for x in range(8):
                        pe.wait_ge(sem("gate_diag"), x + 1)
                        t = open_bank(pe, 4 + x % 4, ("row", x))
                        close_bank(("row", x), pe.matmul(t, ones, mD[:, x % 2, :], start=True, stop=True))

        def out_projection(pe, kind, c, high, low, ready):
            t = {}
            for j in range(4):
                wh, wl = (x.rearrange("p (k n) -> p k n", k=2) for x in pe_piece(pe, (kind, c), j))
                for k in (2 * j, 2 * j + 1):
                    if c == 0:
                        pe.wait_ge(sem(ready[0]), ready[1] * (k + 1))
                    for i in range(NT):
                        if k == 0:
                            t[i] = open_bank(pe, 4 * c + i, (kind, c, i))
                        tok = slice(i * P, (i + 1) * P)
                        last = triple(pe, t[i], (single(high[:, k, tok]), single(low[:, k, tok])),
                                      (wh[:, k % 2, :], wl[:, k % 2, :]), k == 0, k == KD - 1)
                        if k == KD - 1:
                            close_bank((kind, c, i), last)
                if j < 3:
                    count_piece((kind, c), j, last)
                else:
                    piece_used[piece_no[(kind, c), j]] = (kind, c, NT - 1)
            last_use((kind, c), (kind, c, NT - 1))

        cut3 = Cut()
        hQ = cut3(2 * T).rearrange("p (a n) -> p a n", a=2)
        hF = cut3(2 * T).rearrange("p (a n) -> p a n", a=2)
        hG = cut3(2 * T).rearrange("p (a n) -> p a n", a=2)
        hV = cut3(2 * T).rearrange("p (a i n) -> p a i n", a=2, i=NT)
        hK, hB, hEB, hT2, hKI, hKN, hAT, hO = (cut3(T) for _ in range(8))
        hVT = rows[:, ROW_A, :].rearrange("p (a n) -> p a n", a=2)
        hKX = cut3(2 * CPT * P).rearrange("p (a c n) -> p a c n", a=2, c=CPT)
        hS = cut3(NCHUNK * P).rearrange("p (c n) -> p c n", c=NCHUNK)
        cut4 = Cut()
        mT = cut4(KD * T).rearrange("p (k t) -> p k t", k=KD)
        mS = cut4(4 * T).rearrange("p (a n) -> p a n", a=4)
        mT_high = oH
        mD = cut4(2 * T).rearrange("p (a n) -> p a n", a=2)
        mP = cut4(4 * T).rearrange("p (a n) -> p a n", a=4)

        cut5 = Cut()
        xn2 = cut5(NT * D).rearrange("p (i n) -> p i n", i=NT)
        lg = cut5(NT * 36).rearrange("p (i n) -> p i n", i=NT)
        g8, gtop, etop = (cut5(NT * 8).rearrange("p (i n) -> p i n", i=NT) for _ in range(3))
        gat, eat = (cut5(NT * 8).rearrange("p (i n) -> p i n", i=NT).bitcast(u32) for _ in range(2))
        gexp, gone = (cut5(NT * EXP_GROUPS).rearrange("p (i n) -> p i n", i=NT) for _ in range(2))
        gsum, emax2 = (cut5(NT) for _ in range(2))
        masked, hot0, hot1, both, rank, place, tmp32 = (cut5(NT * NEXP).rearrange("p (i n) -> p i n", i=NT) for _ in range(7))
        counts, blocks_of, block_end, over0, tmp1 = (cut5(NEXP) for _ in range(5))
        cmp7 = cut5(NEXP * 7).rearrange("p (e n) -> p e n", e=NEXP)
        cmp16 = cut5(15 * NEXP).rearrange("p (b e) -> p b e", b=15)
        idxf = cut5(NT * 3).rearrange("p (i n) -> p i n", i=NT)
        slotf = cut5(NT * 2).rearrange("p (i n) -> p i n", i=NT)
        overf = cut5(16)
        tabi = cut5(P).bitcast(i32)
        tabf = cut5(P)
        assert cut5.at <= 9216
        cut5.at = 9216
        rw = cut5(KD * 36).rearrange("p (k n) -> p k n", k=KD)
        rbias = cut5(36)
        cut6 = Cut()
        gx = cut6(D)
        xT = cut6(KD * P).rearrange("p (k n) -> p k n", k=KD)
        sg = cut6(2 * DE).rearrange("p (a n) -> p a n", a=2)
        hx = cut6(2 * DE).rearrange("p (a n) -> p a n", a=2)
        aT = cut6(2 * 4 * CAP).rearrange("p (a k n) -> p a k n", a=2, k=4)
        ysb = cut6(2 * 512).rearrange("p (a n) -> p a n", a=2)
        cut6.at = max(cut6.at, 0)
        yg = scr[:, 0:2 * NT * D].rearrange("p (i a n) -> p i a n", i=NT, a=2)
        w0 = chunk_no[("wout", 0)]
        moe_slot = [ring[:, (w0 - 1) % NS, :], ring[:, w0 % NS, :], ring[:, (w0 + 1) % NS, :], ring[:, NS, :],
                    brn[:, 0, :], brn[:, 1, :]]
        cut7 = Cut()
        zq, zk = (cut7(2 * T).rearrange("p (a n) -> p a n", a=2) for _ in range(2))
        zv = cut7(2 * T).rearrange("p (a i n) -> p a i n", a=2, i=NT)
        zT = cut7(2 * T).rearrange("p (a n) -> p a n", a=2)
        zA, zU = (cut7(3 * T).rearrange("p (a n) -> p a n", a=3) for _ in range(2))
        zR = cut7(3 * (T + 4)).rearrange("p (a n) -> p a n", a=3)
        zvT = cut7(T)
        Z_BANK = (0, 1, 7)
        yb = scr[:, 0:NT * D].rearrange("p (i n) -> p i n", i=NT)
        xn3 = brn[:, 1, :].rearrange("p (i n) -> p i n", i=NT)
        h_low = b0T
        sT, sT_high = oN, b0T
        ff = scr[:, :].rearrange("p (f t) -> p f t", f=FT)
        fS = brn[:, 1, 0:2048].rearrange("p (a n) -> p a n", a=4)
        ffh = brn[:, 1, 2048:4096].rearrange("p (a n) -> p a n", a=4)
        ZU = [(j, hh, i) for j in range(KD) for hh in range(2) for i in range(NT)]

        def pe_router(pe):
            pe.wait_ge(sem("xn2_done"), NT)
            pe_transposes(pe, "h2", xn2)
            pe.wait_ge(sem("router_in"), 64)
            for k in range(KD):
                emptied(pe, ("h2", k))
                for i in range(NT):
                    if k == 0:
                        open_bank(pe, (0, 1, 6, 7)[i], ("logits", i))
                    last = pe.matmul(ps[:, (0, 1, 6, 7)[i], 0:36], hT[:, k, i * P:(i + 1) * P], rw[:, k, :],
                                     start=k == 0, stop=k == KD - 1)
                    if k == KD - 1:
                        close_bank(("logits", i), last)
            pe.wait_ge(sem("chosen"), 1)
            t = open_bank(pe, 1, "rank")
            for i in range(NT + 1):
                for j in range(min(i + 1, NT)):
                    last = pe.matmul(t[:, i * NEXP:(i + 1) * NEXP], const("before") if j == i else ones, both[:, j, :],
                                     start=j == 0, stop=j == min(i, NT - 1))
            close_bank("rank", last)
            pe.wait_ge(sem("slots_float"), 1)
            t = open_bank(pe, 0, "slots")
            close_bank("slots", pe.transpose(t[:, 0:SLOTS // P], tabf[0:SLOTS // P, :], ident[0:SLOTS // P, 0:SLOTS // P]))

        fills_before_moe = [0] * 8

        def pe_experts(pe):
            base = fills_before_moe
            base[:] = fills

            def gathered(p):
                pe.wait_ge(sem("gathered"), 16 * (p + 1) if isinstance(p, int) else p * 16 + 16)
                for b in range(2):
                    pe.wait_ge(empty[b], p + base[b])
                    for k in range(4 * b, 4 * b + 4):
                        last = pe.transpose(ps[:, b, (k % 4) * P:(k % 4 + 1) * P], gx[:, k * P:(k + 1) * P], ident)
                    last.then_inc(full[b], 1)

            def up(p, a):
                if a == 0:
                    for b in range(2):
                        pe.wait_ge(empty[b], p + (base[b] + 1))
                pe.wait_ge(empty[2 + a], p + base[2 + a])
                w = []
                for m in range(2):
                    pe.wait_ge(sem(f"moe_chunk{3 * a + m}_full"), p * 16 + 16)
                    w.append(moe_slot[3 * a + m].rearrange("p (k n) -> p k n", k=KD))
                for k in range(KD):
                    for m in range(2):
                        last = pe.matmul(ps[m * CAP:(m + 1) * CAP, 2 + a, :], xT[:, k, a * CAP:(a + 1) * CAP],
                                         w[m][:, k, :], start=k == 0, stop=k == KD - 1)
                last.then_inc(full[2 + a], 1)

            def down(p, a):
                pe.wait_ge(empty[2 + a], p + (base[2 + a] + 1))
                pe.wait_ge(empty[4 + a], p + base[4 + a])
                for k in range(4):
                    last = pe.matmul(ps[:, 4 + a, k * CAP:(k + 1) * CAP], hx[0:CAP, a, k * P:(k + 1) * P],
                                     ident[0:CAP, 0:CAP], start=True, stop=True)
                last.then_inc(full[4 + a], 1)
                pe.wait_ge(empty[4 + a], p + (base[4 + a] + 1))
                pe.wait_ge(empty[6 + a], p + base[6 + a])
                pe.wait_ge(sem(f"moe_chunk{3 * a + 2}_full"), p * 16 + 16)
                w = moe_slot[3 * a + 2].rearrange("p (k n) -> p k n", k=4)
                for k in range(4):
                    for m in range(2):
                        last = pe.matmul(ps[m * CAP:(m + 1) * CAP, 6 + a, :], aT[:, a, k, :],
                                         w[:, k, m * 512:(m + 1) * 512], start=k == 0, stop=k == 3)
                last.then_inc(full[6 + a], 1)

            gathered(0)
            with pe.Fori(0, NEXP // 2 - 1) as p:
                up(p, 0)
                down(p, 0)
                up(p, 1)
                gathered(p + 1)
                down(p, 1)
            p = NEXP // 2 - 1
            up(p, 0)
            down(p, 0)
            up(p, 1)
            down(p, 1)
            for b in range(8):
                fills[b] += NEXP // 2
            filling["moe_last"] = (7, fills[7])
            filling["moe_gathered"] = (1, fills[1])
            filling["moe_first_down"] = (6, fills[6])
            pe.wait_ge(sem("over_known"), 1)
            n = pe.value_load(over[0:1, 15:16], min_val=0, max_val=OVB)
            emptied(pe, "moe_first_down")
            with pe.If(n > 0):
                with pe.Fori(0, n) as b:
                    pe.wait_ge(sem("ov_x"), b * 16 + 16)
                    for k in range(KD):
                        last = pe.matmul(ps[:, 0, k * CAP:(k + 1) * CAP], gx[0:CAP, k * P:(k + 1) * P], ident[0:CAP, 0:CAP],
                                         start=True, stop=True)
                    last.then_inc(sem("ov_gt"), 1)
                    pe.wait_ge(sem("ov_xt"), b + 1)
                    pe.wait_ge(sem("ov_w"), b * 48 + 48)
                    for k in range(KD):
                        for m in range(2):
                            w = moe_slot[m].rearrange("p (k n) -> p k n", k=KD)
                            last = pe.matmul(ps[m * CAP:(m + 1) * CAP, 2, :], xT[:, k, 0:CAP], w[:, k, :],
                                             start=k == 0, stop=k == KD - 1)
                    last.then_inc(sem("ov_h"), 1)
                    pe.wait_ge(sem("ov_a"), b + 1)
                    for k in range(4):
                        last = pe.matmul(ps[:, 4, k * CAP:(k + 1) * CAP], hx[0:CAP, 0, k * P:(k + 1) * P], ident[0:CAP, 0:CAP],
                                         start=True, stop=True)
                    last.then_inc(sem("ov_at"), 1)
                    pe.wait_ge(sem("ov_ate"), b + 1)
                    w = moe_slot[2].rearrange("p (k n) -> p k n", k=4)
                    for k in range(4):
                        for m in range(2):
                            last = pe.matmul(ps[m * CAP:(m + 1) * CAP, 6, :], aT[:, 0, k, :],
                                             w[:, k, m * 512:(m + 1) * 512], start=k == 0, stop=k == 3)
                    last.then_inc(sem("ov_y"), 1)
            pe.wait_ge(sem("ov_done"), 1)

        def pe_sb(pe):
            pe.wait_ge(sem("xn3_done"), NT)
            pe_transposes(pe, "h3", xn3)
            pe.wait_ge(sem("h3_split"), KD)

            def project(j, which, half):
                name = (("sq", "sk", "sv")[which], j)
                feature_major3(pe, 6 if which == 1 else 5, name, ("sb", j), which, hT, h_low, (half,))
                if half and which == 2:
                    last_use(("sb", j), name)

            def transpose_values(j):
                emptied(pe, ("sv", j))
                transpose_512(pe, 6, ("svT", j), zvT)

            def scores(u):
                j, hh, i = ZU[u]
                if hh == 0 and i == 0:
                    emptied(pe, ("sq", j))
                    emptied(pe, ("sk", j))
                r, n = slice(64 * hh, 64 * hh + 64), P * (i + 1)
                t = open_bank(pe, Z_BANK[u % 3], ("z", u))
                close_bank(("z", u), pe.matmul(t[:, 0:n], zq[r, j % 2, i * P:(i + 1) * P], zk[r, j % 2, 0:n],
                                               start=True, stop=True))

            def transposes(u):
                pe.wait_ge(sem("sb_weights"), u + 1)
                t = open_bank(pe, 2 + u % 2, ("zT", u))
                for k in range(ZU[u][2] + 1):
                    last = pe.transpose(t[:, k * P:(k + 1) * P], zA[:, u % 3, k * P:(k + 1) * P], ident)
                close_bank(("zT", u), last)

            for x in range(6):
                project(0, x // 2, x % 2)
            transpose_values(0)
            for u in range(3):
                scores(u)
            transposes(0)
            for u, (j, hh, i) in enumerate(ZU):
                if u % 8 < 6 and j + 1 < KD:
                    project(j + 1, u % 8 // 2, u % 2)
                if u % 8 == 7 and j + 1 < KD:
                    transpose_values(j + 1)
                if u + 3 < len(ZU):
                    scores(u + 3)
                if u + 1 < len(ZU):
                    transposes(u + 1)
                if hh == 0 and i == 0:
                    emptied(pe, ("svT", j))
                emptied(pe, ("zT", u))
                r = slice(64 * hh, 64 * hh + 64)
                t = open_bank(pe, 4, ("zO", u))
                for k in range(i + 1):
                    last = pe.matmul(t[r, 0:P], zv[:, j % 2, k, 64 * hh:64 * hh + 64], zT[:, u % 2, k * P:(k + 1) * P],
                                     start=k == 0, stop=k == i)
                close_bank(("zO", u), last)
            emptied(pe, ("zO", len(ZU) - 1))
            for c in range(2):
                out_projection(pe, "wo", c, sT_high, sT, ("wo_split", 1))

        def pe_ffn(pe):
            pe.wait_ge(sem("xn4_done"), NT)
            pe_transposes(pe, "h4", xn3)
            pe.wait_ge(sem("h4_split"), KD)
            for f in range(FT):
                for m in range(2):
                    feature_major3(pe, 2 * (f % 4) + m, ("fgu", m, f), ("fi", f // 2), 2 * (f % 2) + m, hT, h_low)
                last_use(("fi", f // 2), ("fgu", 1, f))
            t = {}
            for f in range(FT):
                wh, wl = pe_piece(pe, ("fo", f // 4), f % 4)
                pe.wait_ge(sem("ff_split"), f + 1)
                for i in range(NT):
                    for c in range(2):
                        name = ("fo", c, i)
                        if f == 0:
                            t[c, i] = open_bank(pe, 4 * c + i, name)
                        tok, half = slice(i * P, (i + 1) * P), slice(c * 512, (c + 1) * 512)
                        last = triple(pe, t[c, i], (single(ffh[:, f % 4, tok]), single(ff[:, f, tok])),
                                      (wh[:, half], wl[:, half]), f == 0, f == FT - 1)
                        if f == FT - 1:
                            close_bank(name, last)
                if f < FT - 1:
                    count_piece(("fo", f // 4), f % 4, last)
                    last_use(("fo", f // 4), ("pieces", counted_pieces[0]))
                else:
                    piece_used[piece_no[("fo", f // 4), f % 4]] = name

        N_PACK = 13
        N_SMALL = 3
        pe_stages = [pe_start, pe_kv, pe_attention, pe_hgrn, pe_merge, pe_router, pe_experts, None, pe_sb, pe_ffn]

        @block.tensor
        def _(pe):
            for stage in pe_stages:
                if stage:
                    stage(pe)

        @block.sync
        def _(sp):
            def load(n):
                for view, src in chunk_list[n][1]:
                    sp.dma_start(view(slot_of(chunk_list[n][0])), src).then_inc(arrived_sem[n % NS], 16)

            sp.wait_ge(sem("packs_in"), 16 * N_PACK)
            for n in range(AFTER_MOE):
                if n >= NS:
                    used(sp, used_by[n - NS])
                load(n)
            w = A["exp_w1"][0], A["exp_w3"][0], A["exp_w2"][0]

            def expert_part(x, e):
                kind, k = x % 3, (KD, KD, 4)[x % 3]
                src = w[kind][bass.ds(e, 1), :, :].rearrange("a (k p) n -> p (a k) n", p=P)
                sp.dma_start(moe_slot[x].rearrange("p (k n) -> p k n", k=k), src).then_inc(sem(f"moe_chunk{x}_full"), 16)

            user = [2, 2, 6, 3, 3, 7]
            first = {b: filling["moe_last"][1] - NEXP // 2 + (fills_before_moe[b] - fills_before_moe[7]) for b in (2, 3, 6, 7)}
            for x in range(6):
                if x == 0:
                    filled(sp, used_by[chunk_no[("merge", 7)]])
                elif x == 1:
                    filled(sp, ("wout", 1, NT - 1))
                expert_part(x, x // 3)
            with sp.Fori(1, NEXP // 2) as p:
                for x in range(6):
                    sp.wait_ge(full[user[x]], p + first[user[x]])
                    expert_part(x, p * 2 + x // 3)
            sp.wait_ge(sem("over_known"), 1)
            n = sp.value_load(over[0:1, 15:16], min_val=0, max_val=OVB)
            filled(sp, "moe_first_down")
            with sp.If(n > 0):
                with sp.Fori(0, n) as b:
                    e = sp.value_load(over[0:1, bass.ds(b, 1)], min_val=0, max_val=NEXP - 1)
                    sp.wait_ge(sem("ov_free"), b + 1)
                    for x in range(3):
                        k = (KD, KD, 4)[x]
                        sp.dma_start(moe_slot[x].rearrange("p (k n) -> p k n", k=k),
                                     w[x][bass.ds(e, 1), :, :].rearrange("a (k p) n -> p (a k) n", p=P)).then_inc(sem("ov_w"), 16)
            sp.wait_ge(sem("ov_done"), 1)
            sp.wait_ge(sem(f"y_tile{NT - 1}_gathered"), 32)
            for n in range(AFTER_MOE, len(chunk_list)):
                if n - NS >= AFTER_MOE:
                    used(sp, used_by[n - NS])
                load(n)
            for i in range(NT):
                sp.wait_ge(sem("out_ready"), i + 1)
                sp.dma_start(out[0, i * P:(i + 1) * P, :], xres[:, i, :]).then_inc(sem("out_stored"), 16)
            sp.wait_ge(sem("out_stored"), 16 * NT)

        def pool_start(g):
            g.dma_start(slot_dram, A["no_token"]).then_inc(sem("slots_clear"), 16)
            for c in range(2):
                emptied(g, ("rel", c))
            g.dma_start(rel_dram, relrow[:, :]).then_inc(sem("rel_stored"), 16)
            g.wait_ge(sem("rel_stored"), 16)
            g.wait_ge(arrived_sem[3 % NS], arrived_at["ada", 1, 3])
            g.dma_start(bias_back, bass.AP(tensor=rel_dram.tensor, offset=T - P,
                                           ap=[[1, P], [REL + 1, HEADS], [1, T]])).then_inc(sem("bias_in"), 16)


        def pool_ada(g, key):
            m, c = ada_at[key]
            n = 4 * list(ada_at).index(key)
            s = wide(arrived(g, ("ada", m, c)))
            col = csil[:, (m - 1) * KD:m * KD]
            g.tensor_tensor(s, s, grow(col, 512), ALU.mult).then_inc(sem("ada_added"), 1)
            for x, half in enumerate((4, 2, 1)):
                g.wait_ge(sem("ada_added"), n + x + 1)
                g.tensor_tensor(s[:, 0:half, :], s[:, 0:half, :], s[:, half:2 * half, :], ALU.add).then_inc(sem("ada_added"), 1)

        def pool_attention(g):
            g.wait_ge(sem("silu_c"), 1)
            for h in range(HEADS):
                pool_ada(g, ("attn", h))
            g.wait_ge(sem("const_in"), 16)
            g.dma_start(y_dram[MAIN:SLOTS, :].rearrange("(p a) (b n) -> p (a b) n", p=P, n=T),
                        grow(const("zeros"), (SLOTS - MAIN) // P * D // T, 1)).then_inc(sem("overflow_zero"), 16)

        def pool_hgrn(g):
            for h in range(HEADS):
                pool_ada(g, ("hg", h))

        def pool_merge(g):
            for j in range(KD):
                if j < 4:
                    pool_ada(g, ("merge", j))
                emptied(g, ("mH", j))
                emptied(g, ("mN", j))
                g.tensor_tensor(mT[:, j, :], mP[:, 2 * (j % 2), :], mP[:, 2 * (j % 2) + 1, :],
                                ALU.add).then_inc(sem("merged"), 1)

        def pool_router(g):
            g.wait_ge(sem("slots_clear"), 16)
            g.wait_ge(sem("dest_ready"), 1)
            for i in range(NT):
                for c in range(2):
                    g.indirect_dma_start(slot_dram, bass.IndirectOffsetOnAxis(ap=dest[:, i, c:c + 1], axis=0),
                                         token[:, i:i + 1], None).then_inc(sem("slots_set"), 16)
            g.wait_ge(sem("slots_set"), 16 * 2 * NT)
            g.dma_start(tabi[0:SLOTS // P, :], slot_dram.rearrange("(c p) a -> c (p a)", p=P)).then_inc(sem("slots_in"), 16)

        def pool_experts(g):
            g.wait_ge(sem("xn_stored"), 16)
            g.wait_ge(sem("slots_back"), 1)
            for p in range(NEXP // 2):
                if p:
                    g.wait_ge(full[1], fills_before_moe[1] + p)
                g.indirect_dma_start(gx, None, xn_dram, bass.IndirectOffsetOnAxis(ap=slot_token[:, p:p + 1], axis=0)
                                     ).then_inc(sem("gathered"), 16)
            n = g.value_load(over[0:1, 15:16], min_val=0, max_val=OVB)
            g.memset(st[:, 92:93], 0.0).then_inc(sem("ov_carried"), 1)
            filled(g, "moe_gathered")
            with g.If(n > 0):
                with g.Fori(0, n) as b:
                    g.wait_ge(sem("ov_free"), b + 1)
                    g.dma_start(over_token[:, :], slot_dram[bass.ds(b * CAP + MAIN, CAP), :]).then_inc(sem("ov_index"), 16)
                    g.wait_ge(sem("ov_index"), b * 16 + 16)
                    g.wait_ge(sem("ov_carried"), b + 1)
                    g.tensor_tensor(st[:, 92:93], ones[:, 0:1], ones[:, 0:1], ALU.add).then_inc(sem("ov_carried"), 1)
                    g.indirect_dma_start(gx[0:CAP, :], None, xn_dram,
                                         bass.IndirectOffsetOnAxis(ap=over_token[:, 0:1], axis=0)).then_inc(sem("ov_x"), 16)
            g.wait_ge(sem("ov_done"), 1)

        def pool_combine(g):
            for x in range(2):
                g.wait_ge(sem(f"y{x}_stored"), 32 * (NEXP // 2))
            g.wait_ge(sem("overflow_zero"), 16)
            for i in range(NT):
                for c in range(2):
                    g.indirect_dma_start(yg[:, i, c, :], None, y_dram, bass.IndirectOffsetOnAxis(ap=dest[:, i, c:c + 1], axis=0)
                                         ).then_inc(sem(f"y_tile{i}_gathered"), 16)

        pool_stages = [pool_start, None, pool_attention, pool_hgrn, pool_merge, pool_router, pool_experts, pool_combine]

        @block.gpsimd
        def _(g):
            for stage in pool_stages:
                if stage:
                    stage(g)

        def act_start(a):
            a.dma_start(cst[:, :], A["shape_const"]).then_inc(sem("const_in"), 16)
            pack = [(0, 0, A["c"].rearrange("a (k p) -> (a k) p", p=P)), (0, 8, A["c_2"].rearrange("a (k p) -> (a k) p", p=P)),
                    (0, 16, A["ada_b"].rearrange("a (k p) -> (a k) p", p=P)),
                    (0, 64, A["cmp_pos_k"][0]), (0, 96, A["cmp_pos_v"][0]),
                    (1, 0, A["b_in"][:, 0:GATE_N].rearrange("a (k p) -> (a k) p", p=P)),
                    (1, BMG, A["b_in"][:, MG_H:MG_H + 2 * D].rearrange("a (k p) -> (a k) p", p=P)),
                    (1, ADAB2, A["ada_b_2"].rearrange("a (k p) -> (a k) p", p=P)),
                    (1, HGN, A["hg_norm_w"].rearrange("a (k p) -> (a k) p", p=P)),
                    (1, B1, A["cmp_b1_k"]), (1, B1 + 1, A["cmp_b1_v"]),
                    (2, 0, A["hg_lb_logits"].rearrange("a (k p) -> (a k) p", p=P)),
                    (2, 16, A["norm_g_2"][0].rearrange("a (k p) -> (a k) p", p=P))]
            assert len(pack) == N_PACK
            for b, r, src in pack:
                a.dma_start(packs[r:r + src.shape[0], b, :], src).then_inc(sem("packs_in"), 16)
            a.dma_start(xres[:, :, :], A["x"][0].rearrange("(i p) n -> p i n", p=P)).then_inc(sem("x_in"), 16)
            with nc.allow_non_contiguous_dma(reason="the small bias table, transposed"):
                a.dma_start(tab[0:BUCKETS, :], A["rel_bias"].rearrange("h b -> b h")).then_inc(sem("rel_in"), 16)
            a.dma_start(tab[BUCKETS:BUCKETS + 1, :], A["neg_row"]).then_inc(sem("rel_in"), 16)
            a.dma_start(hot, A["rel_hot"]).then_inc(sem("rel_in"), 16)
            with nc.allow_non_contiguous_dma(reason="24 gate columns"):
                a.dma_start(wgate, cols(A["w_in"], GATE_N, 24)).then_inc(sem("wgate_in"), 16)
            emptied(a, "vec")
            a.activation(csil[:, :], vec[:, 0, 0:16], ACT.Silu).then_inc(sem("silu_c"), 1)
            a.wait_ge(sem("lb_diff"), 1)
            a.activation(colb[:, 0:8], colb[:, 0:8], ACT.Sigmoid).then_inc(sem("lb_sigmoid"), 1)
            for c in range(2):
                t = filled(a, ("rel", c))
                free_bank(("rel", c), a.activation(relrow[:, c * 512:(c + 1) * 512], t[0:HEADS, :], ACT.Copy))
            act_deviation(a, "x_var", "x_sd")
            a.wait_ge(sem("silu_c"), 1)
            for c in range(4):
                s = wide(arrived(a, ("ada", 1, c)))
                for k in range(KD):
                    w = a.activation(s[:, k, :], s[:, k, :], ACT.Identity, scale=csil[:, k:k + 1])
                w.then_inc(sem("start_ada_scaled"), 1)
            for c in range(4):
                emptied(a, ("ada", 1, c))
            a.wait_ge(sem("rel_stored"), 16)
            filled(a, "cbias")
            act_modulate(a, "h1", SC1, SH1)

        def act_deviation(a, wait, done):
            a.wait_ge(sem(wait), 1)
            a.activation(st[:, 4:8], st[:, 0:4], ACT.Sqrt).then_inc(sem(done), 1)

        def act_modulate(a, name, sc, sh):
            for k in range(KD):
                t = filled(a, (name, k))
                free_bank((name, k), a.activation(hT[:, k, :], t, ACT.Identity, bias=mod[:, sh, k:k + 1],
                                                  scale=mod[:, sc, k:k + 1]))

        def act_high_part(a, name):
            for k in range(KD):
                emptied(a, (name, k))
                a.activation(single(hT[:, k, :]), h_low[:, k, :], ACT.Copy).then_inc(sem(name + "_rounded"), 1)

        def act_kv(a):
            a.wait_ge(sem("ln_done"), 4)
            for k in range(KD):
                filled(a, ("h1", k))
            for k in range(KD):
                a.wait_ge(empty[filling["h1", k][0]], filling["h1", k][1])
                a.activation(single(h1_high[:, k, :]), hT[:, k, :], ACT.Copy).then_inc(sem("h1_rounded"), 1)
            for j in range(4):
                act_round(a, ("kv", 0), j)
            a.wait_ge(sem("wgate_in"), 16)
            a.activation(single(wgate_high), wgate, ACT.Copy).then_inc(sem("wgate_rounded"), 1)

            def bc(src, n):
                return bass.AP(tensor=src.tensor, offset=src.offset, ap=[[0, P], [1, n]])
            a.dma_start(gbias, A["b_in"][0:1, GATE_N:MG_H].rearrange("a n -> n a")).then_inc(sem("small_in"), 16)
            for v, kv in enumerate("kv"):
                a.dma_start(w2cmp[:, v, :], A[f"cmp_w2_{kv}"][0]).then_inc(sem("small_in"), 16)
            a.dma_start(rows[:, ROW_B, :], bc(A["ln1_b"][0, :], D)).then_inc(sem("row_b_in"), 16)
            for c in range(3):
                for j in range(4):
                    if c == 0 or j < 2:
                        dst = kvc[:, j // 2, j % 2, :] if c == 0 else kfull[:, c - 1, j, :]
                    else:
                        dst = vtmp[:, j - 2, :]
                    t = filled(a, ("kvT", c, j))
                    free_bank(("kvT", c, j), a.activation(dst, t, ACT.Identity, bias=bin_col(KV_N + 512 * c + P * j)))
                    if c < 2:
                        act_round(a, ("kv", c + 1), j)
            for x in range(2):
                act_round(a, ("nq", 0), x)
            a.wait_ge(sem("small_in"), 16 * N_SMALL)
            t = filled(a, "gate")
            free_bank("gate", a.activation(gT, t[0:24, :], ACT.Sigmoid, bias=gbias))
            for v, kv in enumerate("kv"):
                t = filled(a, ("hid", kv))
                a.activation(hsig[:, v, :], t[:, 0:GROUPS * NCMP], ACT.Sigmoid,
                             bias=vec[:, 1, B1 + v:B1 + v + 1]).then_inc(sem("hid_sigmoid"), 1)
            t = filled(a, "kcmp")
            free_bank("kcmp", a.activation(kcmpT, t[:, 0:GROUPS * NCMP], ACT.Copy))

        def act_attention(a):
            def query(h):
                t = filled(a, ("nqT", h))
                free_bank(("nqT", h), a.activation(qT[:, h % 2, :], t, ACT.Identity, scale=SCALE,
                                                   bias=colb[:, 16 + h:17 + h]))

            def exps(u):
                h, i = UNITS[u]
                n = P * (i + 1)
                a.wait_ge(sem("neg_max"), u + 1)
                for b, (o, m) in enumerate(((2 * T, NCMP), (0, n), (T, n))):
                    p = prob[:, u % 2, o:o + m]
                    c = 3 * (u % 2) + b
                    e = a.activation(p, p, ACT.Exp, bias=st[:, 18 + c:19 + c], accum_out=st[:, 24 + c:25 + c])
                e.then_inc(sem("exp_done"), 1)

            query(0)
            exps(0)
            exps(1)
            for u, (h, i) in enumerate(UNITS):
                t = filled(a, ("T", 1, u))
                free_bank(("T", 1, u), a.activation(probT[:, u % 2, 4:5 + i, :], t[:, 0:P * (i + 1)], ACT.Copy))
                if i == 1 and h + 1 < HEADS:
                    query(h + 1)
                if u + 2 < len(UNITS):
                    exps(u + 2)
                if i == NT - 1 and h + 2 < HEADS:
                    act_round(a, ("nq", (h + 2) // 2), h % 2)
                t = filled(a, ("O", u))
                free_bank(("O", u), a.activation(oN[:, h, i * P:(i + 1) * P], t[:, 0:P], ACT.Copy))

        def act_hgrn(a):
            filled(a, ("O", len(UNITS) - 1))
            def weights(h, js=range(4)):
                for j in js:
                    act_round(a, ("hg", h), j)

            weights(0)

            def inputs(h):
                t = filled(a, ("hq", h))
                free_bank(("hq", h), a.activation(hQ[:, h % 2, :], t, ACT.Identity, bias=bin_col(Q_H + P * h)))
                t = filled(a, ("hf", h))
                free_bank(("hf", h), a.activation(hF[:, h % 2, :], t, ACT.Sigmoid, bias=bin_col(F_H + P * h)))
            def out_gate(h):
                if h >= 2:
                    a.wait_ge(sem("hg_out"), 2 * (h - 1))
                t = filled(a, ("hg", h))
                free_bank(("hg", h), a.activation(hG[:, h % 2, :], t, ACT.Sigmoid, bias=bin_col(G_H + P * h)))

            def values(h):
                t = filled(a, ("hi", h))
                free_bank(("hi", h), a.activation(hVT[:, h % 2, :], t, ACT.Identity, bias=bin_col(I_H + P * h)))

            inputs(0)
            out_gate(0)
            values(0)
            weights(1)
            for h in range(HEADS):
                a.wait_ge(sem("hg_f"), h + 1)
                if h:
                    a.wait_ge(sem("hg_out"), 2 * h - 1)
                a.activation(hT2, hF[:, h % 2, :], ACT.Ln).then_inc(sem("hg_logf"), 1)
                a.wait_ge(sem("hg_b"), 2 * h + 1)
                a.activation(hEB, hB, ACT.Exp).then_inc(sem("hg_exp"), 1)
                a.activation(hT2, hB, ACT.Exp, scale=-1.0).then_inc(sem("hg_exp"), 1)
                a.wait_ge(sem("hg_b"), 2 * h + 2)
                a.activation(hKN, hKN, ACT.Exp).then_inc(sem("hg_exp"), 1)
                if h + 1 < HEADS:
                    inputs(h + 1)
                    out_gate(h + 1)
                if h + 2 < HEADS:
                    weights(h + 2, range(3))
                emptied(a, ("oT", h))
                a.activation(hT2, hO, ACT.Square).then_inc(sem("hg_square"), 1)
                if h + 1 < HEADS:
                    values(h + 1)
                if h + 2 < HEADS:
                    weights(h + 2, [3])
                t = filled(a, ("ss", h))
                a.activation(hT2, t, ACT.Ln, scale=1.0 / P, bias=colb[:, 32:33]).then_inc(sem("hg_lnvar"), 1)
                a.wait_ge(sem("hg_lnvar"), h + 1)
                free_bank(("ss", h), a.activation(hT2, hT2, ACT.Exp, scale=-0.5))

        def act_merge(a):
            a.wait_ge(sem("hg_out"), 2 * HEADS)
            def weights(j):
                for x in range(2):
                    act_round(a, ("merge", j), x)

            weights(0)
            weights(1)
            for j in range(KD):
                for b, (name, col) in enumerate((("mgh", MG_H), ("mgn", MG_N))):
                    if j >= 2:
                        emptied(a, (("mH", "mN")[b], j - 2))
                    t = filled(a, (name, j))
                    free_bank((name, j), a.activation(mS[:, 2 * (j % 2) + b, :], t, ACT.Sigmoid, bias=bin_col(col + P * j)))
                if j + 2 < KD:
                    weights(j + 2)
            act_output_split(a, "wout", mT, mT_high, "merged")

        def act_output_split(a, kind, src, high, ready):
            for j in range(4):
                act_round(a, (kind, 0), j)
                for k in (2 * j, 2 * j + 1):
                    if ready == "merged":
                        a.wait_ge(sem(ready), KD)
                        filled(a, ("mH", KD - 1))
                    a.activation(single(high[:, k, :]), src[:, k, :], ACT.Copy).then_inc(sem(kind + "_rounded"), 1)
            for j in range(4):
                act_round(a, (kind, 1), j)

        def dve_output_split(v, kind, src, high):
            for j in range(4):
                dve_rest(v, (kind, 0), j)
                for k in (2 * j, 2 * j + 1):
                    v.wait_ge(sem(kind + "_rounded"), k + 1)
                    v.tensor_tensor(single(src[:, k, :]), src[:, k, :], as_float(high[:, k, :]), ALU.subtract).then_inc(sem(kind + "_split"), 1)

        def bcast_row(src, n):
            return bass.AP(tensor=src.tensor, offset=src.offset, ap=[[0, P], [1, n]])

        def act_router(a):
            emptied(a, ("hiT", HEADS - 1))
            a.dma_start(rows[:, ROW_A, :], bcast_row(A["ln1_g"][0, :], D)).then_inc(sem("row_a_in"), 16)
            with nc.allow_non_contiguous_dma(reason="narrow router matrices"):
                a.dma_start(rw[:, :, 0:4], cols(A["router_grp_w"], 0, 4)).then_inc(sem("router_in"), 16)
                a.dma_start(rw[:, :, 4:36], cols(A["router_exp_w"], 0, NEXP)).then_inc(sem("router_in"), 16)
            a.dma_start(rbias[:, 0:4], bcast_row(A["router_grp_b"][0, :], 4)).then_inc(sem("router_in"), 16)
            a.dma_start(rbias[:, 4:36], bcast_row(A["router_exp_b"][0, :], NEXP)).then_inc(sem("router_in"), 16)
            act_deviation(a, "x1_var", "x1_sd")
            act_deviation(a, "xn2_var", "xn2_sd")
            a.wait_ge(sem("xn2_done"), NT)
            a.dma_start(xn_dram.rearrange("(i p) n -> p i n", p=P), xn2).then_inc(sem("xn_stored"), 16)
            a.dma_start(rows[:, ROW_A, :], bcast_row(A["ln2_g"][0, :], D)).then_inc(sem("row_a_in"), 16)
            a.dma_start(rows[:, ROW_B, :], bcast_row(A["ln2_b"][0, :], D)).then_inc(sem("row_b_in"), 16)
            act_modulate(a, "h2", SC2, SH2)
            a.wait_ge(sem("group_logits"), 1)
            a.activation(gexp, gexp, ACT.Exp).then_inc(sem("group_exp"), 1)
            a.wait_ge(sem("second_logit"), 1)
            a.activation(emax2, emax2, ACT.Exp).then_inc(sem("second_exp"), 1)

        def act_experts(a):
            base = fills_before_moe

            def tokens(p):
                for b in range(2):
                    a.wait_ge(full[b], p + (base[b] + 1))
                    for k in range(4 * b, 4 * b + 4):
                        e = a.activation(xT[:, k, :], ps[:, b, (k % 4) * P:(k % 4 + 1) * P], ACT.Identity,
                                         bias=mod[:, SH2, k:k + 1], scale=mod[:, SC2, k:k + 1])
                    e.then_inc(empty[b], 1)

            def gate(p, x):
                a.wait_ge(full[2 + x], p + (base[2 + x] + 1))
                a.activation(sg[0:CAP, x, :], ps[0:CAP, 2 + x, :], ACT.Silu).then_inc(sem("moe_silu"), 1)

            def store(p, x, first=False):
                a.wait_ge(full[6 + x], p + (base[6 + x] + 1))
                if not first:
                    a.wait_ge(sem(f"y{x}_stored"), p * 32)
                a.activation(ysb[:, x, :], ps[:, 6 + x, :], ACT.Copy).then_inc(empty[6 + x], 1)
                a.wait_ge(empty[6 + x], p + (base[6 + x] + 1))
                for m in range(2):
                    a.dma_start(y_dram[bass.ds(p * (2 * CAP) + x * CAP, CAP), m * 512:(m + 1) * 512],
                                ysb[m * CAP:(m + 1) * CAP, x, :]).then_inc(sem(f"y{x}_stored"), 16)

            a.activation(st[:, 90:91], st[:, 8:9], ACT.Copy).then_inc(sem("ov_free"), 1)
            tokens(0)

            def pair(p, first=False, last=False):
                gate(p, 0)
                store(p, 0, first)
                gate(p, 1)
                if not last:
                    tokens(p + 1)
                store(p, 1, first)

            pair(0, first=True)
            with a.Fori(1, NEXP // 2 - 1) as p:
                pair(p)
            pair(NEXP // 2 - 1, last=True)
            for x in range(2):
                a.wait_ge(sem(f"y{x}_stored"), 32 * (NEXP // 2))
            a.wait_ge(sem("over_known"), 1)
            n = a.value_load(over[0:1, 15:16], min_val=0, max_val=OVB)
            a.wait_ge(sem("overflow_zero"), 16)
            with a.If(n > 0):
                with a.Fori(0, n) as b:
                    a.wait_ge(sem("ov_gt"), b + 1)
                    for k in range(KD):
                        e = a.activation(xT[:, k, 0:CAP], ps[:, 0, k * CAP:(k + 1) * CAP], ACT.Identity,
                                         bias=mod[:, SH2, k:k + 1], scale=mod[:, SC2, k:k + 1])
                    e.then_inc(sem("ov_xt"), 1)
                    a.wait_ge(sem("ov_h"), b + 1)
                    a.activation(sg[0:CAP, 0, :], ps[0:CAP, 2, :], ACT.Silu).then_inc(sem("ov_s"), 1)
                    a.wait_ge(sem("ov_y"), b + 1)
                    a.activation(ysb[:, 0, :], ps[:, 6, :], ACT.Copy).then_inc(sem("ov_ys"), 1)
                    a.wait_ge(sem("ov_ys"), b + 1)
                    for m in range(2):
                        a.dma_start(y_dram[bass.ds(b * CAP + MAIN, CAP), m * 512:(m + 1) * 512],
                                    ysb[m * CAP:(m + 1) * CAP, 0, :]).then_inc(sem("ov_stored"), 16)
                    a.wait_ge(sem("ov_stored"), b * 32 + 32)
                    a.activation(st[:, 90:91], st[:, 8:9], ACT.Copy).then_inc(sem("ov_free"), 1)
            a.activation(st[:, 91:92], st[:, 8:9], ACT.Copy).then_inc(sem("ov_done"), 1)

        def act_combine(a):
            for i in range(NT):
                a.wait_ge(sem(f"y_tile{i}_gathered"), 32)
                y = yg[:, i, 0, :]
                a.activation(y, y, ACT.Identity, scale=comb[:, i, 0:1]).then_inc(sem("first_weighted"), 1)
            act_deviation(a, "x2_var", "x2_sd")

        def act_rms(a, src, ready, name, dump):
            for i in range(NT):
                a.wait_ge(sem(ready), i + 1)
                e = a.activation(dump[:, i, :], src[:, i, :], ACT.Square, accum_out=st[:, 80 + i:81 + i])
            e.then_inc(sem(name + "_ss"), 1)
            a.wait_ge(sem(name + "_ss"), 1)
            a.activation(st[:, 84:88], st[:, 80:84], ACT.Sqrt, scale=1.0 / D, bias=colb[:, 32:33]).then_inc(sem(name + "_rms"), 1)

        def act_sb(a):
            unused = brn[:, 0, :].rearrange("p (i n) -> p i n", i=NT)
            act_rms(a, xres, "x2_ready", "x2n", unused)
            act_high_part(a, "h3")

            def weights(j, which):
                act_round(a, ("sb", j), which)

            for which in range(3):
                weights(0, which)

            def inputs(j):
                t = filled(a, ("sq", j))
                free_bank(("sq", j), a.activation(zq[:, j % 2, :], t, ACT.Copy, scale=SB_SCALE))

            def sigmoids(u):
                j, hh, i = ZU[u]
                n = P * (i + 1)
                a.wait_ge(sem("sb_masked"), u + 1)
                if u >= 3:
                    filled(a, ("zT", u - 3))
                t = ps[:, Z_BANK[u % 3], 0:n]
                a.activation(zU[:, u % 3, 0:n], t, ACT.Sigmoid, scale=-1.0)
                free_bank(("z", u), a.activation(zA[:, u % 3, 0:n], t, ACT.Sigmoid))

            def output(u):
                j, hh, i = ZU[u]
                t = filled(a, ("zO", u))
                r = slice(64 * hh, 64 * hh + 64)
                free_bank(("zO", u), a.activation(sT[r, j, i * P:(i + 1) * P], t[r, 0:P], ACT.Copy))

            inputs(0)
            for which in range(3):
                weights(1, which)
            sigmoids(0)
            sigmoids(1)
            for u, (j, hh, i) in enumerate(ZU):
                if u % 8 == 2 and j + 1 < KD:
                    inputs(j + 1)
                if u + 2 < len(ZU):
                    sigmoids(u + 2)
                t = filled(a, ("zT", u))
                free_bank(("zT", u), a.activation(zT[:, u % 2, 0:P * (i + 1)], t[:, 0:P * (i + 1)], ACT.Copy))
                if u:
                    output(u - 1)
                if u % 8 >= 5 and j + 2 < KD:
                    weights(j + 2, u % 8 - 5)
            output(len(ZU) - 1)
            emptied(a, ("zO", len(ZU) - 1))
            act_output_split(a, "wo", sT, sT_high, "")
            act_rms(a, yb, "y1_ready", "y1", hT4)
            act_rms(a, xres, "x3_ready", "x3n", unused)

        def ffn_pieces(f, split):
            if f < FT:
                for m in range(2):
                    split(("fi", f // 2), 2 * (f % 2) + m)
            else:
                for j in range(2):
                    split(("fo", 0), 2 * (f - FT) + j)

        def act_ffn(a):
            act_high_part(a, "h4")
            for f in range(2):
                ffn_pieces(f, lambda chunk, j: act_round(a, chunk, j))
            for f in range(FT):
                if f >= 4:
                    emptied(a, ("fgu", 1, f - 4))
                t = filled(a, ("fgu", 0, f))
                free_bank(("fgu", 0, f), a.activation(fS[:, f % 4, :], t, ACT.Silu))
                ffn_pieces(f + 2, lambda chunk, j: act_round(a, chunk, j))

            def hidden(f):
                if f < FT:
                    emptied(a, ("fgu", 1, f))
                    a.activation(single(ffh[:, f % 4, :]), ff[:, f, :], ACT.Copy).then_inc(sem("ff_rounded"), 1)

            for f in range(4):
                hidden(f)
            for f in range(FT - 4):
                act_round(a, ("fo", (f + 4) // 4), f % 4)
                hidden(f + 4)
            act_rms(a, hT4, "y2_ready", "y2", brn[:, 0, :].rearrange("p (i n) -> p i n", i=NT))

        hT4 = hT[:, :, :].rearrange("p k t -> p (k t)").rearrange("p (i n) -> p i n", i=NT)

        act_stages = [act_start, act_kv, act_attention, act_hgrn, act_merge, act_router, act_experts, act_combine, act_sb, act_ffn]

        @block.scalar
        def _(a):
            for stage in act_stages:
                stage(a)

        dve_steps = [0]

        def step(v, instruction):
            dve_steps[0] += 1
            instruction.then_inc(sem("dve_step"), 1)
            v.wait_ge(sem("dve_step"), dve_steps[0])

        def dve_tile_stats(v, src, i):
            for c in range(2):
                w = v.bn_stats(bnb[:, i, c, :], src[:, i, c * 512:(c + 1) * 512])
            return w

        def dve_layer_norm_affine(v, name, done=None):
            step(v, v.memset(st[:, 94:95], 0.0))
            dve_moments(v, NT, 1e-5).then_inc(sem(name + "_var"), 1)
            v.wait_ge(sem("row_a_in"), ROW_LOADS[0])
            v.wait_ge(sem("row_b_in"), ROW_LOADS[1])
            v.wait_ge(sem(name + "_sd"), 1)
            step(v, v.reciprocal(st[:, 4:8], st[:, 4:8]))
            for i in range(NT):
                v.scalar_tensor_tensor(xres[:, i, :], xres[:, i, :], st[:, 8 + i:9 + i], rows[:, ROW_A, :], ALU.subtract,
                                       ALU.mult).then_inc(sem("dve_step"), 1)
            dve_steps[0] += NT
            for i in range(NT):
                v.wait_ge(sem("dve_step"), dve_steps[0] - NT + i + 1)
                w = v.scalar_tensor_tensor(xres[:, i, :], xres[:, i, :], st[:, 4 + i:5 + i], rows[:, ROW_B, :], ALU.mult, ALU.add)
                if done:
                    w.then_inc(sem(done), 1)
            if not done:
                step(v, w)

        def dve_stats(v, src, nt=NT, eps=1e-5):
            for i in range(nt):
                for c in range(2):
                    w = v.bn_stats(bnb[:, i, c, :], src[:, i, c * 512:(c + 1) * 512])
            step(v, w)
            return dve_moments(v, nt, eps)

        def dve_moments(v, nt, eps):
            for i in range(nt):
                w = v.bn_aggr(mv[:, i, :], bnb[:, i, :, :])
            step(v, w)
            v.tensor_copy(st[:, 8:8 + nt], mv[:, 0:nt, 0])
            return v.tensor_scalar(st[:, 0:nt], mv[:, 0:nt, 1], eps, None, ALU.add)

        def dve_ada(v, m, c):
            name = ("ada", m, c)
            t = filled(v, name)
            b = vec[:, 0, ADAB1 + 4 * c:ADAB1 + 4 * c + 4] if m == 1 else vec[:, 1, ADAB2 + 4 * c:ADAB2 + 4 * c + 4]
            one = 0.0 if c // 2 in (0, 3) or (m, c // 2) in ((2, 2), (2, 5)) else 1.0
            dst = mod[:, 6 * (m - 1) + c // 2, 4 * (c % 2):4 * (c % 2) + 4]
            free_bank(name, v.scalar_tensor_tensor(dst, t[:, 0:4], one, b, ALU.add, ALU.add))

        def dve_start(v):
            t = filled(v, "vec")
            flat = vec[:, :, :].rearrange("p a n -> p (a n)")
            v.tensor_copy(flat[:, 0:P + 126], t[:, 0:P + 126])
            free_bank("vec", v.tensor_copy(flat[:, 2 * P:2 * P + 48], t[:, 2 * P:2 * P + 48]))
            emptied(v, "vec")
            v.tensor_tensor(colb[:, 0:8], vec[:, 2, 0:8], vec[:, 2, 8:16], ALU.subtract).then_inc(sem("lb_diff"), 1)
            v.memset(colb[:, 32:33], 1e-6)
            v.tensor_scalar(colb[:, 16:24], vec[:, 1, Q_N // P:Q_N // P + 8], SCALE, None, ALU.mult)
            v.wait_ge(sem("lb_sigmoid"), 1)
            step(v, v.tensor_scalar(colb[:, 8:16], colb[:, 0:8], -1.0, 1.0, ALU.mult, ALU.add))
            v.wait_ge(sem("x_in"), 16)
            dve_stats(v, xres).then_inc(sem("x_var"), 1)
            v.wait_ge(sem("x_sd"), 1)
            step(v, v.reciprocal(st[:, 4:8], st[:, 4:8]))
            for i in range(NT):
                v.tensor_scalar(xn[:, i, :], xres[:, i, :], st[:, 8 + i:9 + i], st[:, 4 + i:5 + i], ALU.subtract,
                                ALU.mult).then_inc(sem("ln_done"), 1)
            for c in range(4):
                v.wait_ge(sem("start_ada_scaled"), c + 1)
                s = wide(slot_of(("ada", 1, c)))
                for x, half in enumerate((4, 2, 1)):
                    if x:
                        v.wait_ge(sem("start_ada_added"), 3 * c + x)
                    v.tensor_tensor(s[:, 0:half, :], s[:, 0:half, :], s[:, half:2 * half, :], ALU.add).then_inc(sem("start_ada_added"), 1)
                if c:
                    dve_ada(v, 1, c - 1)
            dve_ada(v, 1, 3)

        def dve_kv(v):
            t = filled(v, "cbias").rearrange("p (m h) -> p h m", h=HEADS)
            for i in range(NT):
                w = v.tensor_copy(cbias[:, :, i, :], t[:, :, P // STRIDE * i:P // STRIDE * i + NCMP][:, :, ::-1])
                if i < NT - 1:
                    w.then_inc(sem("cbias_done"), 1)
                else:
                    free_bank("cbias", w)
            emptied(v, "cbias")
            v.wait_ge(sem("cbias_done"), NT - 1)
            v.tensor_scalar(cmask, cbias[:, 0, :, :], NEG / 10, None, ALU.is_gt)

            def cmp_blocks(a):
                for g in range(GROUPS):
                    emptied(v, ("kvT", 0, 2 * a + g))
                if a:
                    filled(v, ("hid", "k"))
                for g in range(GROUPS):
                    for half in range(2):
                        src = kvc[:, a, g, :].rearrange("p (n t) -> p t n", t=STRIDE)[:, :, half:half + NCMP]
                        pos = vec[:, 0, (POSK, POSV)[a] + STRIDE * half:(POSK, POSV)[a] + STRIDE * (half + 1)]
                        v.tensor_tensor(blocks[:, STRIDE * half:STRIDE * (half + 1), g, :], src, grow(pos, NCMP),
                                        ALU.add).then_inc(sem("blocks_ready"), 1)

            def hid_silu(a, kv):
                v.wait_ge(sem("hid_sigmoid"), a + 1)
                t = filled(v, ("hid", kv))
                free_bank(("hid", kv), v.scalar_tensor_tensor(hid[:, a, :], t[:, 0:GROUPS * NCMP],
                                                              vec[:, 1, B1 + a:B1 + a + 1], hsig[:, a, :], ALU.add, ALU.mult))

            for k in range(KD):
                v.wait_ge(sem("h1_rounded"), k + 1)
                v.tensor_tensor(single(hT[:, k, :]), hT[:, k, :], as_float(h1_high[:, k, :]), ALU.subtract).then_inc(sem("h1_split"), 1)
            for j in range(4):
                dve_rest(v, ("kv", 0), j)
            v.wait_ge(sem("wgate_rounded"), 1)
            v.tensor_tensor(single(wgate), wgate, as_float(wgate_high), ALU.subtract).then_inc(sem("wgate_split"), 1)
            for j in range(4):
                dve_rest(v, ("kv", 1), j)
            cmp_blocks(0)
            for j in range(4):
                dve_rest(v, ("kv", 2), j)
            for c in (1, 2):
                for g in range(GROUPS):
                    t = filled(v, ("vtok", c, g))
                    free_bank(("vtok", c, g), v.tensor_copy(vfull[:, c - 1, :, g * P:(g + 1) * P], t.rearrange("p (i n) -> p i n", i=NT)))
            t = filled(v, "gateT")
            free_bank("gateT", v.tensor_copy(gates, t[:, 0:96].rearrange("p (i n) -> p i n", i=NT)))
            cmp_blocks(1)
            hid_silu(0, "k")
            hid_silu(1, "v")
            t = filled(v, "vcmp")
            free_bank("vcmp", v.tensor_copy(vcmp[0:NCMP, :, :], t[0:NCMP, 0:GROUPS * P].rearrange("p (g n) -> p g n", g=GROUPS)))
            for x in range(2):
                dve_rest(v, ("nq", 0), x)

        def dve_attention(v):
            def add_and_max(u, b, scores, o, m, bias):
                c = 12 + 3 * (u % 2) + b
                return v.tensor_tensor_reduce(out=prob[:, u % 2, o:o + m], in0=scores, in1=bias, scale=1.0, scalar=-3e38,
                                              op0=ALU.add, op1=ALU.max, accum_out=st[:, c:c + 1])

            def full_scores(u):
                h, i = UNITS[u]
                n = P * (i + 1)
                for a in range(2):
                    t = filled(v, ("S", a, u))
                    free_bank(("S", a, u), add_and_max(u, 1 + a, t[:, 0:n], a * T, n, biasT[:, h, T - n:T]))

            def compressed(u):
                t = filled(v, ("C", u))
                if u:
                    w = v.tensor_copy(probT[0:NCMP, (u - 1) % 2, 8, :], t[0:NCMP, P:2 * P])
                if u < len(UNITS):
                    h, i = UNITS[u]
                    w = add_and_max(u, 0, t[:, 0:NCMP], 2 * T, NCMP, cbias[:, h, i, :])
                free_bank(("C", u), w)
                if u < len(UNITS):
                    for a in range(2):
                        emptied(v, ("S", a, u))
                    emptied(v, ("C", u))
                    c = 3 * (u % 2)
                    v.tensor_scalar(st[:, 18 + c:21 + c], st[:, 12 + c:15 + c], -1.0, None, ALU.mult).then_inc(sem("neg_max"), 1)

            def diagonals(u):
                h, i = UNITS[u]
                c = 3 * (u % 2)
                v.wait_ge(sem("exp_done"), u + 1)
                p = prob[:, u % 2, 2 * T:2 * T + NCMP]
                v.tensor_tensor(p, p, cmask[:, i, :], ALU.mult)
                step(v, v.reciprocal(st[:, 30 + c:33 + c], st[:, 24 + c:27 + c]))
                step(v, v.tensor_tensor(st[:, 36 + c:39 + c], st[:, 30 + c:33 + c], gates[:, i, 3 * h:3 * h + 3], ALU.mult))
                v.tensor_tensor(dg[:, u % 2, :, :], grow(ident, 3, 1), grow(st[:, 36 + c:39 + c], P), ALU.mult).then_inc(sem("diag_ready"), 1)

            emptied(v, "gateT")
            v.wait_ge(sem("bias_in"), 16)
            full_scores(0)
            compressed(0)
            full_scores(1)
            diagonals(0)
            compressed(1)
            for u, (h, i) in enumerate(UNITS):
                t = filled(v, ("T", 0, u))
                free_bank(("T", 0, u), v.tensor_copy(probT[:, u % 2, 0:i + 1, :].rearrange("p a n -> p (a n)"), t[:, 0:P * (i + 1)]))
                if i == 2:
                    dve_ada(v, *ada_at[("attn", h)])
                if u + 1 < len(UNITS):
                    diagonals(u + 1)
                if u + 2 < len(UNITS):
                    full_scores(u + 2)
                if u + 1 < len(UNITS):
                    compressed(u + 2)
                if i == NT - 1 and h + 2 < HEADS:
                    dve_rest(v, ("nq", (h + 2) // 2), h % 2)

        def dve_hgrn(v):
            filled(v, ("O", len(UNITS) - 1))
            attmask = const("attmask").bitcast(u32)
            def weights(h, js=range(4)):
                for j in js:
                    dve_rest(v, ("hg", h), j)

            weights(0)
            weights(1)
            v.memset(hAT, 0.0)

            def values(h):
                t = filled(v, ("hiT", h))
                free_bank(("hiT", h), v.tensor_copy(hV[:, h % 2, :, :].rearrange("p i n -> p (i n)"), t))

            for h in range(HEADS):
                f = hF[:, h % 2, :]
                emptied(v, ("hf", h))
                v.tensor_scalar(f, f, colb[:, 8 + h:9 + h], colb[:, h:h + 1], ALU.mult, ALU.add).then_inc(sem("hg_f"), 1)
                v.wait_ge(sem("hg_f"), h + 1)
                v.tensor_scalar(hK, f, -1.0, 1.0, ALU.mult, ALU.add)
                v.wait_ge(sem("hg_logf"), h + 1)
                v.tensor_tensor_scan(hB, const("reset"), hT2, 0.0, ALU.mult, ALU.add).then_inc(sem("hg_b"), 1)
                v.wait_ge(sem("hg_b"), 2 * h + 1)
                if h:
                    filled(v, ("kendT", h - 1))
                b3 = hB.rearrange("p (n c) -> p n c", c=CHUNK)
                v.tensor_tensor(hKN.rearrange("p (n c) -> p n c", c=CHUNK), b3[:, :, CHUNK - 1:CHUNK].to_broadcast([P, NCHUNK, CHUNK]),
                                b3, ALU.subtract).then_inc(sem("hg_b"), 1)
                emptied(v, ("hq", h))
                v.wait_ge(sem("hg_exp"), 3 * h + 1)
                v.tensor_tensor(hQ[:, h % 2, :], hQ[:, h % 2, :], hEB, ALU.mult)
                v.wait_ge(sem("hg_exp"), 3 * h + 2)
                if h:
                    filled(v, ("att", h - 1))
                v.tensor_tensor(hKI, hK, hT2, ALU.mult)
                v.wait_ge(sem("hg_exp"), 3 * h + 3)
                v.tensor_tensor(hKN, hKN, hK, ALU.mult).then_inc(sem("hg_kend"), 1)
                values(h)

                def chunk_blocks(i):
                    t = filled(v, ("kendT", h))
                    if i >= 2:
                        filled(v, ("U", h, i - 2))
                    elif h:
                        filled(v, ("U", h - 1, i + 2))
                    w = v.tensor_tensor(hKX[:, i % 2, :, :], grow(t[:, i * P:(i + 1) * P], CPT, 1),
                                        grow(const("chunk"), P), ALU.mult)
                    if i < NT - 1:
                        w.then_inc(sem("hg_kblocks"), 1)
                    else:
                        free_bank(("kendT", h), w)

                chunk_blocks(0)
                chunk_blocks(1)
                t = filled(v, ("att", h))
                if h:
                    filled(v, ("oT", h - 1))
                free_bank(("att", h), v.copy_predicated(hAT.rearrange("p (i n) -> p i n", i=NT), grow(attmask, NT, 1),
                                                        t.rearrange("p (i n) -> p i n", i=NT)))
                for i in range(NT):
                    t = filled(v, ("U", h, i))
                    for c in range(CPT):
                        n = CPT * i + c
                        if n == NCHUNK - 1:
                            continue
                        u = t[:, c * P:(c + 1) * P]
                        if n == 0:
                            w = v.tensor_copy(hS[:, 1, :], u)
                        else:
                            state_ready(v, h, n)
                            w = v.scalar_tensor_tensor(hS[:, n + 1, :], hS[:, n, :], hEB[:, CHUNK * (n + 1) - 1:CHUNK * (n + 1)],
                                                       u, ALU.mult, ALU.add)
                        if c == CPT - 1 or n == NCHUNK - 2:
                            free_bank(("U", h, i), w)
                        else:
                            w.then_inc(sem("hg_state"), 1)
                    if i + 2 < NT:
                        chunk_blocks(i + 2)
                if h + 2 < HEADS:
                    weights(h + 2, range(3))
                t = filled(v, ("oT", h))
                free_bank(("oT", h), v.tensor_copy(hO, t))
                dve_ada(v, *ada_at[("hg", h)])
                if h + 2 < HEADS:
                    weights(h + 2, [3])
                emptied(v, ("ss", h))
                v.tensor_tensor(hO, hO, hT2, ALU.mult).then_inc(sem("hg_out"), 1)
                v.wait_ge(sem("hg_out"), 2 * h + 1)
                v.scalar_tensor_tensor(oH[:, h, :], hO, vec[:, 1, HGN + h:HGN + h + 1], hG[:, h % 2, :], ALU.mult,
                                       ALU.mult).then_inc(sem("hg_out"), 1)

        def dve_merge(v):
            def weights(j):
                for x in range(2):
                    dve_rest(v, ("merge", j), x)

            weights(0)
            weights(1)
            v.wait_ge(sem("hg_out"), 2 * HEADS)
            for j in range(KD):
                for b, m in ((1, "mN"), (0, "mH")):
                    t = filled(v, (m, j))
                    emptied(v, (("mgh", "mgn")[b], j))
                    if j >= 2:
                        v.wait_ge(sem("merged"), j - 1)
                    free_bank((m, j), v.tensor_tensor(mP[:, 2 * (j % 2) + b, :], t, mS[:, 2 * (j % 2) + b, :], ALU.mult))
                if j + 2 < KD:
                    weights(j + 2)
                if j < 4:
                    dve_ada(v, *ada_at[("merge", j)])
            emptied(v, ("ada", 2, 11))
            for which, gain in ((GM, 1), (GF, 3), (SCM, 0), (SCF, 2)):
                step(v, v.tensor_tensor(mod[:, which, :], mod[:, which, :], vec[:, 2, 16 + 8 * gain:24 + 8 * gain], ALU.mult))
            dve_output_split(v, "wout", mT, mT_high)
            for x in range(8):
                if x >= 2:
                    filled(v, ("row", x - 2))
                g = mod[:, (G1, G2, GM, GF)[x // 2], 4 * (x % 2):4 * (x % 2) + 4]
                v.tensor_tensor(mD[:, x % 2, :].rearrange("p (a n) -> p a n", a=4), grow(ident, 4, 1), grow(g, P),
                                ALU.mult).then_inc(sem("gate_diag"), 1)
                if x:
                    t = filled(v, ("row", x - 1))
                    free_bank(("row", x - 1), v.tensor_copy(rows[:, (x - 1) // 2, ((x - 1) % 2) * 512:((x - 1) % 2 + 1) * 512], t))
            t = filled(v, ("row", 7))
            free_bank(("row", 7), v.tensor_copy(rows[:, 3, 512:1024], t))
            emptied(v, ("row", 7))
            for j in range(4):
                dve_rest(v, ("wout", 1), j)
            for c in range(2):
                for i in range(NT):
                    t = filled(v, ("wout", c, i))
                    half = slice(512 * c, 512 * (c + 1))
                    tmp = mP[:, i, :]
                    free_bank(("wout", c, i), v.tensor_tensor(tmp, t, rows[:, ROW_G1, half], ALU.mult))
                    emptied(v, ("wout", c, i))
                    w = v.scalar_tensor_tensor(xres[:, i, half], xres[:, i, half], ALPHA, tmp, ALU.mult, ALU.add)
            step(v, w)

        def dve_layer_norm(v, src, dst, name, done=None):
            dve_stats(v, src).then_inc(sem(name + "_var"), 1)
            v.wait_ge(sem(name + "_sd"), 1)
            step(v, v.reciprocal(st[:, 4:8], st[:, 4:8]))
            for i in range(NT):
                w = v.tensor_scalar(dst[:, i, :], src[:, i, :], st[:, 8 + i:9 + i], st[:, 4 + i:5 + i], ALU.subtract, ALU.mult)
                if done:
                    w.then_inc(sem(done), 1)
            if not done:
                step(v, w)

        ROW_LOADS = [16, 16]

        def dve_router(v):
            for i in range(NT):
                dve_tile_stats(v, xres, i)
            dve_layer_norm_affine(v, "x1")
            dve_layer_norm(v, xres, xn2, "xn2", "xn2_done")
            step(v, v.tensor_copy(token[:, :], const("token")))
            step(v, v.memset(g8, NEG))
            v.wait_ge(sem("router_in"), 64)
            for i in range(NT):
                t = filled(v, ("logits", i))
                free_bank(("logits", i), v.tensor_tensor(lg[:, i, :], t[:, 0:36], rbias, ALU.add))
            for i in range(NT):
                emptied(v, ("logits", i))
            step(v, v.tensor_copy(g8[:, :, 0:EXP_GROUPS], lg[:, :, 0:EXP_GROUPS]))
            for i in range(NT):
                w = v.max(gtop[:, i, :], g8[:, i, :])
            step(v, w)
            for i in range(NT):
                w = v.max_index(gat[:, i, :], gtop[:, i, :], g8[:, i, :])
            step(v, w)
            v.tensor_tensor(gexp, lg[:, :, 0:EXP_GROUPS], gtop[:, :, 0:1].to_broadcast([P, NT, EXP_GROUPS]),
                            ALU.subtract).then_inc(sem("group_logits"), 1)
            step(v, v.tensor_copy(idxf[:, :, 0:1], gat[:, :, 0:1]))
            step(v, v.tensor_tensor(gone, grow(const("iota")[:, 0:EXP_GROUPS], NT, 1),
                                    idxf[:, :, 0:1].to_broadcast([P, NT, EXP_GROUPS]), ALU.is_equal))
            m4 = masked.rearrange("p i (g e) -> p (i g) e", g=EXP_GROUPS)
            t4 = tmp32.rearrange("p i (g e) -> p (i g) e", g=EXP_GROUPS)
            gf = gone.rearrange("p i g -> p (i g)")
            step(v, v.tensor_scalar(t4, grow(gf, EPG), -NEG, NEG, ALU.mult, ALU.add))
            step(v, v.tensor_copy(masked, lg[:, :, EXP_GROUPS:36]))
            step(v, v.tensor_tensor(m4, m4, grow(gf, EPG), ALU.mult))
            step(v, v.tensor_tensor(masked, masked, tmp32, ALU.add))
            for i in range(NT):
                w = v.max(etop[:, i, :], masked[:, i, :])
            step(v, w)
            for i in range(NT):
                w = v.max_index(eat[:, i, :], etop[:, i, :], masked[:, i, :])
            step(v, w)
            v.tensor_tensor(emax2.unsqueeze(2), etop[:, :, 1:2], etop[:, :, 0:1], ALU.subtract).then_inc(sem("second_logit"), 1)
            step(v, v.tensor_copy(idxf[:, :, 1:3], eat[:, :, 0:2]))
            iota = grow(const("iota"), NT, 1)
            v.tensor_tensor(hot0, iota, idxf[:, :, 1:2].to_broadcast([P, NT, NEXP]), ALU.is_equal)
            step(v, v.tensor_tensor(hot1, iota, idxf[:, :, 2:3].to_broadcast([P, NT, NEXP]), ALU.is_equal))
            v.tensor_tensor(both, hot0, hot1, ALU.add).then_inc(sem("chosen"), 1)
            v.wait_ge(sem("group_exp"), 1)
            step(v, v.tensor_reduce(gsum, gexp, AX.X, ALU.add))
            v.wait_ge(sem("second_exp"), 1)
            step(v, v.tensor_scalar(st[:, 60:64], emax2, 1.0, None, ALU.add))
            step(v, v.tensor_tensor(st[:, 60:64], st[:, 60:64], gsum, ALU.mult))
            step(v, v.reciprocal(comb[:, :, 0], st[:, 60:64]))
            step(v, v.tensor_tensor(comb[:, :, 1], comb[:, :, 0], emax2, ALU.mult))
            t = filled(v, "rank")
            v.tensor_copy(rank, t[:, 0:NT * NEXP].rearrange("p (i n) -> p i n", i=NT))
            free_bank("rank", v.tensor_copy(counts, t[:, NT * NEXP:(NT + 1) * NEXP]))
            emptied(v, "rank")
            step(v, v.tensor_tensor(cmp7, grow(counts, 7), grow(const("full"), NEXP, 1), ALU.is_gt))
            step(v, v.tensor_reduce(blocks_of, cmp7, AX.X, ALU.add))
            step(v, v.tensor_tensor_scan(block_end, ones[:, 0:NEXP], blocks_of, 0.0, ALU.mult, ALU.add))
            step(v, v.tensor_tensor(tmp1, block_end, blocks_of, ALU.subtract))
            step(v, v.tensor_scalar(over0, tmp1, float(CAP), float(MAIN - CAP), ALU.mult, ALU.add))
            step(v, v.tensor_tensor(over0, over0, const("slot0"), ALU.subtract))
            step(v, v.tensor_scalar(place, rank, float(CAP), None, ALU.is_ge))
            step(v, v.tensor_tensor(place, place, grow(over0, NT, 1), ALU.mult))
            step(v, v.tensor_tensor(place, place, rank, ALU.add))
            step(v, v.tensor_tensor(place, place, grow(const("slot0"), NT, 1), ALU.add))
            v.tensor_tensor(hot0, hot0, place, ALU.mult)
            step(v, v.tensor_tensor(hot1, hot1, place, ALU.mult))
            v.tensor_reduce(slotf[:, :, 0], hot0, AX.X, ALU.add)
            step(v, v.tensor_reduce(slotf[:, :, 1], hot1, AX.X, ALU.add))
            v.tensor_copy(dest[:, :, :], slotf).then_inc(sem("dest_ready"), 1)
            step(v, v.tensor_tensor(cmp16, grow(block_end, 15, 1), grow(const("block")[:, 0:15], NEXP), ALU.is_le))
            step(v, v.tensor_reduce(overf[:, 0:15], cmp16, AX.X, ALU.add))
            step(v, v.tensor_scalar(overf[:, 0:15], overf[:, 0:15], float(NEXP - 1), None, ALU.min))
            step(v, v.tensor_copy(overf[:, 15:16], block_end[:, NEXP - 1:NEXP]))
            v.tensor_copy(over[:, :], overf).then_inc(sem("over_known"), 1)
            v.wait_ge(sem("slots_in"), 16)
            v.tensor_copy(tabf[0:SLOTS // P, :], tabi[0:SLOTS // P, :]).then_inc(sem("slots_float"), 1)
            t = filled(v, "slots")
            free_bank("slots", v.tensor_copy(slot_token[:, :], t[:, 0:SLOTS // P]))
            emptied(v, "slots")
            v.memset(st[:, 89:90], 0.0).then_inc(sem("slots_back"), 1)

        def dve_experts(v):
            base = fills_before_moe

            def gated(p, x, n):
                v.wait_ge(sem("moe_silu"), p * 2 + (x + 1))
                v.wait_ge(full[2 + x], p + (base[2 + x] + 1))
                v.tensor_tensor(hx[0:CAP, x, :], sg[0:CAP, x, :], ps[CAP:2 * CAP, 2 + x, :], ALU.mult).then_inc(empty[2 + x], 1)
                v.wait_ge(full[4 + x], p + (base[4 + x] + 1))
                v.tensor_copy(aT[:, x, :, :].rearrange("p k n -> p (k n)"), ps[:, 4 + x, 0:4 * CAP]).then_inc(empty[4 + x], 1)

            with v.Fori(0, NEXP // 2) as p:
                gated(p, 0, None)
                gated(p, 1, None)
            n = v.value_load(over[0:1, 15:16], min_val=0, max_val=OVB)
            with v.If(n > 0):
                with v.Fori(0, n) as b:
                    v.wait_ge(sem("ov_s"), b + 1)
                    v.tensor_tensor(hx[0:CAP, 0, :], sg[0:CAP, 0, :], ps[CAP:2 * CAP, 2, :], ALU.mult).then_inc(sem("ov_a"), 1)
                    v.wait_ge(sem("ov_at"), b + 1)
                    v.tensor_copy(aT[:, 0, :, :].rearrange("p k n -> p (k n)"), ps[:, 4, 0:4 * CAP]).then_inc(sem("ov_ate"), 1)
            v.wait_ge(sem("ov_done"), 1)

        def dve_combine(v):
            for i in range(NT):
                v.wait_ge(sem("first_weighted"), i + 1)
                y = yg[:, i, 0, :]
                step(v, v.scalar_tensor_tensor(y, yg[:, i, 1, :], comb[:, i, 1:2], y, ALU.mult, ALU.add))
                step(v, v.tensor_tensor(y, y, rows[:, ROW_G2, :], ALU.mult))
                step(v, v.scalar_tensor_tensor(xres[:, i, :], xres[:, i, :], ALPHA, y, ALU.mult, ALU.add))
                dve_tile_stats(v, xres, i)
            ROW_LOADS[:] = [32, 32]
            dve_layer_norm_affine(v, "x2", "x2_ready")

        def dve_rms(v, name, dst, done):
            v.wait_ge(sem(name + "_rms"), 1)
            step(v, v.reciprocal(st[:, 84:88], st[:, 84:88]))
            for i in range(NT):
                v.tensor_scalar(dst[:, i, :], xres[:, i, :], st[:, 84 + i:85 + i], None, ALU.mult).then_inc(sem(done), 1)

        def dve_residual(v, kind, y, row, name, done):
            for i in range(NT):
                for c in range(2):
                    t = filled(v, (kind, c, i))
                    free_bank((kind, c, i), v.tensor_copy(y[:, i, c * 512:(c + 1) * 512], t))
                for c in range(2):
                    emptied(v, (kind, c, i))
                v.memset(st[:, 88:89], 0.0).then_inc(sem(name + "_ready"), 1)
            v.wait_ge(sem(name + "_rms"), 1)
            step(v, v.reciprocal(st[:, 84:88], st[:, 84:88]))
            for i in range(NT):
                step(v, v.scalar_tensor_tensor(y[:, i, :], y[:, i, :], st[:, 84 + i:85 + i], rows[:, row, :], ALU.mult, ALU.mult))
                v.tensor_tensor(xres[:, i, :], xres[:, i, :], y[:, i, :], ALU.add).then_inc(sem(done), 1)

        def dve_low_part(v, name, sc, sh):
            for k in range(KD + 1):
                if k < KD:
                    t = filled(v, (name, k))
                    free_bank((name, k), v.tensor_scalar(h_low[:, k, :], t, mod[:, sc, k:k + 1], mod[:, sh, k:k + 1],
                                                         ALU.mult, ALU.add))
                if k:
                    low = h_low[:, k - 1, :]
                    v.wait_ge(sem(name + "_rounded"), k)
                    v.tensor_tensor(single(low), low, as_float(hT[:, k - 1, :]), ALU.subtract).then_inc(sem(name + "_split"), 1)

        def dve_sb(v):
            dve_rms(v, "x2n", xn3, "xn3_done")
            dve_low_part(v, "h3", SCM, SHM)
            for which in range(3):
                dve_rest(v, ("sb", 0), which)

            def keys(j):
                t = filled(v, ("sk", j))
                free_bank(("sk", j), v.tensor_copy(zk[:, j % 2, :], t))

            def values_feature_major(j):
                t = filled(v, ("sv", j))
                free_bank(("sv", j), v.tensor_copy(zvT, t))

            def values(j):
                t = filled(v, ("svT", j))
                free_bank(("svT", j), v.tensor_copy(zv[:, j % 2, :, :].rearrange("p i n -> p (i n)"), t))

            def mask(u):
                i = ZU[u][2]
                t = filled(v, ("z", u))
                t = t[:, i * P:(i + 1) * P]
                v.tensor_tensor(t, t, const("sbmask"), ALU.add).then_inc(sem("sb_masked"), 1)

            for n in range(1, NT + 1):
                for a in range(3):
                    w = v.memset(zR[:, a, n * P:n * P + 1], 1.0)
            step(v, w)
            keys(0)
            values_feature_major(0)
            for which in range(3):
                dve_rest(v, ("sb", 1), which)
            values(0)
            mask(0)
            mask(1)
            for u, (j, hh, i) in enumerate(ZU):
                if u % 8 == 4 and j + 1 < KD:
                    keys(j + 1)
                if u % 8 == 6 and j + 1 < KD:
                    values_feature_major(j + 1)
                n = P * (i + 1)
                emptied(v, ("z", u))
                if u >= 3:
                    v.wait_ge(sem("sb_weights"), u - 2)
                step(v, v.memset(zR[:, u % 3, n:n + 1], 1.0))
                v.tensor_tensor_scan(zR[:, u % 3, 0:n][:, ::-1], zU[:, u % 3, 0:n][:, ::-1], const("zeros")[:, 0:n], 1.0,
                                     ALU.mult, ALU.add).then_inc(sem("sb_scan"), 1)
                v.wait_ge(sem("sb_scan"), u + 1)
                v.tensor_tensor(zA[:, u % 3, 0:n], zA[:, u % 3, 0:n], zR[:, u % 3, 1:n + 1], ALU.mult).then_inc(sem("sb_weights"), 1)
                if u + 2 < len(ZU):
                    mask(u + 2)
                if u % 8 == 7 and j + 1 < KD:
                    values(j + 1)
                for which in range(3):
                    if (u - 6 - which) % 8 == 0 and u >= 6 and (u - 6) // 8 + 2 < KD:
                        dve_rest(v, ("sb", (u - 6 - which) // 8 + 2), which)
            dve_output_split(v, "wo", sT, sT_high)
            for j in range(4):
                dve_rest(v, ("wo", 1), j)
            dve_residual(v, "wo", yb, ROW_GM, "y1", "x3_ready")

        def dve_ffn(v):
            dve_rms(v, "x3n", xn3, "xn4_done")
            dve_low_part(v, "h4", SCF, SHF)
            for f in range(2):
                ffn_pieces(f, lambda chunk, j: dve_rest(v, chunk, j))
            for f in range(FT):
                emptied(v, ("fgu", 0, f))
                t = filled(v, ("fgu", 1, f))
                free_bank(("fgu", 1, f), v.tensor_tensor(ff[:, f, :], fS[:, f % 4, :], t, ALU.mult))
                ffn_pieces(f + 2, lambda chunk, j: dve_rest(v, chunk, j))

            def hidden(f):
                v.wait_ge(sem("ff_rounded"), f + 1)
                v.tensor_tensor(single(ff[:, f, :]), ff[:, f, :], as_float(ffh[:, f % 4, :]), ALU.subtract).then_inc(sem("ff_split"), 1)

            for f in range(4):
                hidden(f)
            for f in range(FT - 4):
                dve_rest(v, ("fo", (f + 4) // 4), f % 4)
                hidden(f + 4)
            dve_residual(v, "fo", hT4, ROW_GF, "y2", "out_ready")

        dve_stages = [dve_start, dve_kv, dve_attention, dve_hgrn, dve_merge, dve_router, dve_experts, dve_combine, dve_sb, dve_ffn]

        @block.vector
        def _(v):
            for stage in dve_stages:
                stage(v)


_OUT = (1, T, D)


def kernel(**inputs):
    import concourse.bacc as bacc
    from concourse.bass_utils import run_bass_kernel_spmd

    nc = bacc.Bacc("TRN2", target_bir_lowering=False, num_devices=1)
    arrays, io = {}, {}
    given = {k: v for k, v in inputs.items() if v.size and not k.startswith(("sg_", "sc_", "cb_"))}
    for name, a in {**given, **shape_constants()}.items():
        a = np.ascontiguousarray(a)
        arrays[f"in_{name}"] = a
        io[name] = nc.dram_tensor(f"in_{name}", a.shape, mybir.dt.from_np(a.dtype), kind="ExternalInput").ap()
    out = nc.dram_tensor("out", _OUT, mybir.dt.float32, kind="ExternalOutput").ap()
    block_kernel(nc, io, out)
    return run_bass_kernel_spmd(nc, [arrays], core_ids=[0]).results[0]["out"]
```
